# Optimizing a Trainium2 kernel written in Bass

```python
import math
import jax, jax.numpy as jnp
from jax import lax
import numpy as np

D_MODEL = 1024
BATCH = 1
SEQ = 256
DEPTH = 2

N_A_LAYERS = DEPTH // 2
N_B_LAYERS = DEPTH - N_A_LAYERS

GLA_HEADS = 4
GLA_KEY_DIM = D_MODEL // 2
GLA_VAL_DIM = D_MODEL
GLA_HK = GLA_KEY_DIM // GLA_HEADS
GLA_HV = GLA_VAL_DIM // GLA_HEADS
GLA_GATE_RANK = 16
GLA_GATE_NORM = 16.0
GLA_CHUNK = 64
A_PROJ = 2 * GLA_KEY_DIM + 2 * GLA_VAL_DIM + GLA_GATE_RANK

SWA_HEAD_DIM = 64
SWA_Q_HEADS = D_MODEL // SWA_HEAD_DIM
SWA_GROUP = 8
SWA_KV_HEADS = SWA_Q_HEADS // SWA_GROUP
WINDOW = 128
BLOCK = 128
KV_PROJ = 2 * SWA_KV_HEADS * SWA_HEAD_DIM

REL_BUCKETS = 32
REL_MAX_DIST = 128

D_FF = 4 * D_MODEL
EPS = 1e-6
NEG = -1e30


def rmsnorm(x, g):
    xf = x.astype(jnp.float32)
    y = xf * lax.rsqrt(jnp.mean(xf * xf, axis=-1, keepdims=True) + EPS) * g.astype(jnp.float32)
    return y.astype(x.dtype)

def sq_relu_mlp(h, w_up, w_down):
    u = jax.nn.relu(h @ w_up)
    return (u * u) @ w_down

def gla_mixer(h, w_in, w_gk2, b_gk, g_onorm, w_out):
    B, T, _ = h.shape
    C = GLA_CHUNK
    NC = T // C
    f32 = jnp.float32
    proj = h @ w_in
    q, k, v, gate, glr = jnp.split(
        proj, [GLA_KEY_DIM, 2 * GLA_KEY_DIM, 2 * GLA_KEY_DIM + GLA_VAL_DIM,
               2 * GLA_KEY_DIM + 2 * GLA_VAL_DIM], axis=-1)
    gk = jax.nn.log_sigmoid((glr @ w_gk2 + b_gk).astype(f32)) / GLA_GATE_NORM

    def heads(t, d):
        return t.astype(f32).reshape(B, NC, C, GLA_HEADS, d).transpose(1, 0, 3, 2, 4)

    qf = heads(q, GLA_HK) * (GLA_HK ** -0.5)
    kf = heads(k, GLA_HK)
    vf = heads(v, GLA_HV)
    bcum = jnp.cumsum(heads(gk, GLA_HK), axis=-2)
    q_t = qf * jnp.exp(bcum)
    k_t = kf * jnp.exp(-bcum)
    causal = jnp.asarray(np.tril(np.ones((C, C), dtype=bool)))
    attn = jnp.where(causal, jnp.einsum('nbhik,nbhjk->nbhij', q_t, k_t), 0.0)
    o_intra = jnp.einsum('nbhij,nbhjv->nbhiv', attn, vf)
    b_last = bcum[..., -1:, :]
    k_dec = kf * jnp.exp(b_last - bcum)

    def step(S, xs):
        q_c, k_c, v_c, bl = xs
        o = jnp.einsum('bhik,bhkv->bhiv', q_c, S)
        S = S * jnp.exp(bl)[..., 0, :, None] + jnp.einsum('bhjk,bhjv->bhkv', k_c, v_c)
        return S, o

    S0 = jnp.zeros((B, GLA_HEADS, GLA_HK, GLA_HV), f32)
    _, o_inter = lax.scan(step, S0, (q_t, k_dec, vf, b_last))
    o = (o_intra + o_inter).transpose(1, 0, 3, 2, 4).reshape(B, T, GLA_HEADS, GLA_HV)
    o = o * lax.rsqrt(jnp.mean(o * o, axis=-1, keepdims=True) + EPS) * g_onorm.astype(f32)
    o = o * jax.nn.silu(gate.astype(f32).reshape(B, T, GLA_HEADS, GLA_HV))
    return o.reshape(B, T, GLA_VAL_DIM).astype(h.dtype) @ w_out

def rel_bucket_band():
    i = np.arange(BLOCK)[:, None]
    j = np.arange(2 * BLOCK)[None, :]
    dist = i + BLOCK - j
    n = np.maximum(dist, 0)
    max_exact = REL_BUCKETS // 2
    large = max_exact + (np.log(np.maximum(n, 1) / max_exact)
                         / np.log(REL_MAX_DIST / max_exact)
                         * (REL_BUCKETS - max_exact)).astype(np.int32)
    large = np.minimum(large, REL_BUCKETS - 1)
    bucket = np.where(n < max_exact, n, large).astype(np.int32)
    valid = (dist >= 0) & (dist < WINDOW)
    return bucket, valid

def shared_kv(h, w_kv):
    B, T, _ = h.shape
    NB = T // BLOCK
    k, v = jnp.split(h @ w_kv, 2, axis=-1)

    def band(t):
        t = t.reshape(B, NB, BLOCK, SWA_KV_HEADS, SWA_HEAD_DIM)
        prev = jnp.concatenate([jnp.zeros_like(t[:, :1]), t[:, :-1]], axis=1)
        return jnp.concatenate([prev, t], axis=2)

    return band(k), band(v)

def swa_mixer(h, kb, vb, w_q, sinks, rel_table, w_out):
    B, T, _ = h.shape
    NB = T // BLOCK
    q = (h @ w_q).reshape(B, NB, BLOCK, SWA_KV_HEADS, SWA_GROUP, SWA_HEAD_DIM)
    s = jnp.einsum('bnqhgd,bnkhd->bnhgqk', q, kb).astype(jnp.float32) * (SWA_HEAD_DIM ** -0.5)
    bucket, valid = rel_bucket_band()
    bias = rel_table.astype(jnp.float32)[bucket]
    bias = bias.transpose(2, 0, 1).reshape(SWA_KV_HEADS, SWA_GROUP, BLOCK, 2 * BLOCK)
    first = (np.arange(NB)[:, None] == 0) & (np.arange(2 * BLOCK)[None, :] < BLOCK)
    mask = jnp.asarray(valid[None] & ~first[:, None, :])
    s = jnp.where(mask[None, :, None, None], s + bias, NEG)
    sink = sinks.astype(jnp.float32).reshape(SWA_KV_HEADS, SWA_GROUP, 1, 1)
    m = jnp.maximum(jnp.max(s, axis=-1, keepdims=True), sink)
    p = jnp.exp(s - m)
    p = p / (jnp.sum(p, axis=-1, keepdims=True) + jnp.exp(sink - m))
    o = jnp.einsum('bnhgqk,bnkhd->bnqhgd', p.astype(vb.dtype), vb)
    return o.reshape(B, T, SWA_Q_HEADS * SWA_HEAD_DIM) @ w_out

def first_inputs(seed: int = 0) -> dict:
    key = jax.random.key(seed)
    ks = jax.random.split(key, 20)
    f32 = jnp.float32

    def w(k, shape, fan_in, scale=1.0):
        return jax.random.normal(k, shape, f32) * (scale * fan_in ** -0.5)

    def gain(k, shape):
        return 1.0 + 0.02 * jax.random.normal(k, shape, f32)

    return {
        "x": jax.random.normal(ks[0], (BATCH, SEQ, D_MODEL), f32),
        "a_w_in": w(ks[1], (N_A_LAYERS, D_MODEL, A_PROJ), D_MODEL),
        "a_w_gk2": w(ks[2], (N_A_LAYERS, GLA_GATE_RANK, GLA_KEY_DIM), GLA_GATE_RANK),
        "a_b_gk": 0.1 * jax.random.normal(ks[3], (N_A_LAYERS, GLA_KEY_DIM), f32),
        "a_onorm": gain(ks[4], (N_A_LAYERS, GLA_HV)),
        "a_w_out": w(ks[5], (N_A_LAYERS, GLA_VAL_DIM, D_MODEL), GLA_VAL_DIM),
        "kv_norm": gain(ks[6], (D_MODEL,)),
        "w_kv": w(ks[7], (D_MODEL, KV_PROJ), D_MODEL),
        "b_w_q": w(ks[8], (N_B_LAYERS, D_MODEL, SWA_Q_HEADS * SWA_HEAD_DIM), D_MODEL),
        "b_sinks": 0.5 * jax.random.normal(ks[9], (N_B_LAYERS, SWA_Q_HEADS), f32),
        "b_w_out": w(ks[10], (N_B_LAYERS, SWA_Q_HEADS * SWA_HEAD_DIM, D_MODEL), D_MODEL),
        "rel_table": 0.5 * jax.random.normal(ks[11], (REL_BUCKETS, SWA_Q_HEADS), f32),
        "ln_mix": gain(ks[12], (DEPTH, D_MODEL)),
        "ln_mlp": gain(ks[13], (DEPTH, D_MODEL)),
        "w_up": w(ks[14], (DEPTH, D_MODEL, D_FF), D_MODEL),
        "w_down": w(ks[15], (DEPTH, D_FF, D_MODEL), D_FF, scale=0.5),
        "ln_final": gain(ks[16], (D_MODEL,)),
    }

def first_block(x, a_w_in, a_w_gk2, a_b_gk, a_onorm, a_w_out, kv_norm, w_kv, b_w_q, b_sinks,
              b_w_out, rel_table, ln_mix, ln_mlp, w_up, w_down, ln_final):
    h = x
    kb = vb = None
    for layer in range(DEPTH):
        if layer < N_A_LAYERS:
            h = h + gla_mixer(rmsnorm(h, ln_mix[layer]), a_w_in[layer], a_w_gk2[layer],
                              a_b_gk[layer], a_onorm[layer], a_w_out[layer])
        else:
            if layer == N_A_LAYERS:
                kb, vb = shared_kv(rmsnorm(h, kv_norm), w_kv)
            j = layer - N_A_LAYERS
            h = h + swa_mixer(rmsnorm(h, ln_mix[layer]), kb, vb, b_w_q[j], b_sinks[j],
                              rel_table, b_w_out[j])
        h = h + sq_relu_mlp(rmsnorm(h, ln_mlp[layer]), w_up[layer], w_down[layer])
    return rmsnorm(h, ln_final)


DEPTH_2 = 1

GRID_W = 64
HEAD_DIM_A = 128
N_Q_HEADS_A = 8
N_KV_HEADS_A = 2
ROPE_THETA = 10000.0
Q_BLOCK = 128
HEAD_DIM_B = 64
N_HEADS_PER_DIL = 4
DIL_PAIRS = ((128, 1), (512, 4), (2048, 16))
N_HEADS_B = N_HEADS_PER_DIL * len(DIL_PAIRS)
BAND_BLOCK = 64
N_REL_BUCKETS = 32
REL_MAX_DIST_2 = 1024
D_FF_2 = 4 * D_MODEL
D_PLE = 256
NORM_EPS = 1e-6
NEG_INF = -1e30

SPLIT_SIZES = (
    N_Q_HEADS_A * HEAD_DIM_A,
    N_KV_HEADS_A * HEAD_DIM_A,
    N_KV_HEADS_A * HEAD_DIM_A,
    N_HEADS_B * HEAD_DIM_B,
    N_HEADS_B * HEAD_DIM_B,
    N_HEADS_B * HEAD_DIM_B,
    D_MODEL,
    D_MODEL,
)
D_IN_PROJ = sum(SPLIT_SIZES)


def rmsnorm_2(x, g):
    xf = x.astype(jnp.float32)
    y = xf * lax.rsqrt(jnp.mean(xf * xf, axis=-1, keepdims=True) + NORM_EPS)
    return (y * g.astype(jnp.float32)).astype(x.dtype)

def rope_1d(x, pos):
    d = x.shape[-1]
    inv_freq = jnp.power(ROPE_THETA, -jnp.arange(0, d, 2, dtype=jnp.float32) / d)
    ang = pos.astype(jnp.float32)[:, None] * inv_freq[None, :]
    cos = jnp.cos(ang)[None, :, None, :]
    sin = jnp.sin(ang)[None, :, None, :]
    xf = x.astype(jnp.float32)
    x1, x2 = xf[..., : d // 2], xf[..., d // 2:]
    out = jnp.concatenate([x1 * cos - x2 * sin, x2 * cos + x1 * sin], axis=-1)
    return out.astype(x.dtype)

def axial_rope(x, row_ids, col_ids):
    half = x.shape[-1] // 2
    return jnp.concatenate([rope_1d(x[..., :half], row_ids),
                            rope_1d(x[..., half:], col_ids)], axis=-1)

def t5_bucket(rel):
    nb = N_REL_BUCKETS // 2
    ret = (rel > 0).astype(np.int32) * nb
    n = np.abs(rel)
    max_exact = nb // 2
    large = max_exact + (np.log(np.maximum(n, 1) / max_exact)
                         / math.log(REL_MAX_DIST_2 / max_exact)
                         * (nb - max_exact)).astype(np.int32)
    large = np.minimum(large, nb - 1)
    return ret + np.where(n < max_exact, n, large).astype(np.int32)

def mixer_a(q, k, v, q_g, k_g, row_ids, col_ids):
    b, s, hq, hd = q.shape
    hkv = k.shape[2]
    grp = hq // hkv
    q = axial_rope(rmsnorm_2(q, q_g), row_ids, col_ids) * (hd ** -0.5)
    k = axial_rope(rmsnorm_2(k, k_g), row_ids, col_ids)
    nblk = s // Q_BLOCK
    qb = q.reshape(b, nblk, Q_BLOCK, hkv, grp, hd).transpose(1, 0, 3, 4, 2, 5)
    kt = k.transpose(0, 2, 1, 3)
    vt = v.transpose(0, 2, 1, 3)

    def attend(qblk):
        sc = jnp.einsum('bkgqd,bksd->bkgqs', qblk, kt).astype(jnp.float32)
        pr = jax.nn.softmax(sc, axis=-1).astype(vt.dtype)
        return jnp.einsum('bkgqs,bksd->bkgqd', pr, vt)

    o = lax.map(attend, qb)
    return o.transpose(1, 0, 4, 2, 3, 5).reshape(b, s, hq * hd)

def dilated_group(q, k, v, bias_table, window, dilation):
    b, s, hh, hd = q.shape
    L = s // dilation
    W = window // (2 * dilation)
    qb_len = math.gcd(L, BAND_BLOCK)
    nb = L // qb_len
    kw_len = qb_len + 2 * W

    def to_sub(t):
        return t.reshape(b, L, dilation, hh, hd).transpose(0, 2, 3, 1, 4)

    off = np.arange(kw_len)[None, :] - W - np.arange(qb_len)[:, None]
    band = np.abs(off) <= W
    kpos = np.arange(nb)[:, None] * qb_len - W + np.arange(kw_len)[None, :]
    inb = (kpos >= 0) & (kpos < L)
    mask = band[None, :, :] & inb[:, None, :]
    bucket = t5_bucket(off * dilation)
    bias = bias_table[bucket].astype(jnp.float32).transpose(2, 0, 1)
    idx = np.arange(nb)[:, None] * qb_len + np.arange(kw_len)[None, :]

    qs = to_sub(q).reshape(b, dilation, hh, nb, qb_len, hd) * (hd ** -0.5)
    pad = ((0, 0), (0, 0), (0, 0), (W, W), (0, 0))
    ks = jnp.pad(to_sub(k), pad)[:, :, :, idx, :]
    vs = jnp.pad(to_sub(v), pad)[:, :, :, idx, :]
    sc = jnp.einsum('bchnqd,bchnkd->bchnqk', qs, ks).astype(jnp.float32) + bias[:, None]
    sc = jnp.where(mask, sc, NEG_INF)
    lse = jax.nn.logsumexp(sc, axis=-1)
    pr = jnp.exp(sc - lse[..., None]).astype(vs.dtype)
    o = jnp.einsum('bchnqk,bchnkd->bchnqd', pr, vs)
    o = o.reshape(b, dilation, hh, L, hd).transpose(0, 3, 1, 2, 4).reshape(b, s, hh, hd)
    lse = lse.reshape(b, dilation, hh, L).transpose(0, 3, 1, 2).reshape(b, s, hh)
    return o, lse

def mixer_b(q, k, v, rel_bias):
    b, s, _, hd = q.shape
    outs, lses = [], []
    for g, (window, dilation) in enumerate(DIL_PAIRS):
        sl = slice(g * N_HEADS_PER_DIL, (g + 1) * N_HEADS_PER_DIL)
        o, l = dilated_group(q[:, :, sl], k[:, :, sl], v[:, :, sl], rel_bias[:, sl], window, dilation)
        outs.append(o)
        lses.append(l)
    wts = jax.nn.softmax(jnp.stack(lses, axis=0), axis=0).astype(q.dtype)
    o = jnp.sum(wts[..., None] * jnp.stack(outs, axis=0), axis=0)
    return o.reshape(b, s, N_HEADS_PER_DIL * hd)

def second_inputs(seed: int = 0) -> dict:
    key = jax.random.key(seed)
    ks = jax.random.split(key, 20)
    f32 = jnp.float32

    def w(k, shape, fan_in):
        return jax.random.normal(k, shape, f32) * (fan_in ** -0.5)

    def gain(k, shape):
        return 1.0 + 0.05 * jax.random.normal(k, shape, f32)

    return {
        "x": jax.random.normal(ks[0], (BATCH, SEQ, D_MODEL), f32),
        "p": jax.random.normal(ks[1], (DEPTH_2, BATCH, SEQ, D_PLE), f32),
        "norm_mix_g": gain(ks[2], (DEPTH_2, D_MODEL)),
        "w_in": w(ks[3], (DEPTH_2, D_MODEL, D_IN_PROJ), D_MODEL),
        "b_gate": 0.02 * jax.random.normal(ks[4], (DEPTH_2, 2 * D_MODEL), f32),
        "q_norm_g": gain(ks[5], (DEPTH_2, HEAD_DIM_A)),
        "k_norm_g": gain(ks[6], (DEPTH_2, HEAD_DIM_A)),
        "rel_bias": 0.5 * jax.random.normal(ks[7], (N_REL_BUCKETS, N_HEADS_B), f32),
        "w_out_a": w(ks[8], (DEPTH_2, N_Q_HEADS_A * HEAD_DIM_A, D_MODEL), N_Q_HEADS_A * HEAD_DIM_A),
        "w_out_b": w(ks[9], (DEPTH_2, N_HEADS_PER_DIL * HEAD_DIM_B, D_MODEL), N_HEADS_PER_DIL * HEAD_DIM_B),
        "w_out": w(ks[10], (DEPTH_2, D_MODEL, D_MODEL), D_MODEL),
        "norm_mlp_g": gain(ks[11], (DEPTH_2, D_MODEL)),
        "w_ff1": w(ks[12], (DEPTH_2, D_MODEL, D_FF_2), D_MODEL),
        "w_ff2": w(ks[13], (DEPTH_2, D_FF_2, D_MODEL), D_FF_2),
        "norm_ple_g": gain(ks[14], (DEPTH_2, D_MODEL)),
        "w_ple_gate": w(ks[15], (DEPTH_2, D_MODEL, D_MODEL), D_MODEL),
        "w_ple": w(ks[16], (DEPTH_2, D_PLE, D_MODEL), D_PLE),
        "final_norm_g": gain(ks[17], (D_MODEL,)),
    }

def second_block(x, p, norm_mix_g, w_in, b_gate, q_norm_g, k_norm_g, rel_bias,
              w_out_a, w_out_b, w_out, norm_mlp_g, w_ff1, w_ff2,
              norm_ple_g, w_ple_gate, w_ple, final_norm_g):
    b, s, _ = x.shape
    rows = s // GRID_W
    row_ids = jnp.repeat(jnp.arange(rows, dtype=jnp.int32), GRID_W)
    col_ids = jnp.arange(s, dtype=jnp.int32) % GRID_W
    split_at = list(np.cumsum(SPLIT_SIZES)[:-1])

    for i in range(DEPTH_2):
        h = rmsnorm_2(x, norm_mix_g[i])
        z = h @ w_in[i]
        qa, ka, va, qb, kb, vb, ga, gb = jnp.split(z, split_at, axis=-1)
        qa = qa.reshape(b, s, N_Q_HEADS_A, HEAD_DIM_A)
        ka = ka.reshape(b, s, N_KV_HEADS_A, HEAD_DIM_A)
        va = va.reshape(b, s, N_KV_HEADS_A, HEAD_DIM_A)
        qb = qb.reshape(b, s, N_HEADS_B, HEAD_DIM_B)
        kb = kb.reshape(b, s, N_HEADS_B, HEAD_DIM_B)
        vb = vb.reshape(b, s, N_HEADS_B, HEAD_DIM_B)

        y_a = mixer_a(qa, ka, va, q_norm_g[i], k_norm_g[i], row_ids, col_ids) @ w_out_a[i]
        y_b = mixer_b(qb, kb, vb, rel_bias) @ w_out_b[i]
        gate_a = jax.nn.sigmoid(ga + b_gate[i, :D_MODEL])
        gate_b = jax.nn.sigmoid(gb + b_gate[i, D_MODEL:])
        x = x + (gate_a * y_a + gate_b * y_b) @ w_out[i]

        h = rmsnorm_2(x, norm_mlp_g[i])
        x = x + jnp.square(jax.nn.relu(h @ w_ff1[i])) @ w_ff2[i]

        gate_p = jax.nn.sigmoid(rmsnorm_2(x, norm_ple_g[i]) @ w_ple_gate[i])
        x = x + gate_p * (p[i] @ w_ple[i])

    return rmsnorm_2(x, final_norm_g)


def setup_inputs(seed=0):
    out = dict(first_inputs(seed))
    for name, value in second_inputs(seed + 1).items():
        if name != "x":
            out[name + "_2"] = value
    return out


def reference(
    x, a_w_in, a_w_gk2, a_b_gk, a_onorm, a_w_out, kv_norm, w_kv, b_w_q, b_sinks, b_w_out,
    rel_table, ln_mix, ln_mlp, w_up, w_down, ln_final, p_2, norm_mix_g_2, w_in_2, b_gate_2,
    q_norm_g_2, k_norm_g_2, rel_bias_2, w_out_a_2, w_out_b_2, w_out_2, norm_mlp_g_2, w_ff1_2,
    w_ff2_2, norm_ple_g_2, w_ple_gate_2, w_ple_2, final_norm_g_2,
):
    x = first_block(
        x, a_w_in, a_w_gk2, a_b_gk, a_onorm, a_w_out, kv_norm, w_kv, b_w_q, b_sinks, b_w_out,
        rel_table, ln_mix, ln_mlp, w_up, w_down, ln_final,
    )
    return second_block(
        x, p_2, norm_mix_g_2, w_in_2, b_gate_2, q_norm_g_2, k_norm_g_2, rel_bias_2, w_out_a_2,
        w_out_b_2, w_out_2, norm_mlp_g_2, w_ff1_2, w_ff2_2, norm_ple_g_2, w_ple_gate_2, w_ple_2,
        final_norm_g_2,
    )


_drawn_inputs = setup_inputs


def setup_inputs(seed=0):
    import zlib

    import numpy as np

    out = dict(_drawn_inputs(seed))
    spreads = {}
    factors = {'a_onorm': 5.153,
     'kv_norm': 8.0,
     'b_sinks': 6.324,
     'ln_mlp': 3.58,
     'ln_final': 2.669,
     'norm_mix_g_2': 4.493,
     'b_gate_2': 8.0,
     'q_norm_g_2': 8.0,
     'k_norm_g_2': 8.0,
     'norm_ple_g_2': 62.84,
     'norm_mlp_g_2': 3.688}
    for name, (base, spread) in spreads.items():
        noise = np.random.default_rng([zlib.crc32(name.encode()), seed]).standard_normal(out[name].shape)
        drawn = base * np.exp(spread * noise) if base else spread * noise
        out[name] = __import__('jax').numpy.asarray(drawn.astype(out[name].dtype))
    for name, factor in factors.items():
        out[name] = (out[name] * factor).astype(out[name].dtype)
    return out
```

```python
from contextlib import ExitStack

import concourse.bass as bass
from concourse import mybir
import numpy as np

ALU = mybir.AluOpType
ACT = mybir.ActivationFunctionType
F32 = mybir.dt.float32
F32R = mybir.dt.float32r
I32 = mybir.dt.int32
AX = mybir.AxisListType.X

T, D, FF = 256, 1024, 4096
EPS = 1e-6
NR = 3
NS = 3
SLOT = 2048
PROJ = 3088


class Tok:

    def __init__(self, sem=None, val=None):
        self.sem, self.val, self.used = sem, val, False


class Queue:

    def __init__(self, sem):
        self.sem, self.items = sem, []

    def __call__(self, fn, *waits):
        for w in waits:
            for t in (w if isinstance(w, (list, tuple)) else (w,)):
                if t is not None:
                    t.used = True
                    self.items.append((None, t))
        tok = Tok(self.sem)
        self.items.append((fn, tok))
        return tok

    def number(self):
        n = 0
        for fn, t in self.items:
            if fn is not None and t.used and t.val is None:
                n += 1
                t.val = n

    def write(self, eng):
        met = {}
        for fn, t in self.items:
            if fn is None:
                if met.get(id(t.sem), 0) < t.val:
                    eng.wait_ge(t.sem, t.val)
                    met[id(t.sem)] = t.val
            else:
                ins = fn(eng)
                if t.used:
                    ins.then_inc(t.sem, 1)


class Dma:

    def __init__(self, new_sem):
        self.new_sem, self.items, self.sems = new_sem, [], {}

    def __call__(self, name, out, in_, *waits):
        sem, n = self.sems.get(name) or (self.new_sem("d_" + name), 0)
        self.sems[name] = (sem, n + 16)
        for w in waits:
            for t in (w if isinstance(w, (list, tuple)) else (w,)):
                if t is not None:
                    t.used = True
                    self.items.append((None, t))
        tok = Tok(sem, n + 16)
        self.items.append(((out, in_), tok))
        return tok

    def write(self, eng):
        met = {}
        for what, t in self.items:
            if what is None:
                if met.get(id(t.sem), 0) < t.val:
                    eng.wait_ge(t.sem, t.val)
                    met[id(t.sem)] = t.val
            else:
                eng.dma_start(*what).then_inc(t.sem, 16)


class Bank:
    def __init__(self, t):
        self.t, self.free = t, None


class Stream:

    def __init__(self, plan, q, raw, hi, lo):
        self.plan, self.q, self.raw, self.hi, self.lo = plan, q, raw, hi, lo
        self.seen, self.i = [], 0
        self.loaded, self.split, self.used = [], [], []

    def _load(self, j):
        srcs = self.plan[j]
        s = j % NR
        at, toks = 0, []
        free = self.split[j - NR] if j >= NR else None
        for src, kt, n in srcs:
            dst = self.raw[:, s, at:at + kt * n].rearrange("p (k n) -> p k n", k=kt)
            toks.append(self.q.sp("w%d" % s, dst, src.rearrange("(k p) n -> p k n", p=128), free))
            at += kt * n
        self.loaded.append((toks[-1], at))

    def _split(self, j):
        tok, n = self.loaded[j]
        r, h, l = self.raw[:, j % NR, 0:n], self.hi[:, j % NS, 0:n], self.lo[:, j % NS, 0:n]
        free = self.used[j - NS] if j >= NS else None
        a = self.q.act(lambda e: e.activation(h, r, ACT.Copy), tok, free)
        d = self.q.dve(lambda e: e.tensor_tensor(l, r, h.bitcast(F32), ALU.subtract), tok, free, a)
        self.split.append([a, d])

    def next(self, srcs):
        self.seen.append(srcs)
        i = self.i
        self.i += 1
        assert len(self.used) == i, "a block is taken before the last is given back"
        if self.plan is None:
            self.split.append(None)
            n = sum(k * c for _, k, c in srcs)
            return self.hi[:, 0, 0:n], self.lo[:, 0, 0:n], None
        last = len(self.plan)
        while len(self.split) < min(i + NS, last):
            while len(self.loaded) < min(len(self.split) + NR, last):
                self._load(len(self.loaded))
            self._split(len(self.split))
        while len(self.loaded) < min(len(self.split) + NR, last):
            self._load(len(self.loaded))
        n = self.loaded[i][1]
        return self.hi[:, i % NS, 0:n], self.lo[:, i % NS, 0:n], self.split[i]

    def start(self):
        while self.plan is not None and len(self.loaded) < NR:
            self._load(len(self.loaded))

    def done(self, tok):
        self.used.append(tok)


class Queues:
    def __init__(self, sems, dma_sem):
        self.pe, self.dve, self.act, self.pool = (Queue(s) for s in sems)
        self.sp = Dma(dma_sem)


def run_all(*gens):
    gens = [(g, n) for g, n in gens]
    while gens:
        for it in list(gens):
            g, n = it
            for _ in range(n):
                try:
                    next(g)
                except StopIteration:
                    gens.remove(it)
                    break


def write_program(q, S, st, A, banks):
    pe, dve, act, pool, sp = q.pe, q.dve, q.act, q.pool, q.sp
    M, RR, xs, x = S["M"], S["RR"], S["xs"], S["x"]
    hT = (RR[:, 0:2048].rearrange("p (k t) -> p k t", t=T), RR[:, 2048:4096].rearrange("p (k t) -> p k t", t=T))
    acc, misc = banks[0:4], banks[4:8]
    turn = {"misc": 0, "acc": 0}

    def misc_bank():
        turn["misc"] += 1
        return misc[(turn["misc"] - 1) % 4]

    def acc_pair():
        turn["acc"] += 1
        n = (turn["acc"] - 1) % 2
        return [acc[2 * n], acc[2 * n + 1]]

    def mm(out, lhsT, rhs, start, stop, *w):
        return pe(lambda e: e.matmul(out, lhsT, rhs, start=start, stop=stop, skip_group_check=True), *w)

    def tr(out, in_, *w):
        n = in_.shape[0]
        return pe(lambda e: e.transpose(out, in_, S["ident"][0:n, 0:n]), *w)

    def copy(eng, out, in_, *w):
        if eng is act:
            return act(lambda e: e.activation(out, in_, ACT.Copy), *w)
        return eng(lambda e: e.tensor_copy(out, in_), *w)

    def tt(eng, out, a, b, op, *w):
        return eng(lambda e: e.tensor_tensor(out, a, b, op), *w)

    def ts(eng, out, a, s1, s2, op0, op1, *w):
        if s2 is None:
            return eng(lambda e: e.tensor_scalar(out, a, s1, None, op0), *w)
        return eng(lambda e: e.tensor_scalar(out, a, s1, s2, op0, op1), *w)

    def stt(out, a, s, b, op0, op1, *w):
        return dve(lambda e: e.scalar_tensor_tensor(out=out, in0=a, scalar=s, in1=b, op0=op0, op1=op1), *w)

    def actf(out, in_, f, *w, **k):
        return act(lambda e: e.activation(out, in_, f, **k), *w)

    def prod(out, sh, sl, mh, ml, first, last, *w):
        mm(out, sh, mh, first, False, *w)
        mm(out, sh, ml, False, False)
        return mm(out, sl, mh, False, last)

    t_id = sp("id", S["ident"][:, :], A["c_ident"])
    t_x = sp("x", x[:, :, :], A["x"].rearrange("a (c p) d -> p (a c) d", p=128))
    st.start()
    t_g = None
    gin = M[0:68, 0:128]
    for n, (name, rows) in enumerate([("ln_mix", 16), ("ln_mlp", 16), ("kv_norm", 8), ("norm_mix_g_2", 8),
                                      ("norm_mlp_g_2", 8), ("norm_ple_g_2", 8), ("a_b_gk", 4)]):
        a = A[name]
        a = a.rearrange("a (k p) -> (a k) p", p=128) if len(a.shape) == 2 else a.rearrange("(k p) -> k p", p=128)
        o = sum([16, 16, 8, 8, 8, 8, 4][:n])
        t_g = sp("g", M[o:o + rows, 0:128], a)
    t_gk2 = sp("gk2", S["gk2"][:, :], A["a_w_gk2"][0])
    t_tab = sp("tab", S["tab"][0:32, 0:16], A["rel_table"])
    t_tab = sp("tab", S["tab"][0:32, 16:28], A["rel_bias_2"])
    t_sel = sp("sel", S["sel"], A["c_sel"])
    t_msk = sp("msk", S["mask"][:, :], A["c_mask"])

    def spread(a):
        n = a.shape[-1]
        return bass.AP(tensor=a.tensor, offset=a.offset, ap=[[0, 128], [1, n]])

    t_bc = sp("bc", S["onorm"], spread(A["a_onorm"]))
    t_bc = sp("bc", S["qg"], spread(A["q_norm_g_2"]))
    t_bc = sp("bc", S["kg"], spread(A["k_norm_g_2"]))
    t_bc = sp("bc", S["sink"], spread(A["b_sinks"]))
    for n in range(2):
        t_bc = sp("bc", S["cos"][:, n, :], A["c_cos"][n * 128:n * 128 + 128, :])
        t_bc = sp("bc", S["sin"][:, n, :], A["c_sin"][n * 128:n * 128 + 128, :])

    t_ms = pool(lambda e: e.memset(S["tab"][32:33, :], -1e30))
    t_hm = pool(lambda e: e.memset(S["half_"][:, :], -0.5), t_ms)
    t_one = pool(lambda e: e.memset(S["scan"][:, :], 1.0))
    t_one = pool(lambda e: e.memset(S["scan"][:, :].rearrange("p (c t) -> p c t", t=64)[:, :, 0:1], 0.0), t_one)
    AT = M[:, 17408:18432]
    t_at0 = pool(lambda e: e.memset(AT, 0.0))

    b = misc_bank()
    t = tr(b.t[:, 0:68], gin, t_id, t_g)
    t_G = copy(dve, S["G"][:, :], b.t[:, 0:68], t)
    b.free = [t_G]
    G = S["G"]

    b = misc_bank()
    t = mm(b.t[0:16, 0:383], S["tab"][0:33, 0:16], S["sel"][:, 0:383], True, True, b.free, t_tab, t_ms, t_sel)
    r = copy(dve, M[0:16, 14336:14719], b.t[0:16, 0:383], t)
    b.free = [r]
    t_scr1 = sp("scr1", A["scr1"], M[0:16, 14336:14719], r)
    for g in range(3):
        b = misc_bank()
        t = mm(b.t[0:4, 0:511], S["tab"][0:33, 16 + 4 * g:20 + 4 * g], S["sel"][:, 383 + 511 * g:894 + 511 * g],
               True, True, b.free)
        r = copy(dve, M[32 * g:32 * g + 4, 14848:15359], b.t[0:4, 0:511], t)
        b.free = [r]
        t_scr2 = sp("scr2", A["scr2"][4 * g:4 * g + 4, :], M[32 * g:32 * g + 4, 14848:15359], r)

    def norm(w, gains, ts_=None):
        st_ = S["st"]
        a = act(lambda e: e.activation(xs[:, 0, :], x[:, 0, :], ACT.Square, accum_out=st_[:, 0:1]), w, q.xs_free)
        d = dve(lambda e: e.tensor_tensor_reduce(xs[:, 1, :], x[:, 1, :], x[:, 1, :], 1.0, 0.0, ALU.mult, ALU.add,
                                                 st_[:, 1:2]), w, q.xs_free)
        p = ts(pool, st_[:, 2:4], st_[:, 0:2], 1.0 / D, EPS, ALU.mult, ALU.add, a, d)
        p = tt(pool, st_[:, 4:6], st_[:, 2:4], S["half"][:, :], ALU.pow, p, t_hm)
        a = actf(xs[:, 1, :], x[:, 1, :], ACT.Copy, p, d, scale=st_[:, 5:6])
        d = ts(dve, xs[:, 0, :], x[:, 0, :], st_[:, 4:5], None, ALU.mult, None, p, a)
        parts = []
        for k2 in range(4):
            b = misc_bank()
            for j in range(2):
                k = 2 * k2 + j
                for c in range(2):
                    t = tr(b.t[:, j * 256 + c * 128:j * 256 + c * 128 + 128], xs[:, c, k * 128:k * 128 + 128],
                           b.free, d, a, t_id)
            last = None
            for j in range(2):
                k = 2 * k2 + j
                for col, (hi, lo) in gains:
                    src = b.t[:, j * 256:j * 256 + 256]
                    g = G[:, col + k:col + k + 1]
                    h = actf(hi[:, k, :], src, ACT.Copy, t, last, q.hT_free, t_G, scale=g)
                    last = stt(lo[:, k, :], src, g, hi[:, k, :].bitcast(F32), ALU.mult, ALU.subtract, h, q.hT_free)
            b.free = [last]
            parts.append(last)
        q.xs_free = [t]
        return parts

    def gemm_a(w, c0, n, xT, ready, evac):
        kt = xT[0].shape[1]
        for f in range(0, n, 256):
            m = min(256, n - f)
            hi, lo, split = st.next([(w[:, c0 + f:c0 + f + m], kt, m)])
            hi = hi.rearrange("p (k n) -> p k n", k=kt)
            lo = lo.rearrange("p (k n) -> p k n", k=kt)
            b = misc_bank()
            for j in range(0, m, 128):
                mj = min(128, m - j)
                for k in range(kt):
                    t = prod(b.t[0:mj, 2 * j:2 * j + 256], hi[:, k, j:j + mj], lo[:, k, j:j + mj],
                             xT[0][:, k, :], xT[1][:, k, :], k == 0, k == kt - 1, b.free, split, ready)
                if j + 128 < m:
                    yield
            st.done(t)
            evac(f, m, b, t)
            yield

    def gemm_b(w, c0, n, xT, ready, evac, width=512):
        kt = xT[0].shape[1]
        for f in range(0, n, width):
            m = min(width, n - f)
            per = min(kt, SLOT // m)
            bs = acc_pair()
            for k0 in range(0, kt, per):
                hi, lo, split = st.next([(w[k0 * 128:(k0 + per) * 128, c0 + f:c0 + f + m], per, m)])
                hi = hi.rearrange("p (k n) -> p k n", k=per)
                lo = lo.rearrange("p (k n) -> p k n", k=per)
                for c in range(2):
                    for k in range(k0, k0 + per):
                        t = prod(bs[c].t[:, 0:m], xT[0][:, k, c * 128:c * 128 + 128],
                                 xT[1][:, k, c * 128:c * 128 + 128], hi[:, k - k0, :], lo[:, k - k0, :],
                                 k == 0, k == kt - 1, bs[c].free, split, ready)
                    if k0 + per == kt:
                        evac(f, m, c, bs[c], t)
                    if c == 0:
                        yield
                st.done(t)
                yield

    def split_parts(hi, lo, src, *w):
        h = copy(act, hi, src, *w)
        return tt(dve, lo, src, hi.bitcast(F32), ALU.subtract, h, *w)

    def turn_parts(src, n, hi, lo, w, free, toks=None):
        last = None
        for k2 in range(0, n // 128, 2):
            b = misc_bank()
            for j in range(2):
                for c in range(2):
                    t = tr(b.t[:, j * 256 + c * 128:j * 256 + c * 128 + 128],
                           src[:, c, (k2 + j) * 128:(k2 + j) * 128 + 128], b.free, w, t_id)
            last = split_parts(hi[:, k2:k2 + 2, :].rearrange("p k t -> p (k t)"),
                               lo[:, k2:k2 + 2, :].rearrange("p k t -> p (k t)"), b.t[:, :], t, free)
            b.free = [last]
        return last, t

    q.xw = [t_x]

    def add_x(f, m, c, b, t):
        r = tt(dve, x[:, c, f:f + m], x[:, c, f:f + m], b.t[:, 0:m], ALU.add, t, q.xw)
        b.free = [r]
        q.xn.append(r)

    def project(w, xT, ready):
        q.xn = []
        run_all((gemm_b(w, 0, D, xT, ready, add_x), 1))
        q.xw = q.xn[-2:]

    def mlp(up, down, gain):
        ready = norm(q.xw, [(gain, hT)])
        uT = [(RR[:, 4096 + 2048 * i:5120 + 2048 * i].rearrange("p (k t) -> p k t", t=T),
               RR[:, 5120 + 2048 * i:6144 + 2048 * i].rearrange("p (k t) -> p k t", t=T)) for i in range(2)]
        state = {"n": 0, "u": {}}

        def evac(f, m, b, t):
            n = state["n"]
            state["n"] += 1
            i, o = (n // 2) % 2, (n % 2) * 2
            r = M[:, 1024 + 512 * (n % 4):1536 + 512 * (n % 4)]
            a = actf(r, b.t[:, :], ACT.Relu, t, q.m_free)
            b.free = [a]
            d = tt(dve, r, r, r, ALU.mult, a)
            hi = uT[i][0][:, o:o + 2, :].rearrange("p k t -> p (k t)")
            lo = uT[i][1][:, o:o + 2, :].rearrange("p k t -> p (k t)")
            h = copy(act, hi, r, d, q.u_free[i])
            state["u"][n // 2] = tt(dve, lo, r, hi.bitcast(F32), ALU.subtract, h)

        def down_chunk(c4):
            i = c4 % 2
            for kk in range(2):
                k0 = c4 * 4 + kk * 2
                hi, lo, split = st.next([(down[k0 * 128:k0 * 128 + 256, :], 2, D)])
                hi = hi.rearrange("p (k n) -> p k n", k=2)
                lo = lo.rearrange("p (k n) -> p k n", k=2)
                for c in range(2):
                    for k in range(2):
                        for n in range(2):
                            b = acc[2 * c + n]
                            sl = slice(c * 128, c * 128 + 128)
                            t = prod(b.t[:, :], uT[i][0][:, kk * 2 + k, sl], uT[i][1][:, kk * 2 + k, sl],
                                     hi[:, k, n * 512:n * 512 + 512], lo[:, k, n * 512:n * 512 + 512],
                                     k0 + k == 0, k0 + k == 31, b.free, split, state["u"][c4])
                st.done(t)
            q.u_free[i] = [t]
            return t

        def up_chunk(c4):
            run_all((gemm_a(up, c4 * 512, 512, hT, ready, evac), 1))

        up_chunk(0)
        for c4 in range(8):
            if c4 < 7:
                up_chunk(c4 + 1)
            if c4 == 6:
                q.hT_free = None
            t = down_chunk(c4)
        q.hT_free = [t]
        q.xn = []
        for c in range(2):
            for n in range(2):
                add_x(n * 512, 512, c, acc[2 * c + n], t)
        q.xw = q.xn
        q.m_free = [q.xn[-1]]

    q.u_free = [None, None]
    q.xs_free = None
    q.hT_free = None
    q.m_free = None

    ready = norm(q.xw, [(0, hT)])
    W = A["a_w_in"][0]
    qT, kT = M[:, 0:1024], M[:, 1024:2048]
    bc, e1 = M[:, 2048:3072], M[:, 3072:4096]
    qt, kt_, kd = M[:, 4096:5120], M[:, 5120:6144], M[:, 6144:7168]
    kdt = M[:, 7168:8192]
    V = M[:, 8192:10240].rearrange("p (c n) -> p c n", c=2)
    GT = M[:, 10240:12288].rearrange("p (c n) -> p c n", c=2)
    O = M[:, 12288:14336].rearrange("p (c n) -> p c n", c=2)
    ST = M[:, 14336:17408]
    glr = xs[0:16, 0, 0:256]
    ev = {"qk": []}

    def ev_glr(f, m, b, t):
        r = copy(dve, glr, b.t[0:16, 0:256], t, q.xs_free)
        b.free = [r]
        ev["glr"] = r

    def ev_qk(f, m, b, t):
        dst = M[:, 2 * f:2 * f + 512]
        sc = 128 ** -0.5 if f < 512 else 1.0
        r = actf(dst, b.t[:, :], ACT.Copy, t, t_G, scale=sc)
        b.free = [r]
        ev["qk"].append(r)

    run_all((gemm_a(W, 3072, 16, hT, ready, ev_glr), 1))
    t_toe1 = sp("toe1", A["toe1"], bass.AP(tensor=A["scr1"].tensor, offset=127, ap=[[383, 16], [-1, 128], [1, 256]]),
                t_scr1)
    t_toe2 = sp("toe2", A["toe2"], bass.AP(tensor=A["scr2"].tensor, offset=127, ap=[[511, 12], [-1, 128], [1, 384]]),
                t_scr2)

    def gates():
        for h2 in range(2):
            b = misc_bank()
            for j in range(2):
                h = 2 * h2 + j
                t = mm(b.t[:, j * 256:j * 256 + 256], S["gk2"][:, h * 128:h * 128 + 128], glr, True, True,
                       ev["glr"], t_gk2, b.free)
            for j in range(2):
                h = 2 * h2 + j
                d = ts(dve, bc[:, h * 256:h * 256 + 256], b.t[:, j * 256:j * 256 + 256], G[:, 64 + h:65 + h], None,
                       ALU.add, None, t, t_G)
            b.free = [d]
            yield
        q.xs_free = [t]
        a = actf(e1, bc, ACT.Abs, d)
        a = actf(e1, e1, ACT.Exp, a, scale=-1.0)
        a = actf(e1, e1, ACT.Ln, a, bias=1.0)
        d = ts(dve, bc, bc, 0.0, None, ALU.min, None, d, a)
        d = tt(dve, e1, bc, e1, ALU.subtract, a, d)
        d = ts(dve, e1, e1, 1.0 / 16.0, None, ALU.mult, None, d)
        yield
        for h in range(4):
            sl = slice(h * 256, h * 256 + 256)
            d2 = dve(lambda e, sl=sl: e.tensor_tensor_scan(bc[:, sl], S["scan"][:, :], e1[:, sl], 0.0, ALU.mult,
                                                           ALU.add), d, t_one)
        yield
        a = actf(qt, bc, ACT.Exp, d2)
        a2 = actf(kt_, bc, ACT.Exp, d2, scale=-1.0)
        d = None
        for h in range(4):
            for c in range(4):
                o = h * 256 + c * 64
                d = ts(pool, kd[:, o:o + 64], bc[:, o:o + 64], bc[:, o + 63:o + 64], None, ALU.subtract, None, d2)
        a3 = actf(kd, kd, ACT.Exp, d, scale=-1.0)
        p = copy(pool, S["ebl"][:, :], qt.rearrange("p (g t) -> p g t", t=64)[:, :, 63:64].rearrange("p g t -> p (g t)"), a)
        ev["ebl"] = p
        yield
        ev["exps"] = (a, a2, a3)

    run_all((gemm_a(W, 0, 1024, hT, ready, ev_qk), 1), (gates(), 1))
    ev["qt"] = tt(dve, qt, qt, qT, ALU.mult, ev["exps"][0], ev["ebl"], ev["qk"])
    ev["kt"] = tt(dve, kt_, kt_, kT, ALU.mult, ev["exps"][1], ev["qk"])
    ev["kd"] = tt(pool, kd, kd, kT, ALU.mult, ev["exps"][2], ev["qk"])

    def ev_v(f, m, c, b, t):
        r = copy(act, V[:, c, f:f + m], b.t[:, 0:m], t)
        b.free = [r]
        ev.setdefault("v", []).append(r)

    def ev_gate(f, m, c, b, t):
        sg = xs[:, c, 0:512]
        a = actf(sg, b.t[:, 0:m], ACT.Sigmoid, t, q.xs_free, ev.get("g"))
        r = tt(dve, GT[:, c, f:f + m], sg, b.t[:, 0:m], ALU.mult, a)
        b.free = [r]
        ev["g"] = r

    def attn_gla():
        for h2 in range(2):
            b = misc_bank()
            for j in range(2):
                h = 2 * h2 + j
                for c in range(2):
                    t = tr(b.t[:, j * 256 + c * 128:j * 256 + c * 128 + 128],
                           kd[:, h * 256 + c * 128:h * 256 + c * 128 + 128], b.free, ev["kd"], t_id)
            r = copy(act, kdt[:, h2 * 512:h2 * 512 + 512], b.t[:, :], t)
            b.free = [r]
            ev["kdt"] = r
            yield
            b = misc_bank()
            for j in range(2):
                h = 2 * h2 + j
                for c in range(2):
                    sl = slice(h * 256 + c * 128, h * 256 + c * 128 + 128)
                    t = mm(b.t[:, j * 256 + c * 128:j * 256 + c * 128 + 128], kt_[:, sl], qt[:, sl], True, True,
                           b.free, ev["kt"], ev["qt"])
            msk = S["mask"][:, :]
            for n in range(4):
                r = dve(lambda e, n=n, b=b, h2=h2: e.copy_predicated(
                    AT[:, h2 * 512 + n * 128:h2 * 512 + n * 128 + 128], msk, b.t[:, n * 128:n * 128 + 128]),
                    t, t_at0, t_msk)
            b.free = [r]
            ev["at"] = r
            yield
        prev = None
        for c in range(3):
            rows = slice(64 * (c % 2), 64 * (c % 2) + 64)
            for h2 in range(2):
                b = misc_bank()
                for j in range(2):
                    h = 2 * h2 + j
                    t = mm(b.t[:, j * 256:j * 256 + 256], kdt[rows, h * 256 + (c // 2) * 128:h * 256 + (c // 2) * 128 + 128],
                           V[rows, c // 2, h * 256:h * 256 + 256], True, True, b.free, ev["kdt"], ev["v"])
                for j in range(2):
                    h = 2 * h2 + j
                    o = c * 1024 + h * 256
                    if c == 0:
                        r = copy(dve, ST[:, o:o + 256], b.t[:, j * 256:j * 256 + 256], t, t_scr1, t_scr2)
                    else:
                        r = stt(ST[:, o:o + 256], ST[:, o - 1024:o - 768], S["ebl"][:, h * 4 + c:h * 4 + c + 1],
                                b.t[:, j * 256:j * 256 + 256], ALU.mult, ALU.add, t, prev, ev["ebl"])
                b.free = [r]
            prev = r
            yield
        ev["st"] = prev
        for c2 in range(2):
            for h2 in range(2):
                b = misc_bank()
                for j in range(2):
                    h = 2 * h2 + j
                    out = b.t[:, j * 256:j * 256 + 256]
                    mm(out, AT[:, h * 256 + c2 * 128:h * 256 + c2 * 128 + 128], V[:, c2, h * 256:h * 256 + 256],
                       True, False, b.free, ev["at"], ev["v"])
                    for c in (2 * c2, 2 * c2 + 1):
                        if c:
                            rows = slice(64 * (c % 2), 64 * (c % 2) + 64)
                            t = mm(b.t[rows, j * 256:j * 256 + 256], qt[:, h * 256 + c * 64:h * 256 + c * 64 + 64],
                                   ST[:, (c - 1) * 1024 + h * 256:(c - 1) * 1024 + h * 256 + 256], False, True,
                                   ev["st"])
                r = copy(act, O[:, c2, h2 * 512:h2 * 512 + 512], b.t[:, :], t)
                b.free = [r]
                for j in range(2):
                    h = 2 * h2 + j
                    n = h * 2 + c2
                    s = O[:, c2, h * 256:h * 256 + 256]
                    r2 = dve(lambda e, s=s, n=n, j=j: e.tensor_tensor_reduce(
                        S["sq"][:, 0:256], s, s, 1.0, 0.0, ALU.mult, ALU.add, S["st"][:, 8 + n:9 + n]), r, ev.get("sq"))
                    ev["sq"] = r2
                yield
        p = ts(pool, S["st"][:, 16:24], S["st"][:, 8:16], 1.0 / 256, EPS, ALU.mult, ALU.add, r2)
        ev["ors"] = tt(pool, S["st"][:, 24:32], S["st"][:, 16:24], S["half8"], ALU.pow, p, t_hm)

    run_all((gemm_b(W, 1024, 1024, hT, ready, ev_v), 1))
    run_all((gemm_b(W, 2048, 1024, hT, ready, ev_gate), 1), (attn_gla(), 1))
    for c in range(2):
        for h in range(4):
            s = O[:, c, h * 256:h * 256 + 256]
            r = stt(s, s, S["st"][:, 24 + h * 2 + c:25 + h * 2 + c], S["onorm"], ALU.mult, ALU.mult, ev["ors"], t_bc)
        ev["o%d" % c] = r
    for c in range(2):
        eng = (dve, pool)[c]
        ev["o%d" % c] = tt(eng, O[:, c, :], O[:, c, :], GT[:, c, :], ALU.mult, ev["o%d" % c], ev["g"])
    q.xs_free = [q.xs_free, ev["g"]] if not isinstance(q.xs_free, list) else q.xs_free + [ev["g"]]
    yT = (RR[:, 4096:6144].rearrange("p (k t) -> p k t", t=T), RR[:, 6144:8192].rearrange("p (k t) -> p k t", t=T))
    last, tp = turn_parts(O, 1024, yT[0], yT[1], [ev["o0"], ev["o1"]], None)
    q.hT_free = [tp]
    q.m_free = [tp]

    project(A["a_w_out"][0], yT, last)
    q.u_free = [q.xw, q.xw]

    BS = M[:, 13824:17920].rearrange("p (h c) -> p h c", h=16)
    t_bias = sp("bias", BS, A["toe1"].rearrange("h p c -> p h c"), t_toe1, q.m_free)
    mlp(A["w_up"][0], A["w_down"][0], 16)

    kvp = (RR[:, 4096:6144].rearrange("p (k t) -> p k t", t=T), RR[:, 6144:8192].rearrange("p (k t) -> p k t", t=T))
    hf = q.hT_free
    ready = norm(q.xw, [(8, hT), (32, kvp)])
    QT = M[:, 0:2048].rearrange("p (f t) -> p f t", t=T)
    KT = M[:, 2048:2560].rearrange("p (g t) -> p g t", t=T)
    V = M[:, 2560:2816].rearrange("p (c n) -> p c n", c=2)
    hi, lo, split = st.next([(A["w_kv"], 8, 256)])
    hi = hi.rearrange("p (k n) -> p k n", k=8)
    lo = lo.rearrange("p (k n) -> p k n", k=8)
    b = misc_bank()
    for k in range(8):
        t = prod(b.t[:, 0:256], hi[:, k, 0:128], lo[:, k, 0:128], kvp[0][:, k, :], kvp[1][:, k, :],
                 k == 0, k == 7, b.free, split, ready)
    for g in range(2):
        for half in range(2):
            r = copy(dve, KT[64 * half:64 * half + 64, g, :], b.t[64 * g:64 * g + 64, 0:256], t, q.m_free)
    b.free = [r]
    t_k = r
    b = misc_bank()
    for c in range(2):
        for k in range(8):
            t = prod(b.t[:, c * 128:c * 128 + 128], kvp[0][:, k, c * 128:c * 128 + 128],
                     kvp[1][:, k, c * 128:c * 128 + 128], hi[:, k, 128:256], lo[:, k, 128:256], k == 0, k == 7, b.free)
    st.done(t)
    t_v = copy(dve, V.rearrange("p c n -> p (c n)"), b.t[:, 0:256], t, q.m_free)
    b.free = [t_v]
    kv_used = [t]
    qtok = {}

    def ev_q(f, m, b, t):
        r = copy(act, M[:, 2 * f:2 * f + 512], b.t[:, :], t, q.m_free)
        b.free = [r]
        qtok[f // 256] = r

    oT = (RR[:, 4096:6144].rearrange("p (k t) -> p k t", t=T), RR[:, 6144:8192].rearrange("p (k t) -> p k t", t=T))
    ring = {}

    def swa():
        info = {}

        def scores(h):
            f, r0, kv = h // 2, 64 * (h % 2), h // 8
            b = acc[h % 2]
            s = M[:, 2816 + 384 * (h % 4):3200 + 384 * (h % 4)]
            mm(b.t[:, 0:128], QT[r0:r0 + 64, f, 0:128], KT[r0:r0 + 64, kv, 0:128], True, True, b.free, qtok[f // 2], t_k)
            t = mm(b.t[:, 128:384], QT[r0:r0 + 64, f, 128:256], KT[r0:r0 + 64, kv, :], True, True)
            w = ring.get(("s", h % 4))
            stt(s[:, 0:128], b.t[:, 0:128], 0.125, BS[:, h, 128:256], ALU.mult, ALU.add, t, t_bias, w)
            d = stt(s[:, 128:384], b.t[:, 128:384], 0.125, BS[:, h, :], ALU.mult, ALU.add)
            b.free = [d]
            c = S["cc"][:, 16 * (h % 4):16 * (h % 4) + 16]
            dve(lambda e: e.tensor_reduce(c[:, 0:1], s[:, 0:128], AX, ALU.max), d)
            d = dve(lambda e: e.tensor_reduce(c[:, 1:2], s[:, 128:384], AX, ALU.max))
            sk = S["sink"][:, h:h + 1]
            d = ts(dve, c[:, 2:4], c[:, 0:2], sk, -1.0, ALU.max, ALU.mult, d, t_bc)
            actf(s[:, 0:128], s[:, 0:128], ACT.Exp, d, bias=c[:, 2:3], accum_out=c[:, 4:5])
            actf(s[:, 128:384], s[:, 128:384], ACT.Exp, bias=c[:, 3:4], accum_out=c[:, 5:6])
            a = actf(c[:, 6:8], c[:, 2:4], ACT.Exp, bias=sk)
            info[h] = (s, c, a)

        def turned(h):
            s, c, a = info[h]
            d = tt(dve, c[:, 8:10], c[:, 4:6], c[:, 6:8], ALU.add, a)
            d = dve(lambda e: e.reciprocal(c[:, 10:12], c[:, 8:10]), d)
            ts(dve, s[:, 0:128], s[:, 0:128], c[:, 10:11], None, ALU.mult, None, d)
            d = ts(dve, s[:, 128:384], s[:, 128:384], c[:, 11:12], None, ALU.mult, None)
            b = misc_bank()
            for n in range(3):
                t = tr(b.t[:, n * 128:n * 128 + 128], s[:, n * 128:n * 128 + 128], b.free, d)
            ring[("s", h % 4)] = t
            p = M[:, 4352 + 384 * (h % 4):4736 + 384 * (h % 4)]
            r = copy(act, p, b.t[:, 0:384], t, ring.get(("p", h % 4)))
            b.free = [r]
            info[h] = (p, r)

        def values(h):
            p, r = info[h]
            kv = h // 8
            b = acc[2 + (h // 2) % 2]
            rows = slice(64 * (h % 2), 64 * (h % 2) + 64)
            v0, v1 = V[:, 0, 64 * kv:64 * kv + 64], V[:, 1, 64 * kv:64 * kv + 64]
            mm(b.t[rows, 0:128], v0, p[:, 0:128], True, True, b.free if h % 2 == 0 else None, r, t_v)
            mm(b.t[rows, 128:256], v0, p[:, 128:256], True, False)
            t = mm(b.t[rows, 128:256], v1, p[:, 256:384], False, True)
            ring[("p", h % 4)] = t
            if h % 2:
                r = split_parts(oT[0][:, h // 2, :], oT[1][:, h // 2, :], b.t[:, 0:256], t, kv_used)
                b.free = [r]
                ev["swa"] = r

        for i in range(18):
            if i < 16:
                scores(i)
            if 1 <= i < 17:
                turned(i - 1)
            if i >= 2:
                values(i - 2)
            yield
        ev["swa_end"] = None

    gq = gemm_a(A["b_w_q"][0], 0, 1024, hT, ready, ev_q)
    for _ in range(2):
        next(gq)
    run_all((gq, 1), (swa(), 2))
    q.hT_free = None
    project(A["b_w_out"][0], oT, ev["swa"])
    q.hT_free = q.xw
    q.u_free = [q.xw, q.xw]
    q.m_free = [q.xw[-1]]
    BB = M[:, 13824:18432].rearrange("p (h c) -> p h c", h=12)
    t_bb = sp("bias", BB, A["toe2"].rearrange("h p c -> p h c"), t_toe2, q.m_free)
    t_lnf = sp("lnf", M[:, 0:1024], spread(A["ln_final"]), q.m_free)
    mlp(A["w_up"][1], A["w_down"][1], 24)

    st_ = S["st"]
    a = act(lambda e: e.activation(xs[:, 0, :], x[:, 0, :], ACT.Square, accum_out=st_[:, 0:1]), q.xw, q.xs_free)
    d = dve(lambda e: e.tensor_tensor_reduce(xs[:, 1, :], x[:, 1, :], x[:, 1, :], 1.0, 0.0, ALU.mult, ALU.add,
                                             st_[:, 1:2]), q.xw, q.xs_free)
    p = ts(pool, st_[:, 2:4], st_[:, 0:2], 1.0 / D, EPS, ALU.mult, ALU.add, a, d)
    p = tt(pool, st_[:, 4:6], st_[:, 2:4], S["half"][:, :], ALU.pow, p)
    for c in range(2):
        d = stt(x[:, c, :], x[:, c, :], st_[:, 4 + c:5 + c], M[:, 0:1024], ALU.mult, ALU.mult, p, t_lnf)
    q.xw = [d]
    q.m_free = [d]

    ready = norm(q.xw, [(40, hT)])
    W = A["w_in_2"][0]
    QB = M[:, 0:1536].rearrange("p (f t) -> p f t", t=T)
    KB = M[:, 1536:3072].rearrange("p (f t) -> p f t", t=T)
    VB = M[:, 3072:4608].rearrange("p (c n) -> p c n", c=2)
    QA = M[:, 9216:12288].rearrange("p (c n) -> p c n", c=2)
    ev = {}

    def ev_b(base):
        def f_(f, m, b, t):
            o = base + 2 * f
            ev[(base, f // 256)] = r = copy(act, M[:, o:o + 512], b.t[:, :], t, q.m_free)
            b.free = [r]
        return f_

    def ev_vb(f, m, c, b, t):
        r = copy(act, VB[:, c, f:f + m], b.t[:, 0:m], t, q.m_free)
        b.free = [r]
        ev["vb"] = r

    def ev_a(f, m, c, b, t):
        r = copy(act, QA[:, c, f:f + m], b.t[:, 0:m], t, q.m_free)
        b.free = [r]
        ev["qa%d" % c] = r

    run_all((gemm_a(W, 1536, 768, hT, ready, ev_b(0)), 1))
    run_all((gemm_a(W, 2304, 768, hT, ready, ev_b(1536)), 1))
    run_all((gemm_b(W, 3072, 768, hT, ready, ev_vb), 1))
    oB = (RR[:, 8192:8704].rearrange("p (k t) -> p k t", t=T), RR[:, 8704:9216].rearrange("p (k t) -> p k t", t=T))

    def dilated():
        info = {}

        def scores(h, c):
            s = M[:, 4608 + (h % 2) * 1536 + c * 768:5376 + (h % 2) * 1536 + c * 768]
            cc = S["cc"][:, 8 * (2 * (h % 2) + c):8 * (2 * (h % 2) + c) + 8]
            b0, b1 = misc_bank(), misc_bank()
            for g in range(3):
                hh = 4 * g + h
                r0 = 64 * (hh % 2)
                out = b0.t[:, g * 256:g * 256 + 256] if g < 2 else b1.t[:, 0:256]
                t = mm(out, QB[r0:r0 + 64, hh // 2, c * 128:c * 128 + 128], KB[r0:r0 + 64, hh // 2, :], True, True,
                       b0.free, b1.free, ev[(0, 2)], ev[(1536, 2)])
            c0 = 128 - 128 * c
            stt(s[:, 0:512].rearrange("p (g c) -> p g c", g=2), b0.t[:, :].rearrange("p (g c) -> p g c", g=2), 0.125,
                BB[:, h:h + 5:4, c0:c0 + 256], ALU.mult, ALU.add, t, t_bb, ring.get(("s", h % 2, c)))
            d = stt(s[:, 512:768], b1.t[:, 0:256], 0.125, BB[:, 8 + h, c0:c0 + 256], ALU.mult, ALU.add)
            b0.free = b1.free = [d]
            d = dve(lambda e: e.tensor_reduce(cc[:, 0:1], s, AX, ALU.max, negate=True), d)
            a = actf(s, s, ACT.Exp, d, bias=cc[:, 0:1], accum_out=cc[:, 1:2])
            d = dve(lambda e: e.reciprocal(cc[:, 2:3], cc[:, 1:2]), a)
            d = ts(dve, s, s, cc[:, 2:3], None, ALU.mult, None, d)
            info[(h, c)] = (s, d)

        def turned(h, c):
            s, d = info[(h, c)]
            p = M[:, 7680 + 768 * c:8448 + 768 * c]
            b0, b1 = misc_bank(), misc_bank()
            for n in range(6):
                out = b0.t[:, n * 128:n * 128 + 128] if n < 4 else b1.t[:, n * 128 - 512:n * 128 - 384]
                t = tr(out, s[:, n * 128:n * 128 + 128], b0.free, b1.free, d)
            ring[("s", h % 2, c)] = t
            copy(act, p[:, 0:512], b0.t[:, :], t, ring.get(("p", c)))
            r = copy(act, p[:, 512:768], b1.t[:, 0:256])
            b0.free = b1.free = [r]
            info[(h, c)] = (p, r)

        def values(h, c):
            p, r = info[(h, c)]
            if h % 2 == 0 and c == 0:
                info["b"] = acc_pair()
            b = info["b"][c]
            rows = slice(64 * (h % 2), 64 * (h % 2) + 64)
            for n in range(6):
                hh = 4 * (n // 2) + h
                t = mm(b.t[rows, 0:128], VB[:, n % 2, hh * 64:hh * 64 + 64], p[:, n * 128:n * 128 + 128],
                       n == 0, n == 5, b.free if h % 2 == 0 else None, r, ev["vb"])
            ring[("p", c)] = t
            if h % 2:
                sl = slice(c * 128, c * 128 + 128)
                r = split_parts(oB[0][:, h // 2, sl], oB[1][:, h // 2, sl], b.t[:, 0:128], t)
                b.free = [r]
                ev["ob"] = r

        order = [(h, c) for h in range(4) for c in range(2)]
        for i in range(10):
            if i < 8:
                scores(*order[i])
                yield
            if 1 <= i < 9:
                turned(*order[i - 1])
                yield
            if i >= 2:
                values(*order[i - 2])
                yield
        ev["b_end"] = t_last = ring[("p", 1)]

    RT = M[:, 12288:13568]
    PHASE = {}

    def rope():
        for c in range(2):
            X = QA[:, c, 0:1280]
            X3 = X.rearrange("p (h d) -> p h d", d=128)
            a = actf(RT, X, ACT.Square, ev["qa%d" % c], PHASE.get("r"))
            s = S["st"][:, 32:64]
            d = dve(lambda e: e.tensor_reduce(s[:, 0:10], RT.rearrange("p (h d) -> p h d", d=128), AX, ALU.add), a)
            p = ts(pool, s[:, 10:20], s[:, 0:10], 1.0 / 128, EPS, ALU.mult, ALU.add, d)
            p = tt(pool, s[:, 20:30], s[:, 10:20], S["half10"], ALU.pow, p)
            yield
            for h in range(10):
                g = S["qg"] if h < 8 else S["kg"]
                d = stt(X3[:, h, :], X3[:, h, :], s[:, 20 + h:21 + h], g, ALU.mult, ALU.mult, p)
            yield
            x5 = X.rearrange("p (h a b d) -> p h a b d", a=2, b=2, d=32)
            r5 = RT.rearrange("p (h a b d) -> p h a b d", a=2, b=2, d=32)
            sn = S["sin"][:, c, :].rearrange("p (a b d) -> p a b d", a=2, b=2)
            for bb in range(2):
                for aa in range(2):
                    w = sn[:, aa:aa + 1, bb, :].broadcast_to([128, 10, 32])
                    d = tt(dve, r5[:, :, aa, bb, :], x5[:, :, aa, 1 - bb, :], w, ALU.mult, d if not (aa or bb) else None)
            p = tt(pool, X3, X3, S["cos"][:, c:c + 1, :].broadcast_to([128, 10, 128]), ALU.mult, d)
            PHASE["r"] = tt(dve, X, X, RT, ALU.add, p)
            yield
        QTA = xs[:, :, :].rearrange("p c n -> p (c n)")
        KTA = M[:, 12288:12800]
        for h2 in range(5):
            b = misc_bank()
            for j in range(2):
                for c in range(2):
                    h = 2 * h2 + j
                    t = tr(b.t[:, j * 256 + c * 128:j * 256 + c * 128 + 128], QA[:, c, h * 128:h * 128 + 128], b.free,
                           PHASE["r"])
            dst = QTA[:, h2 * 512:h2 * 512 + 512] if h2 < 4 else KTA
            r = copy(dve, dst, b.t[:, :], t, q.xs_free)
            b.free = [r]
            PHASE["qt%d" % h2] = r
            yield

    ga = gemm_b(W, 0, 1536, hT, ready, ev_a)
    run_all((ga, 1), (dilated(), 2))
    b_end = ev["b_end"]
    QTA = xs[:, :, :].rearrange("p c n -> p (c n)")
    KTA = M[:, 12288:12800]
    SA = M[:, 2560:4608].rearrange("p (c n) -> p c n", c=2)
    SB = M[:, 4608:6656].rearrange("p (c n) -> p c n", c=2)
    BG = M[:, 6656:8704]
    t_bg = sp("bg", BG, spread(A["b_gate_2"]), b_end)

    def ev_gates(f, m, c, b, t):
        dst = (SA if f < 1024 else SB)[:, c, f % 1024:f % 1024 + m]
        r = tt(dve, dst, b.t[:, 0:m], BG[:, f:f + m], ALU.add, t, t_bg, b_end)
        b.free = [r]
        ev["pre"] = r

    gg = gemm_b(W, 3840, 2048, hT, ready, ev_gates)
    oA = yT
    u_free = q.u_free

    def full():
        yield from rope()
        info = {}

        def scores(h):
            b = misc_bank()
            s = M[:, 512 * (h % 3):512 * (h % 3) + 512]
            cc = S["cc"][:, 8 * (h % 3):8 * (h % 3) + 8]
            for c in range(2):
                t = mm(b.t[:, c * 256:c * 256 + 256], QTA[:, h * 256 + c * 128:h * 256 + c * 128 + 128],
                       KTA[:, (h // 4) * 256:(h // 4) * 256 + 256], True, True, b.free, PHASE["qt%d" % (h // 2)],
                       PHASE["qt4"])
            d = dve(lambda e: e.tensor_reduce(cc[:, 0:2], b.t[:, :].rearrange("p (c k) -> p c k", c=2), AX, ALU.max), t)
            d = ts(dve, cc[:, 2:4], cc[:, 0:2], -(128 ** -0.5), None, ALU.mult, None, d)
            for c in range(2):
                a = actf(s[:, c * 256:c * 256 + 256], b.t[:, c * 256:c * 256 + 256], ACT.Exp, d, b_end,
                         ring.get(("sa", h % 3)), bias=cc[:, 2 + c:3 + c], scale=128 ** -0.5, accum_out=cc[:, 4 + c:5 + c])
            b.free = [a]
            d = dve(lambda e: e.reciprocal(cc[:, 6:8], cc[:, 4:6]), a)
            for c in range(2):
                d = ts(dve, s[:, c * 256:c * 256 + 256], s[:, c * 256:c * 256 + 256], cc[:, 6 + c:7 + c], None, ALU.mult,
                       None, d if c == 0 else None)
            info[h] = (s, d)

        def turned(h):
            s, d = info[h]
            p = M[:, 1536 + 512 * (h % 2):2048 + 512 * (h % 2)]
            b = misc_bank()
            for kt in range(2):
                for c in range(2):
                    t = tr(b.t[:, kt * 256 + c * 128:kt * 256 + c * 128 + 128],
                           s[:, c * 256 + kt * 128:c * 256 + kt * 128 + 128], b.free, d)
            ring[("sa", h % 3)] = t
            r = copy(act, p, b.t[:, :], t, ring.get(("pa", h % 2)), b_end)
            b.free = [r]
            info[h] = (p, r)

        def values(h):
            p, r = info[h]
            b = misc_bank()
            for kt in range(2):
                t = mm(b.t[:, 0:256], QA[:, kt, 1280 + (h // 4) * 128:1408 + (h // 4) * 128], p[:, kt * 256:kt * 256 + 256],
                       kt == 0, kt == 1, b.free, r)
            ring[("pa", h % 2)] = t
            r = split_parts(oA[0][:, h, :], oA[1][:, h, :], b.t[:, 0:256], t, u_free)
            b.free = [r]
            ev["oa"] = r

        for i in range(10):
            if i < 8:
                scores(i)
                yield
            if 1 <= i < 9:
                turned(i - 1)
                yield
            if i >= 2:
                values(i - 2)
                yield

    u_free = [t for f in q.u_free for t in (f or [])]
    run_all((gg, 1), (full(), 2))
    q.xs_free = [ring[("pa", 1)]]
    a = actf(SA, SA, ACT.Sigmoid, ev["pre"])
    a = actf(SB, SB, ACT.Sigmoid)
    PT_ = M[:, 0:512].rearrange("p (c n) -> p c n", c=2)
    t_p = sp("p", PT_, A["p_2"][0, 0].rearrange("(c p) n -> p c n", p=128), ring[("pa", 1)])

    def ev_ya(f, m, c, b, t):
        r = tt(dve, SA[:, c, f:f + m], SA[:, c, f:f + m], b.t[:, 0:m], ALU.mult, t, a)
        b.free = [r]

    def ev_yb(f, m, c, b, t):
        s = SB[:, c, f:f + m]
        r = tt(dve, s, s, b.t[:, 0:m], ALU.mult, t, a)
        b.free = [r]
        ev["m"] = tt(dve, s, s, SA[:, c, f:f + m], ALU.add, r)

    run_all((gemm_b(A["w_out_a_2"][0], 0, D, oA, ev["oa"], ev_ya), 1))
    run_all((gemm_b(A["w_out_b_2"][0], 0, D, oB, ev["ob"], ev_yb), 1))
    last, tp = turn_parts(SB, 1024, hT[0], hT[1], ev["m"], None)
    project(A["w_out_2"][0], hT, last)
    q.hT_free = q.xw
    q.u_free = [[tp], [tp]]
    q.m_free = [tp]
    pT = oB
    b = misc_bank()
    for j in range(2):
        for c in range(2):
            t = tr(b.t[:, j * 256 + c * 128:j * 256 + c * 128 + 128], PT_[:, c, j * 128:j * 128 + 128], b.free, t_p)
    t_pT = split_parts(pT[0].rearrange("p k t -> p (k t)"), pT[1].rearrange("p k t -> p (k t)"), b.t[:, :], t, tp)
    b.free = [t_pT]
    t_fin = sp("fin", M[:, 0:1024], spread(A["final_norm_g_2"]), t)
    mlp(A["w_ff1_2"][0], A["w_ff2_2"][0], 48)

    PW = M[:, 4096:6144].rearrange("p (c n) -> p c n", c=2)
    SG = M[:, 6144:8192].rearrange("p (c n) -> p c n", c=2)
    q.xn = []

    def ev_pw(f, m, c, b, t):
        r = copy(dve, PW[:, c, f:f + m], b.t[:, 0:m], t)
        b.free = [r]

    def ev_pg(f, m, c, b, t):
        s = SG[:, c, f:f + m]
        a = actf(s, b.t[:, 0:m], ACT.Sigmoid, t)
        b.free = [a]
        d = tt(dve, s, s, PW[:, c, f:f + m], ALU.mult, a, ev["pw"])
        q.xn.append(tt(dve, x[:, c, f:f + m], x[:, c, f:f + m], s, ALU.add, d))

    ready = norm(q.xw, [(56, hT)])
    run_all((gemm_b(A["w_ple_2"][0], 0, D, pT, t_pT, ev_pw), 1))
    ev["pw"] = acc[0].free + acc[1].free + acc[2].free + acc[3].free
    run_all((gemm_b(A["w_ple_gate_2"][0], 0, D, hT, ready, ev_pg), 1))

    w = q.xn
    a = act(lambda e: e.activation(xs[:, 0, :], x[:, 0, :], ACT.Square, accum_out=st_[:, 0:1]), w, q.xs_free)
    d = dve(lambda e: e.tensor_tensor_reduce(xs[:, 1, :], x[:, 1, :], x[:, 1, :], 1.0, 0.0, ALU.mult, ALU.add,
                                             st_[:, 1:2]), w, q.xs_free)
    p = ts(pool, st_[:, 2:4], st_[:, 0:2], 1.0 / D, EPS, ALU.mult, ALU.add, a, d)
    p = tt(pool, st_[:, 4:6], st_[:, 2:4], S["half"][:, :], ALU.pow, p)
    for c in range(2):
        d = stt(x[:, c, :], x[:, c, :], st_[:, 4 + c:5 + c], M[:, 0:1024], ALU.mult, ALU.mult, p, t_fin)
        sp("out", A["out"][0, c * 128:c * 128 + 128, :], x[:, c, :], d)


def build(nc, A):
    with ExitStack() as ctx:
        def sb(name, shape, dt=F32):
            return ctx.enter_context(nc.sbuf_tensor(name, shape, dt))

        def sem(name):
            return ctx.enter_context(nc.semaphore(name))

        A = dict(A)
        A["scr1"] = nc.dram_tensor("scr1", (16, 383), F32, kind="Internal").ap()
        A["scr2"] = nc.dram_tensor("scr2", (12, 511), F32, kind="Internal").ap()
        A["toe1"] = nc.dram_tensor("toe1", (16, 128, 256), F32, kind="Internal").ap()
        A["toe2"] = nc.dram_tensor("toe2", (12, 128, 384), F32, kind="Internal").ap()
        raw = sb("raw", [128, NR, SLOT])
        hi = sb("whi", [128, NS, SLOT], F32R)
        lo = sb("wlo", [128, NS, SLOT], F32R)
        S = {
            "M": sb("M", [128, 18432]), "RR": sb("RR", [128, 9216], F32R), "x": sb("x", [128, 2, D]),
            "xs": sb("xs", [128, 2, D]), "ident": sb("ident", [128, 128]), "cos": sb("cos", [128, 2, 128]),
            "sin": sb("sin", [128, 2, 128]), "scan": sb("scan", [128, 256]), "mask": sb("mask", [128, 128], I32),
            "G": sb("G", [128, 68]), "tab": sb("tab", [33, 28]), "gk2": sb("gk2", [16, 512]),
            "st": sb("st", [128, 64]), "cc": sb("cc", [128, 64]), "ebl": sb("ebl", [128, 16]),
            "half_": sb("half_", [128, 10]), "bcs": sb("bcs", [128, 528]), "sq": sb("sq", [128, 256]),
        }
        bcs = S["bcs"]
        S["onorm"], S["qg"], S["kg"], S["sink"] = bcs[:, 0:256], bcs[:, 256:384], bcs[:, 384:512], bcs[:, 512:528]
        S["half"] = S["half_"][:, 0:2]
        S["half8"] = S["half_"][:, 0:8]
        S["half10"] = S["half_"][:, 0:10]
        S["sel"] = S["M"][0:33, 12288:14204]
        banks = [ctx.enter_context(nc.psum_tensor("ps%d" % i, [128, 512], F32)) for i in range(8)]

        sems = [sem("s_pe"), sem("s_dve"), sem("s_act"), sem("s_pool")]
        made = {}

        def dma_sem(name):
            if name not in made:
                made[name] = sem(name)
            return made[name]

        plan = None
        for _ in range(2):
            q = Queues(sems, dma_sem)
            st = Stream(plan, q, raw, hi, lo)
            write_program(q, S, st, A, [Bank(b) for b in banks])
            plan = st.seen
        for engine in (q.pe, q.dve, q.act, q.pool):
            engine.number()
        ends = [(s, n) for s, n in q.sp.sems.values()]

        block = ctx.enter_context(nc.Block())

        @block.sync
        def _(e):
            q.sp.write(e)
            for s, n in ends:
                e.wait_ge(s, n)

        @block.tensor
        def _(e):
            q.pe.write(e)

        @block.vector
        def _(e):
            q.dve.write(e)

        @block.scalar
        def _(e):
            q.act.write(e)

        @block.gpsimd
        def _(e):
            q.pool.write(e)


def constants():
    c = {"c_ident": np.eye(128, dtype=np.float32)}
    j, i = np.arange(128)[:, None], np.arange(128)[None, :]
    c["c_mask"] = ((j <= i) & (j // 64 == i // 64)).astype(np.int32)
    sel = np.zeros((33, 383 + 3 * 511), np.float32)
    d = 255 - np.arange(383)
    n = np.maximum(d, 0)
    large = 16 + (np.log(np.maximum(n, 1) / 16) / np.log(128 / 16) * 16).astype(np.int32)
    bucket = np.where(n < 16, n, np.minimum(large, 31))
    valid = (d >= 0) & (d < 128)
    for m in range(383):
        sel[bucket[m] if valid[m] else 32, m] = 1.0
    for g, (window, dil) in enumerate(((128, 1), (512, 4), (2048, 16))):
        rel = np.arange(511) - 255
        n = np.abs(rel)
        large = 8 + (np.log(np.maximum(n, 1) / 8) / np.log(1024 / 8) * 8).astype(np.int32)
        bucket = (rel > 0) * 16 + np.where(n < 8, n, np.minimum(large, 15))
        valid = (rel % dil == 0) & (n <= window // 2)
        for m in range(511):
            sel[bucket[m] if valid[m] else 32, 383 + 511 * g + m] = 1.0
    c["c_sel"] = sel
    f = np.power(np.float32(10000.0), -np.arange(0, 64, 2, dtype=np.float32) / np.float32(64))
    t = np.arange(256)
    ang = [(p.astype(np.float32)[:, None] * f[None, :]).astype(np.float32) for p in (t // 64, t % 64)]
    cos, sin = [np.cos(a) for a in ang], [np.sin(a) for a in ang]
    c["c_cos"] = np.concatenate([cos[0], cos[0], cos[1], cos[1]], 1).astype(np.float32)
    c["c_sin"] = np.concatenate([-sin[0], sin[0], -sin[1], sin[1]], 1).astype(np.float32)
    return c


INS = ["x", "a_w_in", "a_w_gk2", "a_b_gk", "a_onorm", "a_w_out", "kv_norm", "w_kv", "b_w_q", "b_sinks", "b_w_out",
       "rel_table", "ln_mix", "ln_mlp", "w_up", "w_down", "ln_final", "p_2", "norm_mix_g_2", "w_in_2", "b_gate_2",
       "q_norm_g_2", "k_norm_g_2", "rel_bias_2", "w_out_a_2", "w_out_b_2", "w_out_2", "norm_mlp_g_2", "w_ff1_2",
       "w_ff2_2", "norm_ple_g_2", "w_ple_gate_2", "w_ple_2", "final_norm_g_2"]


def kernel(**inputs):
    import concourse.bacc as bacc
    from concourse.bass_utils import run_bass_kernel_spmd as run

    nc = bacc.Bacc("TRN2", target_bir_lowering=False, num_devices=1)
    arrays, A = {}, {}
    for name in INS:
        arrays["in_" + name] = np.ascontiguousarray(inputs[name])
    for name, a in constants().items():
        arrays["in_" + name] = a
    for name, a in arrays.items():
        A[name[3:]] = nc.dram_tensor(name, a.shape, mybir.dt.from_np(a.dtype), kind="ExternalInput").ap()
    A["out"] = nc.dram_tensor("out_0", (1, T, D), F32, kind="ExternalOutput").ap()
    build(nc, A)
    r = run(nc, [arrays], core_ids=[0])
    return r.results[0]["out_0"]
```

```python
from contextlib import ExitStack

import concourse.bass as bass
from concourse import mybir
import numpy as np

ALU = mybir.AluOpType
ACT = mybir.ActivationFunctionType
F32 = mybir.dt.float32
F32R = mybir.dt.float32r
I32 = mybir.dt.int32
AX = mybir.AxisListType.X

T, D, FF = 256, 1024, 4096
EPS = 1e-6
NR = 3
NS = 3
SLOT = 2048
PROJ = 3088


class Tok:

    def __init__(self, sem=None, val=None):
        self.sem, self.val, self.used, self.step = sem, val, False, 1


class Queue:

    def __init__(self, sem):
        self.sem, self.items = sem, []

    def __call__(self, fn, *waits):
        for w in waits:
            for t in (w if isinstance(w, (list, tuple)) else (w,)):
                if t is not None:
                    t.used = True
                    self.items.append((None, t))
        tok = Tok(self.sem)
        self.items.append((fn, tok))
        return tok

    def number(self):
        n = 0
        for fn, t in self.items:
            if fn is not None and t.used and t.val is None:
                n += 1
                t.val = n

    def write(self, eng):
        met = {}
        for fn, t in self.items:
            if fn is None:
                if met.get(id(t.sem), 0) < t.val:
                    eng.wait_ge(t.sem, t.val)
                    met[id(t.sem)] = t.val
            else:
                ins = fn(eng)
                if t.used or t.step == 16:
                    ins.then_inc(t.sem, t.step)


class Dma:

    def __init__(self, new_sem):
        self.new_sem, self.items, self.sems = new_sem, [], {}

    def __call__(self, name, out, in_, *waits):
        sem, n = self.sems.get(name) or (self.new_sem("d_" + name), 0)
        self.sems[name] = (sem, n + 16)
        for w in waits:
            for t in (w if isinstance(w, (list, tuple)) else (w,)):
                if t is not None:
                    t.used = True
                    self.items.append((None, t))
        tok = Tok(sem, n + 16)
        self.items.append(((out, in_), tok))
        return tok

    def on(self, queue, name, out, in_):
        sem, n = self.sems.get(name) or (self.new_sem("d_" + name), 0)
        self.sems[name] = (sem, n + 16)
        tok = Tok(sem, n + 16)
        tok.step = 16
        queue.items.append((lambda e: e.dma_start(out, in_), tok))
        return tok

    def write(self, eng):
        met = {}
        for what, t in self.items:
            if what is None:
                if met.get(id(t.sem), 0) < t.val:
                    eng.wait_ge(t.sem, t.val)
                    met[id(t.sem)] = t.val
            else:
                eng.dma_start(*what).then_inc(t.sem, 16)


class Bank:
    def __init__(self, all_banks, n):
        self.n, self.t, self.free = n, all_banks[:, n, :], None


class Stream:

    def __init__(self, plan, q, raw, hi, lo):
        self.plan, self.q, self.raw, self.hi, self.lo = plan, q, raw, hi, lo
        self.seen, self.i = [], 0
        self.loaded, self.his, self.split, self.used = [], [], [], []

    def _load(self, j):
        srcs = self.plan[j]
        s = j % NR
        at, toks = 0, []
        free = self.split[j - NR] if j >= NR else None
        for src, kt, n in srcs:
            dst = self.raw[:, s, at:at + kt * n].rearrange("p (k n) -> p k n", k=kt)
            toks.append(self.q.sp("w%d" % s, dst, src.rearrange("(k p) n -> p k n", p=128), free))
            at += kt * n
        self.loaded.append((toks[-1], at))

    def _hi(self, j):
        tok, n = self.loaded[j]
        r, h = self.raw[:, j % NR, 0:n], self.hi[:, j % NS, 0:n]
        self.his.append(self.q.act(lambda e: e.activation(h, r, ACT.Copy), tok, self.used[j - NS] if j >= NS else None))

    def _lo(self, j):
        n = self.loaded[j][1]
        r, h, l = self.raw[:, j % NR, 0:n], self.hi[:, j % NS, 0:n], self.lo[:, j % NS, 0:n]
        m = n // 2
        self.q.dve(lambda e: e.tensor_tensor(l[:, 0:m], r[:, 0:m], h[:, 0:m].bitcast(F32), ALU.subtract),
                   self.his[j], self.used[j - NS] if j >= NS else None)
        self.split.append(self.q.dve(lambda e: e.tensor_tensor(l[:, m:n], r[:, m:n], h[:, m:n].bitcast(F32),
                                                               ALU.subtract)))

    def next(self, srcs):
        self.seen.append(srcs)
        i = self.i
        self.i += 1
        assert len(self.used) == i, "a block is taken before the last is given back"
        if self.plan is None:
            n = sum(k * c for _, k, c in srcs)
            return self.hi[:, 0, 0:n], self.lo[:, 0, 0:n], None
        last = len(self.plan)
        self._ahead(min(i + 3, last), min(i + 2, last))
        n = self.loaded[i][1]
        return self.hi[:, i % NS, 0:n], self.lo[:, i % NS, 0:n], self.split[i]

    def _ahead(self, his, los):
        last = len(self.plan)
        while len(self.loaded) < min(len(self.split) + NR, last):
            self._load(len(self.loaded))
        while len(self.split) < los or len(self.his) < his:
            if len(self.his) < his and len(self.his) < len(self.loaded):
                self._hi(len(self.his))
            if len(self.split) < los:
                self._lo(len(self.split))
            while len(self.loaded) < min(len(self.split) + NR, last):
                self._load(len(self.loaded))

    def start(self):
        while self.plan is not None and len(self.loaded) < NR:
            self._load(len(self.loaded))

    def first(self):
        if self.plan is not None:
            self._ahead(1, 1)

    def done(self, tok):
        self.used.append(tok)


class Queues:
    def __init__(self, sems, dma_sem):
        self.pe, self.dve, self.act, self.pool = (Queue(s) for s in sems)
        self.sp = Dma(dma_sem)


def run_all(*gens):
    gens = [(g, n) for g, n in gens]
    while gens:
        for it in list(gens):
            g, n = it
            for _ in range(n):
                try:
                    next(g)
                except StopIteration:
                    gens.remove(it)
                    break


def write_program(q, S, st, A, banks, PS):
    pe, dve, act, pool, sp = q.pe, q.dve, q.act, q.pool, q.sp
    M, RR, xs, x = S["M"], S["RR"], S["xs"], S["x"]
    hT = (RR[:, 0:2048].rearrange("p (k t) -> p k t", t=T), RR[:, 2048:4096].rearrange("p (k t) -> p k t", t=T))
    acc, misc = banks[0:4], banks[4:8]
    turn = {"misc": 0, "acc": 0}

    def misc_bank():
        turn["misc"] += 1
        return misc[(turn["misc"] - 1) % 4]

    def misc_pair():
        turn["misc"] += turn["misc"] % 2
        return misc_bank(), misc_bank()

    def acc_pair():
        turn["acc"] += 1
        n = (turn["acc"] - 1) % 2
        return [acc[2 * n], acc[2 * n + 1]]

    def mm(out, lhsT, rhs, start, stop, *w):
        return pe(lambda e: e.matmul(out, lhsT, rhs, start=start, stop=stop, skip_group_check=True), *w)

    def tr(out, in_, *w):
        n = in_.shape[0]
        return pe(lambda e: e.transpose(out, in_, S["ident"][0:n, 0:n]), *w)

    def copy(eng, out, in_, *w):
        if eng is act:
            return act(lambda e: e.activation(out, in_, ACT.Copy), *w)
        return eng(lambda e: e.tensor_copy(out, in_), *w)

    def tt(eng, out, a, b, op, *w):
        return eng(lambda e: e.tensor_tensor(out, a, b, op), *w)

    def ts(eng, out, a, s1, s2, op0, op1, *w):
        if s2 is None:
            return eng(lambda e: e.tensor_scalar(out, a, s1, None, op0), *w)
        return eng(lambda e: e.tensor_scalar(out, a, s1, s2, op0, op1), *w)

    def stt(out, a, s, b, op0, op1, *w):
        return dve(lambda e: e.scalar_tensor_tensor(out=out, in0=a, scalar=s, in1=b, op0=op0, op1=op1), *w)

    def actf(out, in_, f, *w, **k):
        return act(lambda e: e.activation(out, in_, f, **k), *w)

    def prod(out, sh, sl, mh, ml, first, last, *w):
        mm(out, sh, mh, first, False, *w)
        mm(out, sh, ml, False, False)
        return mm(out, sl, mh, False, last)

    t_id = sp("id", S["ident"][:, :], A["c_ident"])
    C = {}

    def gains(at, where, names):
        n = 0
        for name, rows in names:
            a = A[name]
            a = a.rearrange("a (k p) -> (a k) p", p=128) if len(a.shape) == 2 else a.rearrange("(k p) -> k p", p=128)
            t_g = sp("g%d" % at, M[n:n + rows, where:where + 128], a)
            n += rows

        def turn():
            b = misc_bank()
            t = tr(b.t[:, 0:n], M[0:n, where:where + 128], t_id, t_g, b.free)
            C["G"] = copy(dve, S["G"][:, at:at + n], b.t[:, 0:n], t)
            b.free = [C["G"]]
        return turn

    turn_first = gains(0, 0, [("ln_mix", 16)])
    xd = A["x"].rearrange("a (c p) d -> p (a c) d", p=128)
    q.xp = {}
    for n in range(2):
        t = sp("x%d" % n, x[:, :, n * 512:n * 512 + 512], xd[:, :, n * 512:n * 512 + 512])
        q.xp[(0, n)] = q.xp[(1, n)] = t
    st.start()

    def spread(a):
        n = a.shape[-1]
        return bass.AP(tensor=a.tensor, offset=a.offset, ap=[[0, 128], [1, n]])

    t_ms = pool(lambda e: e.memset(S["tab"][32:33, :], -1e30))
    t_hm = pool(lambda e: e.memset(S["half_"][:, :], -0.5), t_ms)
    t_ones = pool(lambda e: e.memset(S["ones"][:, :], 1.0), t_hm)
    t_one = pool(lambda e: e.memset(S["scan"][:, :], 1.0), t_ones)
    t_one = pool(lambda e: e.memset(S["scan"][:, :].rearrange("p (c t) -> p c t", t=64)[:, :, 0:1], 0.0), t_one)
    AT = M[:, 17408:18432]
    t_at0 = pool(lambda e: e.memset(AT, 0.0), t_one)

    turn_first()
    G = S["G"]

    def turn_rest():
        C["rest"]()
        C["G"] = tt(dve, G[:, 76:84], G[:, 40:48], G[:, 68:76], ALU.mult, C["G"])

    def small_loads():
        C["rest"] = gains(16, 15000, [("ln_mlp", 16), ("kv_norm", 8), ("norm_mix_g_2", 8), ("norm_mlp_g_2", 8),
                                      ("norm_ple_g_2", 8), ("a_b_gk", 4), ("ln_final", 8)])
        C["gk2"] = sp("gk2", S["gk2"][:, :], A["a_w_gk2"][0])
        sp("tab", S["tab"][0:32, 0:16], A["rel_table"])
        C["tab"] = sp("tab", S["tab"][0:32, 16:28], A["rel_bias_2"])
        C["sel"] = sp("sel", S["sel"], A["c_sel"])
        C["msk"] = sp("msk", S["mask"][:, :], A["c_mask"])
        sp("bc", S["onorm"], spread(A["a_onorm"]))
        sp("bc", S["qg"], spread(A["q_norm_g_2"]))
        sp("bc", S["kg"], spread(A["k_norm_g_2"]))
        C["bc"] = sp("bc", S["sink"], spread(A["b_sinks"]))

    def bias_rows():
        b = misc_bank()
        t = mm(b.t[0:16, 0:383], S["tab"][0:33, 0:16], S["sel"][:, 0:383], True, True, b.free, C["tab"], t_ms, C["sel"])
        r = copy(dve, M[0:16, 14336:14719], b.t[0:16, 0:383], t)
        b.free = [r]
        C["scr1"] = sp("scr1", A["scr1"], M[0:16, 14336:14719], r)
        for g in range(3):
            b = misc_bank()
            t = mm(b.t[0:4, 0:511], S["tab"][0:33, 16 + 4 * g:20 + 4 * g], S["sel"][:, 383 + 511 * g:894 + 511 * g],
                   True, True, b.free)
            r = copy(dve, M[32 * g:32 * g + 4, 14848:15359], b.t[0:4, 0:511], t)
            b.free = [r]
            C["scr2"] = sp("scr2", A["scr2"][4 * g:4 * g + 4, :], M[32 * g:32 * g + 4, 14848:15359], r)
        C["toe1"] = sp("toe1", A["toe1"], bass.AP(tensor=A["scr1"].tensor, offset=127,
                                                  ap=[[383, 16], [-1, 128], [1, 256]]), C["scr1"])
        C["toe2"] = sp("toe2", A["toe2"], bass.AP(tensor=A["scr2"].tensor, offset=127,
                                                  ap=[[511, 12], [-1, 128], [1, 384]]), C["scr2"])

    def norm(gains):
        parts = []
        for k2 in range(4):
            b = misc_bank()
            for j in range(2):
                k = 2 * k2 + j
                for c in range(2):
                    t = tr(b.t[:, j * 256 + c * 128:j * 256 + c * 128 + 128], x[:, c, k * 128:k * 128 + 128],
                           b.free, q.xp[(c, k // 4)], t_id)
            h = None
            for col, (hi, lo) in gains:
                for j in range(2):
                    k = 2 * k2 + j
                    h = actf(hi[:, k, :], b.t[:, j * 256:j * 256 + 256], ACT.Copy, t, q.hT_free, C["G"],
                             scale=G[:, col + k:col + k + 1])
            for col, (hi, lo) in gains:
                for j in range(2):
                    k = 2 * k2 + j
                    last = stt(lo[:, k, :], b.t[:, j * 256:j * 256 + 256], G[:, col + k:col + k + 1],
                               hi[:, k, :].bitcast(F32), ALU.mult, ALU.subtract, h, q.hT_free)
            b.free = [last]
            parts.append(last)
        q.turned = t
        q.hT_free = None
        return parts

    def scales(at, *w):
        s = S["st"]
        a = act(lambda e: e.activation(xs[:, 0, :], x[:, 0, :], ACT.Square, accum_out=s[:, 0:1]), q.xs_free, w,
                list(q.xp.values()))
        d = dve(lambda e: e.tensor_tensor_reduce(xs[:, 1, :], x[:, 1, :], x[:, 1, :], 1.0, 0.0, ALU.mult, ALU.add,
                                                 s[:, 1:2]), q.xs_free, w, list(q.xp.values()))
        p = ts(pool, s[:, 2:4], s[:, 0:2], 1.0 / D, EPS, ALU.mult, ALU.add, a, d)
        return tt(pool, s[:, at:at + 2], s[:, 2:4], S["half"][:, :], ALU.pow, p, t_hm)

    def diagonals(at, p):
        s = S["st"]
        for c in range(2):
            d = ts(dve, S["dg"][:, c, :], S["ident"][:, :], s[:, at + c:at + c + 1], None, ALU.mult, None, p,
                   q.dg_free)
        return d

    def rows_scale(at, p, d=None):
        s = S["st"]
        d = d or diagonals(at, p)
        p8 = ts(pool, s[:, 6:8], s[:, at:at + 2], 0.125, None, ALU.mult, None, p)
        b = misc_bank()
        t = mm(b.t[:, 0:256], S["ones"][:, :], S["dg"][:, :, :].rearrange("p c t -> p (c t)"), True, True, b.free, d,
               t_ones)
        q.dg_free = t
        dve(lambda e: e.tensor_copy(S["RB"][:, 0:256], b.t[:, 0:256]), t)
        r = copy(dve, S["RB"][:, 256:512], b.t[:, 0:256], t)
        b.free = [r]
        return [r, p8]

    q.dg_free = None

    def gemm_a(w, c0, n, xT, ready, evac):
        kt = xT[0].shape[1]
        for f in range(0, n, 256):
            m = min(256, n - f)
            hi, lo, split = st.next([(w[:, c0 + f:c0 + f + m], kt, m)])
            hi = hi.rearrange("p (k n) -> p k n", k=kt)
            lo = lo.rearrange("p (k n) -> p k n", k=kt)
            b = misc_bank()
            for j in range(0, m, 128):
                mj = min(128, m - j)
                for k in range(kt):
                    t = prod(b.t[0:mj, 2 * j:2 * j + 256], hi[:, k, j:j + mj], lo[:, k, j:j + mj],
                             xT[0][:, k, :], xT[1][:, k, :], k == 0, k == kt - 1, b.free, split,
                             ready[k // 2] if isinstance(ready, list) else ready)
                if j + 128 < m:
                    yield
            st.done(t)
            evac(f, m, b, t)
            yield

    def gemm_b(w, c0, n, xT, ready, evac, width=512, pairs=None):
        kt = xT[0].shape[1]
        for f in range(0, n, width):
            m = min(width, n - f)
            per = min(kt, SLOT // m)
            bs = acc_pair() if pairs is None else acc[2 * pairs:2 * pairs + 2]
            for k0 in range(0, kt, per):
                hi, lo, split = st.next([(w[k0 * 128:(k0 + per) * 128, c0 + f:c0 + f + m], per, m)])
                hi = hi.rearrange("p (k n) -> p k n", k=per)
                lo = lo.rearrange("p (k n) -> p k n", k=per)
                for c in range(2):
                    for k in range(k0, k0 + per):
                        t = prod(bs[c].t[:, 0:m], xT[0][:, k, c * 128:c * 128 + 128],
                                 xT[1][:, k, c * 128:c * 128 + 128], hi[:, k - k0, :], lo[:, k - k0, :],
                                 k == 0, k == kt - 1, bs[c].free, split,
                                 ready[k // 2] if isinstance(ready, list) else ready)
                    if k0 + per == kt:
                        evac(f, m, c, bs[c], t)
                    if c == 0:
                        yield
                st.done(t)
                yield

    def split_parts(hi, lo, src, *w):
        h = copy(act, hi, src, *w)
        return tt(dve, lo, src, hi.bitcast(F32), ALU.subtract, h, *w)

    def turn_parts(src, n, hi, lo, w, free):
        lasts = []
        for k2 in range(0, n // 128, 2):
            b = misc_bank()
            for j in range(2):
                for c in range(2):
                    t = tr(b.t[:, j * 256 + c * 128:j * 256 + c * 128 + 128],
                           src[:, c, (k2 + j) * 128:(k2 + j) * 128 + 128], b.free, w[k2 // 4], t_id)
            last = split_parts(hi[:, k2:k2 + 2, :].rearrange("p k t -> p (k t)"),
                               lo[:, k2:k2 + 2, :].rearrange("p k t -> p (k t)"), b.t[:, :], t, free)
            b.free = [last]
            lasts.append(last)
        return lasts, t

    def add_x(f, m, c, b, t):
        r = tt(dve, x[:, c, f:f + m], x[:, c, f:f + m], b.t[:, 0:m], ALU.add, t, q.xp[(c, f // 512)])
        b.free = [r]
        q.xp[(c, f // 512)] = r

    def project(w, xT, ready):
        run_all((gemm_b(w, 0, D, xT, ready, add_x), 1))

    def mlp(up, down, gain):
        ready = norm([(gain, hT)])
        uT = [(RR[:, 4096 + 2048 * i:5120 + 2048 * i].rearrange("p (k t) -> p k t", t=T),
               RR[:, 5120 + 2048 * i:6144 + 2048 * i].rearrange("p (k t) -> p k t", t=T)) for i in range(2)]
        state = {"n": 0, "u": {}}

        def evac(f, m, b, t):
            n = state["n"]
            if n == 0 and "held" not in state:
                state["held"] = (f, m, b, t)
                state["dg"] = diagonals(4, state["rs"])
                return
            if n == 0:
                state["rb"] = rows_scale(4, state["rs"], state["dg"])
                state["n"] = 1
                fill(0, *state["held"])
                n = 1
            state["n"] += 1
            fill(n, f, m, b, t)

        def fill(n, f, m, b, t):
            i, o = (n // 2) % 2, (n % 2) * 2
            r = M[:, 1024 + 512 * (n % 4):1536 + 512 * (n % 4)]
            a = stt(r, b.t[:, :], 0.0, S["RB"][:, :], ALU.max, ALU.mult, t, q.m_free, state["rb"])
            b.free = [a]
            d = actf(r, r, ACT.Square, a)
            hi = uT[i][0][:, o:o + 2, :].rearrange("p k t -> p (k t)")
            lo = uT[i][1][:, o:o + 2, :].rearrange("p k t -> p (k t)")
            h = copy(act, hi, r, d, q.u_free[i])
            state["u"][n // 2] = tt(dve, lo, r, hi.bitcast(F32), ALU.subtract, h)

        def down_chunk(c4):
            i = c4 % 2
            for kk in range(2):
                k0 = c4 * 4 + kk * 2
                hi, lo, split = st.next([(down[k0 * 128:k0 * 128 + 256, :], 2, D)])
                hi = hi.rearrange("p (k n) -> p k n", k=2)
                lo = lo.rearrange("p (k n) -> p k n", k=2)
                for n in range(2):
                    for c in range(2):
                        for k in range(2):
                            b = acc[2 * c + n]
                            sl = slice(c * 128, c * 128 + 128)
                            t = prod(b.t[:, :], uT[i][0][:, kk * 2 + k, sl], uT[i][1][:, kk * 2 + k, sl],
                                     hi[:, k, n * 512:n * 512 + 512], lo[:, k, n * 512:n * 512 + 512],
                                     k0 + k == 0, k0 + k == 31, b.free, split, state["u"][c4])
                            state["b", c, n] = t
                st.done(t)
            q.u_free[i] = [t]
            return t

        def up_chunk(c4):
            run_all((gemm_a(up, c4 * 512, 512, hT, ready, evac), 1))

        g = gemm_a(up, 0, 512, hT, ready, evac)
        next(g)
        state["rs"] = scales(4)
        run_all((g, 1))
        for c4 in range(8):
            if c4 < 7:
                up_chunk(c4 + 1)
            t = down_chunk(c4)
        q.hT_free = [t]
        for n in range(2):
            for c in range(2):
                add_x(n * 512, 512, c, acc[2 * c + n], state["b", c, n])
        q.m_free = [q.xp[(1, 1)]]

    q.u_free = [None, None]
    q.xs_free = q.hT_free = q.m_free = None

    ready = norm([(0, hT)])
    st.first()
    pr = scales(4)
    small_loads()
    W = A["a_w_in"][0]
    qT, kT = M[:, 0:1024], M[:, 1024:2048]
    bc, e1 = M[:, 2048:3072], M[:, 3072:4096]
    qt, kt_, kd = M[:, 4096:5120], M[:, 5120:6144], M[:, 6144:7168]
    kdt = M[:, 7168:8192]
    V = M[:, 8192:10240].rearrange("p (c n) -> p c n", c=2)
    GT = M[:, 10240:12288].rearrange("p (c n) -> p c n", c=2)
    O = M[:, 12288:14336].rearrange("p (c n) -> p c n", c=2)
    ST = M[:, 14336:17408]
    glr = xs[0:16, 0, 0:256]
    ev = {"qk": []}

    def ev_glr(f, m, b, t):
        r = tt(dve, glr, b.t[0:16, 0:256], S["RB"][0:16, 0:256], ALU.mult, t, ev["rb"], pr)
        b.free = [r]
        ev["glr"] = r

    def ev_qk(f, m, b, t):
        dst = M[:, 2 * f:2 * f + 512]
        sc = 128 ** -0.5 if f < 512 else 1.0
        if f == 0:
            ev["rb"] = rows_scale(4, pr)
        r = stt(dst, b.t[:, :], sc, S["RB"][:, :], ALU.mult, ALU.mult, t, ev["rb"], C["G"])
        b.free = [r]
        ev["qk"].append(r)

    g = gemm_a(W, 0, 1024, hT, ready, ev_qk)
    for _ in range(4):
        next(g)
    run_all((gemm_a(W, 3072, 16, hT, ready, ev_glr), 1))
    turn_rest()
    bias_rows()

    def gates():
        for h2 in range(2):
            b = misc_bank()
            for j in range(2):
                h = 2 * h2 + j
                t = mm(b.t[:, j * 256:j * 256 + 256], S["gk2"][:, h * 128:h * 128 + 128], glr, True, True,
                       ev["glr"], C["gk2"], b.free)
            for j in range(2):
                h = 2 * h2 + j
                d = ts(dve, bc[:, h * 256:h * 256 + 256], b.t[:, j * 256:j * 256 + 256], G[:, 64 + h:65 + h], None,
                       ALU.add, None, t, C["G"])
            b.free = [d]
            yield
        for n in range(2):
            sp("rope", S["cos"][:, n, :], A["c_cos"][n * 128:n * 128 + 128, :], t)
            C["rope"] = sp("rope", S["sin"][:, n, :], A["c_sin"][n * 128:n * 128 + 128, :], t)
        q.xs_free = [t]
        a = stt(e1, bc, -1.0, bc, ALU.mult, ALU.max, d)
        a = actf(e1, e1, ACT.Exp, a, scale=-1.0)
        a = actf(e1, e1, ACT.Ln, a, bias=1.0)
        d = ts(dve, bc, bc, 0.0, None, ALU.min, None, d, a)
        d = tt(dve, e1, bc, e1, ALU.subtract, a, d)
        d = ts(dve, e1, e1, 1.0 / 16.0, None, ALU.mult, None, d)
        yield
        for h in range(4):
            sl = slice(h * 256, h * 256 + 256)
            d2 = dve(lambda e, sl=sl: e.tensor_tensor_scan(bc[:, sl], S["scan"][:, :], e1[:, sl], 0.0, ALU.mult,
                                                           ALU.add), d, t_one)
        yield
        a = actf(qt, bc, ACT.Exp, d2)
        a2 = actf(kt_, bc, ACT.Exp, d2, scale=-1.0)
        b3 = bc.rearrange("p (g t) -> p g t", t=64)
        d = tt(dve, kd.rearrange("p (g t) -> p g t", t=64), b3, b3[:, :, 63:64].broadcast_to([128, 16, 64]), ALU.subtract,
               d2)
        a3 = actf(kd, kd, ACT.Exp, d, scale=-1.0)
        p = copy(pool, S["ebl"][:, :], qt.rearrange("p (g t) -> p g t", t=64)[:, :, 63:64].rearrange("p g t -> p (g t)"), a)
        ev["ebl"] = p
        yield
        while len(ev["qk"]) < 4:
            yield
        ev["qt"] = tt(dve, qt, qt, qT, ALU.mult, a, p, ev["qk"])
        ev["kt"] = tt(dve, kt_, kt_, kT, ALU.mult, a2, ev["qk"])
        ev["kd"] = tt(dve, kd, kd, kT, ALU.mult, a3, ev["qk"])

    def ev_v(f, m, c, b, t):
        r = actf(V[:, c, f:f + m], b.t[:, 0:m], ACT.Copy, t, pr, scale=S["st"][:, 4 + c:5 + c])
        b.free = [r]
        ev.setdefault("v", []).append(r)

    def ev_gate(f, m, c, b, t):
        sg = xs[:, c, 0:512]
        rs = S["st"][:, 4 + c:5 + c]
        a = actf(sg, b.t[:, 0:m], ACT.Sigmoid, t, q.xs_free, ev.get("g"), scale=rs)
        r = stt(GT[:, c, f:f + m], b.t[:, 0:m], rs, sg, ALU.mult, ALU.mult, a)
        b.free = [r]
        ev["g"] = r

    def attn_gla():
        for h2 in range(2):
            b = misc_bank()
            for j in range(2):
                h = 2 * h2 + j
                for c in range(2):
                    t = tr(b.t[:, j * 256 + c * 128:j * 256 + c * 128 + 128],
                           kd[:, h * 256 + c * 128:h * 256 + c * 128 + 128], b.free, ev["kd"], t_id)
            r = copy(act, kdt[:, h2 * 512:h2 * 512 + 512], b.t[:, :], t)
            b.free = [r]
            ev["kdt"] = r
            yield
            b = misc_bank()
            for j in range(2):
                h = 2 * h2 + j
                for c in range(2):
                    sl = slice(h * 256 + c * 128, h * 256 + c * 128 + 128)
                    t = mm(b.t[:, j * 256 + c * 128:j * 256 + c * 128 + 128], kt_[:, sl], qt[:, sl], True, True,
                           b.free, ev["kt"], ev["qt"])
            msk = S["mask"][:, :]
            for n in range(4):
                r = dve(lambda e, n=n, b=b, h2=h2: e.copy_predicated(
                    AT[:, h2 * 512 + n * 128:h2 * 512 + n * 128 + 128], msk, b.t[:, n * 128:n * 128 + 128]),
                    t, t_at0, C["msk"])
            b.free = [r]
            ev["at"] = r
            yield
        prev = None
        for c in range(3):
            rows = slice(64 * (c % 2), 64 * (c % 2) + 64)
            for h2 in range(2):
                b = misc_bank()
                for j in range(2):
                    h = 2 * h2 + j
                    t = mm(b.t[:, j * 256:j * 256 + 256], kdt[rows, h * 256 + (c // 2) * 128:h * 256 + (c // 2) * 128 + 128],
                           V[rows, c // 2, h * 256:h * 256 + 256], True, True, b.free, ev["kdt"], ev["v"])
                for j in range(2):
                    h = 2 * h2 + j
                    o = c * 1024 + h * 256
                    if c == 0:
                        r = copy(dve, ST[:, o:o + 256], b.t[:, j * 256:j * 256 + 256], t, C["scr1"], C["scr2"])
                    else:
                        r = stt(ST[:, o:o + 256], ST[:, o - 1024:o - 768], S["ebl"][:, h * 4 + c:h * 4 + c + 1],
                                b.t[:, j * 256:j * 256 + 256], ALU.mult, ALU.add, t, prev, ev["ebl"])
                b.free = [r]
            prev = r
            yield
        ev["st"] = prev
        for c2 in range(2):
            for h2 in range(2):
                b = misc_bank()
                for j in range(2):
                    h = 2 * h2 + j
                    out = b.t[:, j * 256:j * 256 + 256]
                    mm(out, AT[:, h * 256 + c2 * 128:h * 256 + c2 * 128 + 128], V[:, c2, h * 256:h * 256 + 256],
                       True, False, b.free, ev["at"], ev["v"])
                    for c in (2 * c2, 2 * c2 + 1):
                        if c:
                            rows = slice(64 * (c % 2), 64 * (c % 2) + 64)
                            t = mm(b.t[rows, j * 256:j * 256 + 256], qt[:, h * 256 + c * 64:h * 256 + c * 64 + 64],
                                   ST[:, (c - 1) * 1024 + h * 256:(c - 1) * 1024 + h * 256 + 256], False, True,
                                   ev["st"])
                r = copy(act, O[:, c2, h2 * 512:h2 * 512 + 512], b.t[:, :], t)
                b.free = [r]
                for j in range(2):
                    h = 2 * h2 + j
                    n = h * 2 + c2
                    s = O[:, c2, h * 256:h * 256 + 256]
                    r2 = dve(lambda e, s=s, n=n, j=j: e.tensor_tensor_reduce(
                        S["sq"][:, 0:256], s, s, 1.0, 0.0, ALU.mult, ALU.add, S["st"][:, 8 + n:9 + n]), r, ev.get("sq"), q.dg_free)
                    ev["sq"] = r2
                yield
        p = ts(pool, S["st"][:, 16:24], S["st"][:, 8:16], 1.0 / 256, EPS, ALU.mult, ALU.add, r2)
        p = tt(pool, S["st"][:, 24:32], S["st"][:, 16:24], S["half8"], ALU.pow, p, t_hm)
        yield
        for h in range(4):
            for c in range(2):
                s = O[:, c, h * 256:h * 256 + 256]
                ev["on"] = stt(s, s, S["st"][:, 24 + h * 2 + c:25 + h * 2 + c], S["onorm"], ALU.mult, ALU.mult, p,
                               C["bc"])
        yield

    def k_and_v():
        yield from g
        yield from gemm_b(W, 1024, 1024, hT, ready, ev_v)

    run_all((k_and_v(), 1), (gates(), 1))
    run_all((gemm_b(W, 2048, 1024, hT, ready, ev_gate), 1), (attn_gla(), 2))
    for n in range(2):
        for c in range(2):
            s = O[:, c, n * 512:n * 512 + 512]
            ev["o%d" % n] = tt(dve, s, s, GT[:, c, n * 512:n * 512 + 512], ALU.mult, ev["on"], ev["g"])
    q.xs_free = [ev["g"]]
    yT = (RR[:, 4096:6144].rearrange("p (k t) -> p k t", t=T), RR[:, 6144:8192].rearrange("p (k t) -> p k t", t=T))
    last, tp = turn_parts(O, 1024, yT[0], yT[1], [ev["o0"], ev["o1"]], None)
    q.hT_free = [tp]
    q.m_free = [tp]

    project(A["a_w_out"][0], yT, last)
    q.u_free = [list(q.xp.values())] * 2

    BS = M[:, 13824:17920].rearrange("p (h c) -> p h c", h=16)
    t_bias = sp("bias", BS, A["toe1"].rearrange("h p c -> p h c"), C["toe1"], q.m_free)
    mlp(A["w_up"][0], A["w_down"][0], 16)

    kvp = (RR[:, 4096:6144].rearrange("p (k t) -> p k t", t=T), RR[:, 6144:8192].rearrange("p (k t) -> p k t", t=T))
    ready = norm([(8, hT), (32, kvp)])
    QT = M[:, 0:2048].rearrange("p (f t) -> p f t", t=T)
    KT = M[:, 2048:2560].rearrange("p (g t) -> p g t", t=T)
    V = M[:, 2560:2816].rearrange("p (c n) -> p c n", c=2)
    hi, lo, split = st.next([(A["w_kv"], 8, 256)])
    hi = hi.rearrange("p (k n) -> p k n", k=8)
    lo = lo.rearrange("p (k n) -> p k n", k=8)
    b = misc_bank()
    for k in range(8):
        t = prod(b.t[:, 0:256], hi[:, k, 0:128], lo[:, k, 0:128], kvp[0][:, k, :], kvp[1][:, k, :],
                 k == 0, k == 7, b.free, split, ready[k // 2])
    bk, tk = b, t
    ps_ = scales(4)
    b = misc_bank()
    for c in range(2):
        for k in range(8):
            t = prod(b.t[:, c * 128:c * 128 + 128], kvp[0][:, k, c * 128:c * 128 + 128],
                     kvp[1][:, k, c * 128:c * 128 + 128], hi[:, k, 128:256], lo[:, k, 128:256], k == 0, k == 7, b.free)
    st.done(t)
    for c in range(2):
        t_v = actf(V[:, c, :], b.t[:, c * 128:c * 128 + 128], ACT.Copy, t, ps_, q.m_free, scale=S["st"][:, 4 + c:5 + c])
    b.free = [t_v]
    rb = rows_scale(4, ps_)
    for g in range(2):
        for half in range(2):
            t_k = tt(dve, KT[64 * half:64 * half + 64, g, :], bk.t[64 * g:64 * g + 64, 0:256],
                     S["RB"][64 * g:64 * g + 64, 0:256], ALU.mult, tk, q.m_free, rb)
    bk.free = [t_k]
    kv_used = [t]
    qtok = {}

    def ev_q(f, m, b, t):
        r = copy(act, M[:, 2 * f:2 * f + 512], b.t[:, :], t, q.m_free)
        b.free = [r]
        qtok[f // 256] = r

    oT = (RR[:, 4096:6144].rearrange("p (k t) -> p k t", t=T), RR[:, 6144:8192].rearrange("p (k t) -> p k t", t=T))
    ring = {}

    def swa():
        info = {}

        def scores(p):
            b = acc[0:2]
            kv = p // 4
            for j in range(2):
                r0 = 64 * j
                mm(b[j].t[:, 0:128], QT[r0:r0 + 64, p, 0:128], KT[r0:r0 + 64, kv, 0:128], True, True, b[0].free,
                   b[1].free, qtok[p // 2], t_k)
                t = mm(b[j].t[:, 128:384], QT[r0:r0 + 64, p, 128:256], KT[r0:r0 + 64, kv, :], True, True)
            info[p] = (b, t)

        def soft(p):
            b, t = info[p]
            pp = PS[:, b[0].n:b[0].n + 2, :]
            s = M[:, 2816 + 768 * (p % 3):3584 + 768 * (p % 3)].rearrange("p (h k) -> p h k", h=2)
            rs = S["st"]
            stt(s[:, :, 0:128], pp[:, :, 0:128], rs[:, 6:7], BS[:, 2 * p:2 * p + 2, 128:256], ALU.mult, ALU.add, t,
                t_bias, rb, ring.get(("s", p % 3)))
            d = stt(s[:, :, 128:384], pp[:, :, 128:384], rs[:, 7:8], BS[:, 2 * p:2 * p + 2, :], ALU.mult, ALU.add)
            b[0].free = b[1].free = [d]
            c = S["cc"][:, 32 * (p % 3):32 * (p % 3) + 32]
            dve(lambda e: e.tensor_reduce(c[:, 0:2], s[:, :, 0:128], AX, ALU.max), d)
            d = dve(lambda e: e.tensor_reduce(c[:, 2:4], s[:, :, 128:384], AX, ALU.max))
            sk = S["sink"][:, 2 * p:2 * p + 2]
            c2 = c[:, 0:4].rearrange("p (b h) -> p b h", b=2)
            skb = S["sink"][:, 2 * p:2 * p + 2].rearrange("p (a h) -> p a h", a=1).broadcast_to([128, 2, 2])
            d = tt(dve, c2, c2, skb, ALU.max, d, C["bc"])
            d = ts(dve, c[:, 4:8], c[:, 0:4], -1.0, None, ALU.mult, None, d)
            k = tt(dve, c[:, 8:12].rearrange("p (b h) -> p b h", b=2), c[:, 4:8].rearrange("p (b h) -> p b h", b=2), skb,
                   ALU.add, d)
            for h in range(2):
                actf(s[:, h, 0:128], s[:, h, 0:128], ACT.Exp, d, bias=c[:, 4 + h:5 + h], accum_out=c[:, 12 + h:13 + h])
                actf(s[:, h, 128:384], s[:, h, 128:384], ACT.Exp, bias=c[:, 6 + h:7 + h],
                     accum_out=c[:, 14 + h:15 + h])
            a = actf(c[:, 16:20], c[:, 8:12], ACT.Exp, k)
            info[p] = (s, c, a)

        def turned(p):
            s, c, a = info[p]
            d = tt(dve, c[:, 20:24], c[:, 12:16], c[:, 16:20], ALU.add, a)
            d = dve(lambda e: e.reciprocal(c[:, 24:28], c[:, 20:24]), d)
            for h in range(2):
                ts(dve, s[:, h, 0:128], s[:, h, 0:128], c[:, 24 + h:25 + h], None, ALU.mult, None, d)
                d = ts(dve, s[:, h, 128:384], s[:, h, 128:384], c[:, 26 + h:27 + h], None, ALU.mult, None)
            b = misc_pair()
            for h in range(2):
                for n in range(3):
                    t = tr(b[h].t[:, n * 128:n * 128 + 128], s[:, h, n * 128:n * 128 + 128], b[0].free, b[1].free, d)
            ring[("s", p % 3)] = t
            v = M[:, 5120 + 768 * (p % 2):5888 + 768 * (p % 2)].rearrange("p (h k) -> p h k", h=2)
            r = copy(act, v, PS[:, b[0].n:b[0].n + 2, 0:384], t, ring.get(("p", p % 2)))
            b[0].free = b[1].free = [r]
            info[p] = (v, r)

        def values(p):
            v, r = info[p]
            kv = p // 4
            b = acc[2 + p % 2]
            v0, v1 = V[:, 0, 64 * kv:64 * kv + 64], V[:, 1, 64 * kv:64 * kv + 64]
            for h in range(2):
                rows = slice(64 * h, 64 * h + 64)
                mm(b.t[rows, 0:128], v0, v[:, h, 0:128], True, True, b.free, r, t_v)
                mm(b.t[rows, 128:256], v0, v[:, h, 128:256], True, False)
                t = mm(b.t[rows, 128:256], v1, v[:, h, 256:384], False, True)
            ring[("p", p % 2)] = t
            info[p] = (b, t)

        def parts(p):
            b, t = info[p]
            r = split_parts(oT[0][:, p, :], oT[1][:, p, :], b.t[:, 0:256], t, kv_used)
            b.free = [r]
            ev["swa"] = r

        scores(0)
        for i in range(11):
            if 0 <= i - 1 < 8:
                turned(i - 1)
            if i < 8:
                soft(i)
            if 0 <= i - 3 < 8:
                parts(i - 3)
            if i + 1 < 8:
                scores(i + 1)
            if 0 <= i - 2 < 8:
                values(i - 2)
            yield

    gq = gemm_a(A["b_w_q"][0], 0, 1024, hT, ready, ev_q)
    for _ in range(2):
        next(gq)
    run_all((gq, 1), (swa(), 1))
    q.hT_free = [ev["swa"]]
    project(A["b_w_out"][0], oT, ev["swa"])
    q.hT_free = [q.xp[(1, 1)]]
    q.u_free = [[q.xp[(1, 1)]]] * 2
    q.m_free = [q.xp[(1, 1)]]
    BB = M[:, 13824:18432].rearrange("p (h c) -> p h c", h=12)
    t_bb = sp("bias", BB, A["toe2"].rearrange("h p c -> p h c"), C["toe2"], q.m_free)
    t_lnf = sp("lnf", M[:, 0:1024], spread(A["ln_final"]), q.m_free)
    mlp(A["w_up"][1], A["w_down"][1], 24)

    ready = norm([(76, hT)])
    ev = {}
    QA = M[:, 9216:12288].rearrange("p (c n) -> p c n", c=2)
    products_a = gemm_b(A["w_in_2"][0], 0, 1536, hT, ready, lambda *a: ev["to"](*a))
    next(products_a)
    p = scales(32)
    st_ = S["st"]
    for c in range(2):
        for n in range(2):
            sl = slice(n * 512, n * 512 + 512)
            q.xp[(c, n)] = stt(x[:, c, sl], x[:, c, sl], st_[:, 32 + c:33 + c], M[:, n * 512:n * 512 + 512], ALU.mult,
                               ALU.mult, p, t_lnf, q.turned)
    q.m_free = [q.xp[(1, 1)]]
    pr2 = scales(34, q.xp[(1, 1)])
    pr2 = tt(pool, st_[:, 4:6], st_[:, 32:34], st_[:, 34:36], ALU.mult, pr2)
    W = A["w_in_2"][0]
    QB = M[:, 0:1536].rearrange("p (f t) -> p f t", t=T)
    KB = M[:, 1536:3072].rearrange("p (f t) -> p f t", t=T)
    VB = M[:, 3072:4608].rearrange("p (c n) -> p c n", c=2)

    def ev_b(base):
        def f_(f, m, b, t):
            o = base + 2 * f
            if base:
                r = tt(dve, M[:, o:o + 512], b.t[:, :], S["RB"][:, :], ALU.mult, t, q.m_free, rb2)
            else:
                r = copy(act, M[:, o:o + 512], b.t[:, :], t, q.m_free)
            ev[(base, f // 256)] = r
            b.free = [r]
        return f_

    def ev_vb(f, m, c, b, t):
        r = actf(VB[:, c, f:f + m], b.t[:, 0:m], ACT.Copy, t, q.m_free, pr2, scale=S["st"][:, 4 + c:5 + c])
        b.free = [r]
        ev["vb"] = r

    def ev_a(f, m, c, b, t):
        r = actf(QA[:, c, f:f + m], b.t[:, 0:m], ACT.Copy, t, q.m_free, pr2, scale=S["st"][:, 4 + c:5 + c])
        b.free = [r]
        ev["qa%d" % c] = r

    oB = (RR[:, 8192:8704].rearrange("p (k t) -> p k t", t=T), RR[:, 8704:9216].rearrange("p (k t) -> p k t", t=T))
    ev["to"] = ev_a
    run_all((products_a, 1))
    rb2 = rows_scale(4, pr2)

    def dilated():
        info = {}

        def scores(h, c):
            s = M[:, 4608 + (h % 2) * 1536 + c * 768:5376 + (h % 2) * 1536 + c * 768]
            b0, b1 = misc_pair()
            for g in range(3):
                hh = 4 * g + h
                r0 = 64 * (hh % 2)
                out = b0.t[:, g * 256:g * 256 + 256] if g < 2 else b1.t[:, 0:256]
                t = mm(out, QB[r0:r0 + 64, hh // 2, c * 128:c * 128 + 128], KB[r0:r0 + 64, hh // 2, :], True, True,
                       b0.free, b1.free, ev[(0, 2)], ev[(1536, 2)])
            info[(h, c)] = (s, b0, b1, t)

        def soft(h, c):
            s, b0, b1, t = info[(h, c)]
            cc = S["cc"][:, 8 * (2 * (h % 2) + c):8 * (2 * (h % 2) + c) + 8]
            c0 = 128 - 128 * c
            rs = S["st"][:, 6 + c:7 + c]
            stt(s[:, 0:512].rearrange("p (g c) -> p g c", g=2), b0.t[:, :].rearrange("p (g c) -> p g c", g=2), rs,
                BB[:, h:h + 5:4, c0:c0 + 256], ALU.mult, ALU.add, t, t_bb, rb2, ring.get(("s", h % 2, c)))
            d = stt(s[:, 512:768], b1.t[:, 0:256], rs, BB[:, 8 + h, c0:c0 + 256], ALU.mult, ALU.add)
            b0.free = b1.free = [d]
            d = dve(lambda e: e.tensor_reduce(cc[:, 0:1], s, AX, ALU.max, negate=True), d)
            a = actf(s, s, ACT.Exp, d, bias=cc[:, 0:1], accum_out=cc[:, 1:2])
            d = dve(lambda e: e.reciprocal(cc[:, 2:3], cc[:, 1:2]), a)
            d = ts(dve, s, s, cc[:, 2:3], None, ALU.mult, None, d)
            info[(h, c)] = (s, d)

        def turned(h, c):
            s, d = info[(h, c)]
            p = M[:, 7680 + 768 * c:8448 + 768 * c]
            b0, b1 = misc_pair()
            for n in range(6):
                out = b0.t[:, n * 128:n * 128 + 128] if n < 4 else b1.t[:, n * 128 - 512:n * 128 - 384]
                t = tr(out, s[:, n * 128:n * 128 + 128], b0.free, b1.free, d)
            ring[("s", h % 2, c)] = t
            copy(act, p[:, 0:512], b0.t[:, :], t, ring.get(("p", c)))
            r = copy(act, p[:, 512:768], b1.t[:, 0:256])
            b0.free = b1.free = [r]
            info[(h, c)] = (p, r)

        def values(h, c):
            p, r = info[(h, c)]
            b = acc[2 + h // 2]
            rows = slice(64 * (h % 2), 64 * (h % 2) + 64)
            for n in range(6):
                hh = 4 * (n // 2) + h
                t = mm(b.t[rows, c * 128:c * 128 + 128], VB[:, n % 2, hh * 64:hh * 64 + 64],
                       p[:, n * 128:n * 128 + 128], n == 0, n == 5, b.free, r, ev["vb"])
            ring[("p", c)] = t
            info[(h, c)] = (b, t)

        def parts(h, c):
            b, t = info[(h, c)]
            if h % 2 and c:
                r = split_parts(oB[0][:, h // 2, :], oB[1][:, h // 2, :], b.t[:, 0:256], t)
                b.free = [r]
                ev["ob"] = r

        order = [(h, c) for h in range(4) for c in range(2)]
        scores(*order[0])
        for i in range(11):
            if 0 <= i - 1 < 8:
                turned(*order[i - 1])
            if i < 8:
                soft(*order[i])
            yield
            if 0 <= i - 3 < 8:
                parts(*order[i - 3])
            if i + 1 < 8:
                scores(*order[i + 1])
            if 0 <= i - 2 < 8:
                values(*order[i - 2])
            yield
        ev["b_end"] = t_last = ring[("p", 1)]

    RT = M[:, 12288:13568]
    PHASE = {}

    def rope():
        for c in range(2):
            X = QA[:, c, 0:1280]
            X3 = X.rearrange("p (h d) -> p h d", d=128)
            a = actf(RT, X, ACT.Square, ev["qa%d" % c], PHASE.get("r"))
            s = S["st"][:, 32:64]
            d = dve(lambda e: e.tensor_reduce(s[:, 0:10], RT.rearrange("p (h d) -> p h d", d=128), AX, ALU.add), a)
            p = ts(pool, s[:, 10:20], s[:, 0:10], 1.0 / 128, EPS, ALU.mult, ALU.add, d)
            p = tt(pool, s[:, 20:30], s[:, 10:20], S["half10"], ALU.pow, p)
            yield
            for h in range(10):
                g = S["qg"] if h < 8 else S["kg"]
                d = stt(X3[:, h, :], X3[:, h, :], s[:, 20 + h:21 + h], g, ALU.mult, ALU.mult, p)
            yield
            x5 = X.rearrange("p (h a b d) -> p h a b d", a=2, b=2, d=32)
            r5 = RT.rearrange("p (h a b d) -> p h a b d", a=2, b=2, d=32)
            sn = S["sin"][:, c, :].rearrange("p (a b d) -> p a b d", a=2, b=2)
            for bb in range(2):
                for aa in range(2):
                    w = sn[:, aa:aa + 1, bb, :].broadcast_to([128, 10, 32])
                    d = tt(dve, r5[:, :, aa, bb, :], x5[:, :, aa, 1 - bb, :], w, ALU.mult, d if not (aa or bb) else None, C["rope"])
            p = tt(pool, X3, X3, S["cos"][:, c:c + 1, :].broadcast_to([128, 10, 128]), ALU.mult, d)
            PHASE["r"] = tt(dve, X, X, RT, ALU.add, p)
            yield
        QTA = xs[:, :, :].rearrange("p c n -> p (c n)")
        KTA = M[:, 12288:12800]
        for h2 in range(5):
            b = misc_bank()
            for j in range(2):
                for c in range(2):
                    h = 2 * h2 + j
                    t = tr(b.t[:, j * 256 + c * 128:j * 256 + c * 128 + 128], QA[:, c, h * 128:h * 128 + 128], b.free,
                           PHASE["r"])
            dst = QTA[:, h2 * 512:h2 * 512 + 512] if h2 < 4 else KTA
            r = copy(dve, dst, b.t[:, :], t, pr2)
            b.free = [r]
            PHASE["qt%d" % h2] = r
            yield

    def products_b():
        yield from gemm_a(W, 1536, 768, hT, ready, ev_b(0))
        yield from gemm_a(W, 2304, 768, hT, ready, ev_b(1536))
        yield from gemm_b(W, 3072, 768, hT, ready, ev_vb)

    QTA = xs[:, :, :].rearrange("p c n -> p (c n)")
    KTA = M[:, 12288:12800]
    run_all((products_b(), 2), (rope(), 1))
    SA = QA[:, :, 0:1024]
    SB = M[:, 4608:6656].rearrange("p (c n) -> p c n", c=2)
    BG, BG2 = M[:, 12800:13824], M[:, 6656:7680]
    t_bg = sp("bg", BG, spread(A["b_gate_2"][:, 0:1024]), PHASE["qt4"])

    def ev_ga(f, m, c, b, t):
        r = stt(SA[:, c, f:f + m], b.t[:, 0:m], S["st"][:, 4 + c:5 + c], BG[:, f:f + m], ALU.mult, ALU.add, t, t_bg,
                PHASE["qt4"], pr2)
        b.free = [r]
        ev["prea"] = r

    def ev_gb(f, m, c, b, t):
        r = stt(SB[:, c, f:f + m], b.t[:, 0:m], S["st"][:, 4 + c:5 + c], BG2[:, f:f + m], ALU.mult, ALU.add, t, t_bg2,
                b_end, pr2)
        b.free = [r]
        ev["preb"] = r

    gg = gemm_b(W, 3840, 1024, hT, ready, ev_ga, pairs=0)
    mix = dilated()
    next(mix)
    run_all((gg, 1), (mix, 2))
    b_end = ev["b_end"]
    t_bg2 = sp("bg", BG2, spread(A["b_gate_2"][:, 1024:2048]), b_end)
    gg = gemm_b(W, 4864, 1024, hT, ready, ev_gb)
    oA = yT
    u_free = q.u_free

    def full():
        info = {}

        def scores(h):
            b = misc_bank()
            for c in range(2):
                t = mm(b.t[:, c * 256:c * 256 + 256], QTA[:, h * 256 + c * 128:h * 256 + c * 128 + 128],
                       KTA[:, (h // 4) * 256:(h // 4) * 256 + 256], True, True, b.free, PHASE["qt%d" % (h // 2)],
                       PHASE["qt4"])
            info[h] = (b, t)

        def soft(h):
            b, t = info[h]
            s = M[:, 512 * (h % 3):512 * (h % 3) + 512]
            cc = S["cc"][:, 8 * (h % 3):8 * (h % 3) + 8]
            d = dve(lambda e: e.tensor_reduce(cc[:, 0:2], b.t[:, :].rearrange("p (c k) -> p c k", c=2), AX, ALU.max), t)
            d = ts(dve, cc[:, 2:4], cc[:, 0:2], -(128 ** -0.5), None, ALU.mult, None, d)
            for c in range(2):
                a = actf(s[:, c * 256:c * 256 + 256], b.t[:, c * 256:c * 256 + 256], ACT.Exp, d, b_end,
                         ring.get(("sa", h % 3)), bias=cc[:, 2 + c:3 + c], scale=128 ** -0.5, accum_out=cc[:, 4 + c:5 + c])
            b.free = [a]
            d = dve(lambda e: e.reciprocal(cc[:, 6:8], cc[:, 4:6]), a)
            for c in range(2):
                d = ts(dve, s[:, c * 256:c * 256 + 256], s[:, c * 256:c * 256 + 256], cc[:, 6 + c:7 + c], None, ALU.mult,
                       None, d if c == 0 else None)
            info[h] = (s, d)

        def turned(h):
            s, d = info[h]
            p = M[:, 1536 + 512 * (h % 2):2048 + 512 * (h % 2)]
            b = misc_bank()
            for kt in range(2):
                for c in range(2):
                    t = tr(b.t[:, kt * 256 + c * 128:kt * 256 + c * 128 + 128],
                           s[:, c * 256 + kt * 128:c * 256 + kt * 128 + 128], b.free, d)
            ring[("sa", h % 3)] = t
            r = copy(act, p, b.t[:, :], t, ring.get(("pa", h % 2)), b_end)
            b.free = [r]
            info[h] = (p, r)

        def values(h):
            p, r = info[h]
            b = misc_bank()
            for kt in range(2):
                t = mm(b.t[:, 0:256], QA[:, kt, 1280 + (h // 4) * 128:1408 + (h // 4) * 128], p[:, kt * 256:kt * 256 + 256],
                       kt == 0, kt == 1, b.free, r)
            ring[("pa", h % 2)] = t
            info[h] = (b, t)

        def parts(h):
            b, t = info[h]
            r = split_parts(oA[0][:, h, :], oA[1][:, h, :], b.t[:, 0:256], t, u_free)
            b.free = [r]
            ev["oa"] = r

        scores(0)
        for i in range(11):
            if 0 <= i - 1 < 8:
                turned(i - 1)
            if i < 8:
                soft(i)
            yield
            if 0 <= i - 3 < 8:
                parts(i - 3)
            if i + 1 < 8:
                scores(i + 1)
            if 0 <= i - 2 < 8:
                values(i - 2)
            yield

    u_free = [t for f in q.u_free for t in (f or [])]
    mix = full()
    next(mix)
    run_all((gg, 1), (mix, 2))
    q.xs_free = [ring[("pa", 1)]]
    for c in range(2):
        a = actf(SA[:, c, :], SA[:, c, :], ACT.Sigmoid, ev["prea"])
    a = actf(SB, SB, ACT.Sigmoid, ev["preb"])
    PT_ = M[:, 0:512].rearrange("p (c n) -> p c n", c=2)
    t_p = sp("p", PT_, A["p_2"][0, 0].rearrange("(c p) n -> p c n", p=128), ring[("pa", 1)])

    def ev_ya(f, m, c, b, t):
        r = tt(dve, SA[:, c, f:f + m], SA[:, c, f:f + m], b.t[:, 0:m], ALU.mult, t, a)
        b.free = [r]

    def ev_yb(f, m, c, b, t):
        s = SB[:, c, f:f + m]
        r = tt(dve, s, s, b.t[:, 0:m], ALU.mult, t, a)
        b.free = [r]
        ev["m", f // 512] = tt(dve, s, s, SA[:, c, f:f + m], ALU.add, r)

    run_all((gemm_b(A["w_out_a_2"][0], 0, D, oA, ev["oa"], ev_ya), 1))
    run_all((gemm_b(A["w_out_b_2"][0], 0, D, oB, ev["ob"], ev_yb), 1))
    last, tp = turn_parts(SB, 1024, hT[0], hT[1], [ev["m", 0], ev["m", 1]], None)
    project(A["w_out_2"][0], hT, last)
    q.hT_free = [q.xp[(1, 1)]]
    q.u_free = [[tp], [tp]]
    q.m_free = [tp]
    pT = oB
    b = misc_bank()
    for j in range(2):
        for c in range(2):
            t = tr(b.t[:, j * 256 + c * 128:j * 256 + c * 128 + 128], PT_[:, c, j * 128:j * 128 + 128], b.free, t_p)
    t_pT = split_parts(pT[0].rearrange("p k t -> p (k t)"), pT[1].rearrange("p k t -> p (k t)"), b.t[:, :], t, tp)
    b.free = [t_pT]
    t_fin = sp("fin", M[:, 0:1024], spread(A["final_norm_g_2"]), t)
    mlp(A["w_ff1_2"][0], A["w_ff2_2"][0], 48)

    PW = M[:, 4096:6144].rearrange("p (c n) -> p c n", c=2)
    SG = M[:, 6144:8192].rearrange("p (c n) -> p c n", c=2)
    ev["pw"] = []

    def ev_pw(f, m, c, b, t):
        r = copy(act, PW[:, c, f:f + m], b.t[:, 0:m], t)
        b.free = [r]
        ev["pw"].append(r)

    def ev_pg(f, m, c, b, t):
        s, xc, n = SG[:, c, f:f + m], x[:, c, f:f + m], f // 512
        a = actf(s, b.t[:, 0:m], ACT.Sigmoid, t, pr3, scale=S["st"][:, 4 + c:5 + c])
        b.free = [a]
        d = tt(dve, s, s, PW[:, c, f:f + m], ALU.mult, a, ev["pw"])
        d = tt(dve, xc, xc, s, ALU.add, d, q.turned)
        ev["sq", c, n] = actf(s, xc, ACT.Square, d, accum_out=S["st"][:, 40 + 2 * c + n:41 + 2 * c + n])

    ready = norm([(56, hT)])
    pr3 = scales(4)
    run_all((gemm_b(A["w_ple_2"][0], 0, D, pT, t_pT, ev_pw), 1))
    run_all((gemm_b(A["w_ple_gate_2"][0], 0, D, hT, ready, ev_pg), 1))
    s = S["st"]
    for c in range(2):
        p = tt(pool, s[:, 44 + c:45 + c], s[:, 40 + 2 * c:41 + 2 * c], s[:, 41 + 2 * c:42 + 2 * c], ALU.add,
               ev["sq", c, 0], ev["sq", c, 1])
        p = ts(pool, s[:, 46 + c:47 + c], s[:, 44 + c:45 + c], 1.0 / D, EPS, ALU.mult, ALU.add, p)
        p = tt(pool, s[:, 48 + c:49 + c], s[:, 46 + c:47 + c], S["half_"][:, 0:1], ALU.pow, p)
        for n in range(2):
            sl = slice(n * 512, n * 512 + 512)
            xc = x[:, c, sl]
            d = stt(xc, xc, s[:, 48 + c:49 + c], M[:, n * 512:n * 512 + 512], ALU.mult, ALU.mult, p, t_fin)
            sp("out", A["out"][0, c * 128:c * 128 + 128, sl], xc, d)


def build(nc, A):
    with ExitStack() as ctx:
        def sb(name, shape, dt=F32):
            return ctx.enter_context(nc.sbuf_tensor(name, shape, dt))

        def sem(name):
            return ctx.enter_context(nc.semaphore(name))

        A = dict(A)
        A["scr1"] = nc.dram_tensor("scr1", (16, 383), F32, kind="Internal").ap()
        A["scr2"] = nc.dram_tensor("scr2", (12, 511), F32, kind="Internal").ap()
        A["toe1"] = nc.dram_tensor("toe1", (16, 128, 256), F32, kind="Internal").ap()
        A["toe2"] = nc.dram_tensor("toe2", (12, 128, 384), F32, kind="Internal").ap()
        raw = sb("raw", [128, NR, SLOT])
        hi = sb("whi", [128, NS, SLOT], F32R)
        lo = sb("wlo", [128, NS, SLOT], F32R)
        S = {
            "M": sb("M", [128, 18432]), "RR": sb("RR", [128, 9216], F32R), "x": sb("x", [128, 2, D]),
            "xs": sb("xs", [128, 2, D]), "ident": sb("ident", [128, 128]), "rope": sb("rope", [128, 512]),
            "scan": sb("scan", [128, 256]), "mask": sb("mask", [128, 128], I32),
            "G": sb("G", [128, 84]), "ones": sb("ones", [128, 128]), "dg": sb("dg", [128, 2, 128]),
            "RB": sb("RB", [128, 512]), "tab": sb("tab", [33, 28]),
            "st": sb("st", [128, 64]), "cc": sb("cc", [128, 96]), "ebl": sb("ebl", [128, 16]),
            "half_": sb("half_", [128, 10]), "bcs": sb("bcs", [128, 528]),
        }
        bcs = S["bcs"]
        S["cos"] = S["rope"][:, 0:256].rearrange("p (c d) -> p c d", c=2)
        S["sin"] = S["rope"][:, 256:512].rearrange("p (c d) -> p c d", c=2)
        S["gk2"] = S["rope"][0:16, :]
        S["sq"] = S["dg"][:, :, :].rearrange("p c t -> p (c t)")
        S["onorm"], S["qg"], S["kg"], S["sink"] = bcs[:, 0:256], bcs[:, 256:384], bcs[:, 384:512], bcs[:, 512:528]
        S["half"] = S["half_"][:, 0:2]
        S["half8"] = S["half_"][:, 0:8]
        S["half10"] = S["half_"][:, 0:10]
        S["sel"] = S["M"][0:33, 12288:14204]
        banks = ctx.enter_context(nc.psum_tensor("ps", [128, 8, 512], F32))

        sems = [sem("s_pe"), sem("s_dve"), sem("s_act"), sem("s_pool")]
        made = {}

        def dma_sem(name):
            if name not in made:
                made[name] = sem(name)
            return made[name]

        plan = None
        for _ in range(2):
            q = Queues(sems, dma_sem)
            st = Stream(plan, q, raw, hi, lo)
            write_program(q, S, st, A, [Bank(banks, n) for n in range(8)], banks)
            plan = st.seen
        for engine in (q.pe, q.dve, q.act, q.pool):
            engine.number()
        ends = [(s, n) for s, n in q.sp.sems.values()]

        block = ctx.enter_context(nc.Block())

        @block.sync
        def _(e):
            q.sp.write(e)
            for s, n in ends:
                e.wait_ge(s, n)

        @block.tensor
        def _(e):
            q.pe.write(e)

        @block.vector
        def _(e):
            q.dve.write(e)

        @block.scalar
        def _(e):
            q.act.write(e)

        @block.gpsimd
        def _(e):
            q.pool.write(e)


def constants():
    c = {"c_ident": np.eye(128, dtype=np.float32)}
    j, i = np.arange(128)[:, None], np.arange(128)[None, :]
    c["c_mask"] = ((j <= i) & (j // 64 == i // 64)).astype(np.int32)
    sel = np.zeros((33, 383 + 3 * 511), np.float32)
    d = 255 - np.arange(383)
    n = np.maximum(d, 0)
    large = 16 + (np.log(np.maximum(n, 1) / 16) / np.log(128 / 16) * 16).astype(np.int32)
    bucket = np.where(n < 16, n, np.minimum(large, 31))
    valid = (d >= 0) & (d < 128)
    for m in range(383):
        sel[bucket[m] if valid[m] else 32, m] = 1.0
    for g, (window, dil) in enumerate(((128, 1), (512, 4), (2048, 16))):
        rel = np.arange(511) - 255
        n = np.abs(rel)
        large = 8 + (np.log(np.maximum(n, 1) / 8) / np.log(1024 / 8) * 8).astype(np.int32)
        bucket = (rel > 0) * 16 + np.where(n < 8, n, np.minimum(large, 15))
        valid = (rel % dil == 0) & (n <= window // 2)
        for m in range(511):
            sel[bucket[m] if valid[m] else 32, 383 + 511 * g + m] = 1.0
    c["c_sel"] = sel
    f = np.power(np.float32(10000.0), -np.arange(0, 64, 2, dtype=np.float32) / np.float32(64))
    t = np.arange(256)
    ang = [(p.astype(np.float32)[:, None] * f[None, :]).astype(np.float32) for p in (t // 64, t % 64)]
    cos, sin = [np.cos(a) for a in ang], [np.sin(a) for a in ang]
    c["c_cos"] = np.concatenate([cos[0], cos[0], cos[1], cos[1]], 1).astype(np.float32)
    c["c_sin"] = np.concatenate([-sin[0], sin[0], -sin[1], sin[1]], 1).astype(np.float32)
    return c


INS = ["x", "a_w_in", "a_w_gk2", "a_b_gk", "a_onorm", "a_w_out", "kv_norm", "w_kv", "b_w_q", "b_sinks", "b_w_out",
       "rel_table", "ln_mix", "ln_mlp", "w_up", "w_down", "ln_final", "p_2", "norm_mix_g_2", "w_in_2", "b_gate_2",
       "q_norm_g_2", "k_norm_g_2", "rel_bias_2", "w_out_a_2", "w_out_b_2", "w_out_2", "norm_mlp_g_2", "w_ff1_2",
       "w_ff2_2", "norm_ple_g_2", "w_ple_gate_2", "w_ple_2", "final_norm_g_2"]


def kernel(**inputs):
    import concourse.bacc as bacc
    from concourse.bass_utils import run_bass_kernel_spmd as run

    nc = bacc.Bacc("TRN2", target_bir_lowering=False, num_devices=1)
    arrays, A = {}, {}
    for name in INS:
        arrays["in_" + name] = np.ascontiguousarray(inputs[name])
    for name, a in constants().items():
        arrays["in_" + name] = a
    for name, a in arrays.items():
        A[name[3:]] = nc.dram_tensor(name, a.shape, mybir.dt.from_np(a.dtype), kind="ExternalInput").ap()
    A["out"] = nc.dram_tensor("out_0", (1, T, D), F32, kind="ExternalOutput").ap()
    build(nc, A)
    r = run(nc, [arrays], core_ids=[0])
    return r.results[0]["out_0"]
```

```python
from contextlib import ExitStack

import concourse.bass as bass
from concourse import mybir
import numpy as np

ALU = mybir.AluOpType
ACT = mybir.ActivationFunctionType
F32 = mybir.dt.float32
F32R = mybir.dt.float32r
I32 = mybir.dt.int32
AX = mybir.AxisListType.X

T, D, FF = 256, 1024, 4096
EPS = 1e-6
NR = 3
NS = 3
SLOT = 2048
PROJ = 3088


class Tok:

    def __init__(self, sem=None, val=None):
        self.sem, self.val, self.used, self.step = sem, val, False, 1


class Queue:

    def __init__(self, sem):
        self.sem, self.items = sem, []

    def __call__(self, fn, *waits):
        for w in waits:
            for t in (w if isinstance(w, (list, tuple)) else (w,)):
                if t is not None:
                    t.used = True
                    self.items.append((None, t))
        tok = Tok(self.sem)
        self.items.append((fn, tok))
        return tok

    def number(self):
        n = 0
        for fn, t in self.items:
            if fn is not None and t.used and t.val is None:
                n += 1
                t.val = n

    def write(self, eng):
        met = {}
        for fn, t in self.items:
            if fn is None:
                if met.get(id(t.sem), 0) < t.val:
                    eng.wait_ge(t.sem, t.val)
                    met[id(t.sem)] = t.val
            else:
                ins = fn(eng)
                if t.used or t.step == 16:
                    ins.then_inc(t.sem, t.step)


class Dma:

    def __init__(self, new_sem):
        self.new_sem, self.items, self.sems = new_sem, [], {}

    def __call__(self, name, out, in_, *waits):
        sem, n = self.sems.get(name) or (self.new_sem("d_" + name), 0)
        self.sems[name] = (sem, n + 16)
        for w in waits:
            for t in (w if isinstance(w, (list, tuple)) else (w,)):
                if t is not None:
                    t.used = True
                    self.items.append((None, t))
        tok = Tok(sem, n + 16)
        self.items.append(((out, in_), tok))
        return tok

    def on(self, queue, name, out, in_):
        sem, n = self.sems.get(name) or (self.new_sem("d_" + name), 0)
        self.sems[name] = (sem, n + 16)
        tok = Tok(sem, n + 16)
        tok.step = 16
        queue.items.append((lambda e: e.dma_start(out, in_), tok))
        return tok

    def write(self, eng):
        met = {}
        for what, t in self.items:
            if what is None:
                if met.get(id(t.sem), 0) < t.val:
                    eng.wait_ge(t.sem, t.val)
                    met[id(t.sem)] = t.val
            else:
                eng.dma_start(*what).then_inc(t.sem, 16)


class Bank:
    def __init__(self, all_banks, n):
        self.n, self.t, self.free = n, all_banks[:, n, :], None


class Stream:

    def __init__(self, plan, q, raw, hi, lo):
        self.plan, self.q, self.raw, self.hi, self.lo = plan, q, raw, hi, lo
        self.seen, self.i = [], 0
        self.loaded, self.his, self.split, self.used = [], [], [], []

    def _load(self, j):
        srcs = self.plan[j]
        s = j % NR
        at, toks = 0, []
        free = self.split[j - NR] if j >= NR else None
        for src, kt, n in srcs:
            dst = self.raw[:, s, at:at + kt * n].rearrange("p (k n) -> p k n", k=kt)
            toks.append(self.q.sp("w%d" % s, dst, src.rearrange("(k p) n -> p k n", p=128), free))
            at += kt * n
        self.loaded.append((toks[-1], at))

    def _hi(self, j):
        tok, n = self.loaded[j]
        r, h = self.raw[:, j % NR, 0:n], self.hi[:, j % NS, 0:n]
        self.his.append(self.q.act(lambda e: e.activation(h, r, ACT.Copy), tok, self.used[j - NS] if j >= NS else None))

    def _lo(self, j):
        n = self.loaded[j][1]
        r, h, l = self.raw[:, j % NR, 0:n], self.hi[:, j % NS, 0:n], self.lo[:, j % NS, 0:n]
        m = n // 2
        self.q.dve(lambda e: e.tensor_tensor(l[:, 0:m], r[:, 0:m], h[:, 0:m].bitcast(F32), ALU.subtract),
                   self.his[j], self.used[j - NS] if j >= NS else None)
        self.split.append(self.q.dve(lambda e: e.tensor_tensor(l[:, m:n], r[:, m:n], h[:, m:n].bitcast(F32),
                                                               ALU.subtract)))

    def next(self, srcs, beside=False):
        self.seen.append(srcs)
        i = self.i
        self.i += 1
        assert len(self.used) == i - beside, "a block is taken before the last is given back"
        if self.plan is None:
            n = sum(k * c for _, k, c in srcs)
            return self.hi[:, 0, 0:n], self.lo[:, 0, 0:n], None
        last = len(self.plan)
        self._ahead(min(i + 3 - beside, last), min(i + 2, last))
        n = self.loaded[i][1]
        return self.hi[:, i % NS, 0:n], self.lo[:, i % NS, 0:n], self.split[i]

    def early(self):
        assert len(self.used) == self.i
        if self.plan is not None:
            last = len(self.plan)
            self._ahead(min(self.i + 3, last), min(self.i + 2, last))

    def _ahead(self, his, los):
        last = len(self.plan)
        while len(self.loaded) < min(len(self.split) + NR, last):
            self._load(len(self.loaded))
        while len(self.split) < los or len(self.his) < his:
            if len(self.his) < his and len(self.his) < len(self.loaded):
                self._hi(len(self.his))
            if len(self.split) < los:
                self._lo(len(self.split))
            while len(self.loaded) < min(len(self.split) + NR, last):
                self._load(len(self.loaded))

    def start(self):
        while self.plan is not None and len(self.loaded) < NR:
            self._load(len(self.loaded))

    def first(self):
        if self.plan is not None:
            self._ahead(1, 1)

    def done(self, tok):
        self.used.append(tok)


class Queues:
    def __init__(self, sems, dma_sem):
        self.pe, self.dve, self.act, self.pool = (Queue(s) for s in sems)
        self.sp = Dma(dma_sem)


def run_all(*gens):
    gens = [(g, n) for g, n in gens]
    while gens:
        for it in list(gens):
            g, n = it
            for _ in range(n):
                try:
                    next(g)
                except StopIteration:
                    gens.remove(it)
                    break


def write_program(q, S, st, A, banks, PS):
    pe, dve, act, pool, sp = q.pe, q.dve, q.act, q.pool, q.sp
    M, RR, xs, x = S["M"], S["RR"], S["xs"], S["x"]
    hT = (RR[:, 0:2048].rearrange("p (k t) -> p k t", t=T), RR[:, 2048:4096].rearrange("p (k t) -> p k t", t=T))
    acc, misc = banks[0:4], banks[4:8]
    turn = {"misc": 0, "acc": 0}

    def misc_bank():
        turn["misc"] += 1
        return misc[(turn["misc"] - 1) % 4]

    def misc_pair():
        turn["misc"] += turn["misc"] % 2
        return misc_bank(), misc_bank()

    def acc_pair():
        turn["acc"] += 1
        n = (turn["acc"] - 1) % 2
        return [acc[2 * n], acc[2 * n + 1]]

    def mm(out, lhsT, rhs, start, stop, *w):
        return pe(lambda e: e.matmul(out, lhsT, rhs, start=start, stop=stop, skip_group_check=True), *w)

    def tr(out, in_, *w):
        n = in_.shape[0]
        return pe(lambda e: e.transpose(out, in_, S["ident"][0:n, 0:n]), *w)

    def copy(eng, out, in_, *w):
        if eng is act:
            return act(lambda e: e.activation(out, in_, ACT.Copy), *w)
        return eng(lambda e: e.tensor_copy(out, in_), *w)

    def tt(eng, out, a, b, op, *w):
        return eng(lambda e: e.tensor_tensor(out, a, b, op), *w)

    def ts(eng, out, a, s1, s2, op0, op1, *w):
        if s2 is None:
            return eng(lambda e: e.tensor_scalar(out, a, s1, None, op0), *w)
        return eng(lambda e: e.tensor_scalar(out, a, s1, s2, op0, op1), *w)

    def stt(out, a, s, b, op0, op1, *w):
        return dve(lambda e: e.scalar_tensor_tensor(out=out, in0=a, scalar=s, in1=b, op0=op0, op1=op1), *w)

    def actf(out, in_, f, *w, **k):
        return act(lambda e: e.activation(out, in_, f, **k), *w)

    def prod(out, sh, sl, mh, ml, first, last, *w):
        mm(out, sh, mh, first, False, *w)
        mm(out, sh, ml, False, False)
        return mm(out, sl, mh, False, last)

    t_id = sp("id", S["ident"][:, :], A["c_ident"])
    C = {}

    def gains(at, where, names):
        n = 0
        for name, rows in names:
            a = A[name]
            a = a.rearrange("a (k p) -> (a k) p", p=128) if len(a.shape) == 2 else a.rearrange("(k p) -> k p", p=128)
            t_g = sp("g%d" % at, M[n:n + rows, where:where + 128], a)
            n += rows

        def turn():
            b = misc_bank()
            t = tr(b.t[:, 0:n], M[0:n, where:where + 128], t_id, t_g, b.free)
            C["G"] = copy(dve, S["G"][:, at:at + n], b.t[:, 0:n], t)
            b.free = [C["G"]]
        return turn

    turn_first = gains(0, 0, [("ln_mix", 16)])
    xd = A["x"].rearrange("a (c p) d -> p (a c) d", p=128)
    q.xp = {}
    for n in range(2):
        t = sp("x%d" % n, x[:, :, n * 512:n * 512 + 512], xd[:, :, n * 512:n * 512 + 512])
        q.xp[(0, n)] = q.xp[(1, n)] = t
    st.start()

    def spread(a):
        n = a.shape[-1]
        return bass.AP(tensor=a.tensor, offset=a.offset, ap=[[0, 128], [1, n]])

    t_ms = pool(lambda e: e.memset(S["tab"][32:33, :], -1e30))
    t_hm = pool(lambda e: e.memset(S["half_"][:, :], -0.5), t_ms)
    t_ones = pool(lambda e: e.memset(S["ones"][:, :], 1.0), t_hm)
    t_one = pool(lambda e: e.memset(S["scan"][:, :], 1.0), t_ones)
    t_one = pool(lambda e: e.memset(S["scan"][:, :].rearrange("p (c t) -> p c t", t=64)[:, :, 0:1], 0.0), t_one)
    AT = M[:, 17408:18432]
    t_at0 = pool(lambda e: e.memset(AT, 0.0), t_one)

    turn_first()
    G = S["G"]

    def turn_rest():
        C["rest"]()
        C["G"] = tt(dve, G[:, 76:84], G[:, 40:48], G[:, 68:76], ALU.mult, C["G"])

    def small_loads():
        C["rest"] = gains(16, 15000, [("ln_mlp", 16), ("kv_norm", 8), ("norm_mix_g_2", 8), ("norm_mlp_g_2", 8),
                                      ("norm_ple_g_2", 8), ("a_b_gk", 4), ("ln_final", 8)])
        C["gk2"] = sp("gk2", S["gk2"][:, :], A["a_w_gk2"][0])
        sp("tab", S["tab"][0:32, 0:16], A["rel_table"])
        C["tab"] = sp("tab", S["tab"][0:32, 16:28], A["rel_bias_2"])
        C["sel"] = sp("sel", S["sel"], A["c_sel"])
        C["msk"] = sp("msk", S["mask"][:, :], A["c_mask"])
        sp("bc", S["onorm"], spread(A["a_onorm"]))
        sp("bc", S["qg"], spread(A["q_norm_g_2"]))
        sp("bc", S["kg"], spread(A["k_norm_g_2"]))
        C["bc"] = sp("bc", S["sink"], spread(A["b_sinks"]))

    def bias_rows():
        b = misc_bank()
        t = mm(b.t[0:16, 0:383], S["tab"][0:33, 0:16], S["sel"][:, 0:383], True, True, b.free, C["tab"], t_ms, C["sel"])
        r = copy(dve, M[0:16, 14336:14719], b.t[0:16, 0:383], t)
        b.free = [r]
        C["scr1"] = sp("scr1", A["scr1"], M[0:16, 14336:14719], r)
        for g in range(3):
            b = misc_bank()
            t = mm(b.t[0:4, 0:511], S["tab"][0:33, 16 + 4 * g:20 + 4 * g], S["sel"][:, 383 + 511 * g:894 + 511 * g],
                   True, True, b.free)
            r = copy(dve, M[32 * g:32 * g + 4, 14848:15359], b.t[0:4, 0:511], t)
            b.free = [r]
            C["scr2"] = sp("scr2", A["scr2"][4 * g:4 * g + 4, :], M[32 * g:32 * g + 4, 14848:15359], r)
        C["toe1"] = sp("toe1", A["toe1"], bass.AP(tensor=A["scr1"].tensor, offset=127,
                                                  ap=[[383, 16], [-1, 128], [1, 256]]), C["scr1"])
        C["toe2"] = sp("toe2", A["toe2"], bass.AP(tensor=A["scr2"].tensor, offset=127,
                                                  ap=[[511, 12], [-1, 128], [1, 384]]), C["scr2"])

    class Norm:

        def __init__(self, gains):
            self.gains, self.parts, self.banks = gains, [], []

        def scaled(self, k2, b, t, gains, w):
            for col, (hi, lo) in gains:
                for j in range(2):
                    k = 2 * k2 + j
                    h = actf(hi[:, k, :], b.t[:, j * 256:j * 256 + 256], ACT.Copy, t, w, C["G"],
                             scale=G[:, col + k:col + k + 1])
            for col, (hi, lo) in gains:
                for j in range(2):
                    k = 2 * k2 + j
                    last = stt(lo[:, k, :], b.t[:, j * 256:j * 256 + 256], G[:, col + k:col + k + 1],
                               hi[:, k, :].bitcast(F32), ALU.mult, ALU.subtract, h, w)
            return last

        def turn(self, k2, gains):
            b = misc_bank()
            for j in range(2):
                k = 2 * k2 + j
                for c in range(2):
                    t = tr(b.t[:, j * 256 + c * 128:j * 256 + c * 128 + 128], x[:, c, k * 128:k * 128 + 128],
                           b.free, q.xp[(c, k // 4)], t_id)
            b.free = [self.scaled(k2, b, t, gains, q.hT_free)]
            self.banks.append((b, t))
            self.parts.append(b.free[0])
            return t

        def early(self):
            for k2 in range(2):
                self.turn(k2, self.gains[0:1])
            return self

        def rest(self, w=None):
            self.parts2 = []
            for k2 in range(4):
                if k2 >= len(self.parts):
                    q.turned = self.turn(k2, self.gains[0:1])
                if len(self.gains) > 1:
                    b, t = self.banks[k2]
                    b.free = [self.scaled(k2, b, t, self.gains[1:], [self.parts[k2], w])]
                    self.parts2.append(b.free[0])
            q.hT_free = None
            return self.parts

    def scales(at, *w):
        s = S["st"]
        a = act(lambda e: e.activation(xs[:, 0, :], x[:, 0, :], ACT.Square, accum_out=s[:, 0:1]), q.xs_free, w,
                list(q.xp.values()))
        d = dve(lambda e: e.tensor_tensor_reduce(xs[:, 1, :], x[:, 1, :], x[:, 1, :], 1.0, 0.0, ALU.mult, ALU.add,
                                                 s[:, 1:2]), q.xs_free, w, list(q.xp.values()))
        p = ts(pool, s[:, 2:4], s[:, 0:2], 1.0 / D, EPS, ALU.mult, ALU.add, a, d)
        return tt(pool, s[:, at:at + 2], s[:, 2:4], S["half"][:, :], ALU.pow, p, t_hm)

    def diagonals(at, p):
        s = S["st"]
        for c in range(2):
            d = ts(dve, S["dg"][:, c, :], S["ident"][:, :], s[:, at + c:at + c + 1], None, ALU.mult, None, p,
                   q.dg_free)
        return d

    def rows_scale(at, p, d=None):
        s = S["st"]
        d = d or diagonals(at, p)
        p8 = ts(pool, s[:, 6:8], s[:, at:at + 2], 0.125, None, ALU.mult, None, p)
        b = misc_bank()
        t = mm(b.t[:, 0:256], S["ones"][:, :], S["dg"][:, :, :].rearrange("p c t -> p (c t)"), True, True, b.free, d,
               t_ones)
        q.dg_free = t
        dve(lambda e: e.tensor_copy(S["RB"][:, 0:256], b.t[:, 0:256]), t)
        r = copy(dve, S["RB"][:, 256:512], b.t[:, 0:256], t)
        b.free = [r]
        return [r, p8]

    q.dg_free = None

    def gemm_a(w, c0, n, xT, ready, evac, hook=None):
        kt = xT[0].shape[1]
        for f in range(0, n, 256):
            m = min(256, n - f)
            hi, lo, split = st.next([(w[:, c0 + f:c0 + f + m], kt, m)])
            hi = hi.rearrange("p (k n) -> p k n", k=kt)
            lo = lo.rearrange("p (k n) -> p k n", k=kt)
            b = misc_bank()
            halves = [(0, 4), (4, kt)] if hook and f == 0 else [(0, kt)]
            for k0, k1 in halves:
                for j in range(0, m, 128):
                    mj = min(128, m - j)
                    for k in range(k0, k1):
                        t = prod(b.t[0:mj, 2 * j:2 * j + 256], hi[:, k, j:j + mj], lo[:, k, j:j + mj],
                                 xT[0][:, k, :], xT[1][:, k, :], k == 0 and (j == 0 or k1 == kt), k == kt - 1, b.free, split,
                                 ready[k // 2] if isinstance(ready, list) else ready)
                    if j + 128 < m and len(halves) == 1:
                        yield
                if len(halves) == 2 and k0 == 0:
                    hook()
                    turn["misc"] -= 2
                    yield
            st.done(t)
            evac(f, m, b, t)
            yield

    def gemm_b(w, c0, n, xT, ready, evac, width=512, pairs=None):
        kt = xT[0].shape[1]
        for f in range(0, n, width):
            m = min(width, n - f)
            per = min(kt, SLOT // m)
            bs = acc_pair() if pairs is None else acc[2 * pairs:2 * pairs + 2]
            for k0 in range(0, kt, per):
                hi, lo, split = st.next([(w[k0 * 128:(k0 + per) * 128, c0 + f:c0 + f + m], per, m)])
                hi = hi.rearrange("p (k n) -> p k n", k=per)
                lo = lo.rearrange("p (k n) -> p k n", k=per)
                for c in range(2):
                    for k in range(k0, k0 + per):
                        t = prod(bs[c].t[:, 0:m], xT[0][:, k, c * 128:c * 128 + 128],
                                 xT[1][:, k, c * 128:c * 128 + 128], hi[:, k - k0, :], lo[:, k - k0, :],
                                 k == 0, k == kt - 1, bs[c].free, split,
                                 ready[k // 2] if isinstance(ready, list) else ready)
                    if k0 + per == kt:
                        evac(f, m, c, bs[c], t)
                    if c == 0:
                        yield
                st.done(t)
                yield

    def split_parts(hi, lo, src, *w):
        h = copy(act, hi, src, *w)
        return tt(dve, lo, src, hi.bitcast(F32), ALU.subtract, h, *w)

    def turn_parts(src, n, hi, lo, w, free):
        lasts = []
        for k2 in range(0, n // 128, 2):
            b = misc_bank()
            for j in range(2):
                for c in range(2):
                    t = tr(b.t[:, j * 256 + c * 128:j * 256 + c * 128 + 128],
                           src[:, c, (k2 + j) * 128:(k2 + j) * 128 + 128], b.free, w[k2 // 4], t_id)
            last = split_parts(hi[:, k2:k2 + 2, :].rearrange("p k t -> p (k t)"),
                               lo[:, k2:k2 + 2, :].rearrange("p k t -> p (k t)"), b.t[:, :], t, free)
            b.free = [last]
            lasts.append(last)
        return lasts, t

    def add_x(f, m, c, b, t):
        r = tt(dve, x[:, c, f:f + m], x[:, c, f:f + m], b.t[:, 0:m], ALU.add, t, q.xp[(c, f // 512)])
        b.free = [r]
        q.xp[(c, f // 512)] = r

    def project_by_rows(w, xT, ready, norm):
        last = {}
        for i in range(4):
            hi, lo, split = st.next([(w[i * 256:i * 256 + 256, :], 2, D)])
            hi = hi.rearrange("p (k n) -> p k n", k=2)
            lo = lo.rearrange("p (k n) -> p k n", k=2)
            for at, (c, n) in enumerate(((0, 0), (0, 1), (1, 0), (1, 1)) if i < 3 else ((0, 0), (1, 0), (0, 1), (1, 1))):
                if i == 3 and at == 3:
                    norm.early()
                b = acc[2 * c + n]
                for k in range(2):
                    sl, nl = slice(c * 128, c * 128 + 128), slice(n * 512, n * 512 + 512)
                    last = prod(b.t[:, :], xT[0][:, 2 * i + k, sl], xT[1][:, 2 * i + k, sl],
                                hi[:, k, nl], lo[:, k, nl], i + k == 0, i == 3 and k == 1, b.free, split, ready(i))
                if i == 3:
                    add_x(n * 512, 512, c, b, last)
                if at == 1 and i < 3:
                    yield
            st.done(last)
            yield

    def project(w, xT, ready, norm):
        g = gemm_b(w, 0, D, xT, ready, add_x)
        for _ in range(7):
            next(g)
        norm.early()
        run_all((g, 1))

    def mlp(up, down, norm, after):
        ready = norm.parts
        uT = [(RR[:, 4096 + 2048 * i:5120 + 2048 * i].rearrange("p (k t) -> p k t", t=T),
               RR[:, 5120 + 2048 * i:6144 + 2048 * i].rearrange("p (k t) -> p k t", t=T)) for i in range(2)]
        state = {"n": 0, "u": {}, "late": []}

        def evac(f, m, b, t):
            n = state["n"]
            if n == 0 and "held" not in state:
                state["held"] = (f, m, b, t)
                state["dg"] = diagonals(4, state["rs"])
                return
            if n == 0:
                state["rb"] = rows_scale(4, state["rs"], state["dg"])
                state["n"] = 1
                fill(0, *state["held"])
                n = 1
            state["n"] += 1
            if n > 1:
                lows()
            fill(n, f, m, b, t)

        def fill(n, f, m, b, t):
            i, o = (n // 2) % 2, (n % 2) * 2
            r = M[:, 1024 + 512 * (n % 4):1536 + 512 * (n % 4)]
            a = stt(r, b.t[:, :], 0.0, S["RB"][:, :], ALU.max, ALU.mult, t, q.m_free, state["rb"])
            b.free = [a]
            d = actf(r, r, ACT.Square, a)
            hi = uT[i][0][:, o:o + 2, :].rearrange("p k t -> p (k t)")
            lo = uT[i][1][:, o:o + 2, :].rearrange("p k t -> p (k t)")
            h = copy(act, hi, r, d, q.u_free[i])
            state["late"].append((n, lo, r, hi, h))

        def lows():
            for n, lo, r, hi, h in state["late"]:
                state["u"][n // 2] = tt(dve, lo, r, hi.bitcast(F32), ALU.subtract, h)
            state["late"] = []

        def down_chunk(c4):
            i = c4 % 2
            for kk in range(2):
                k0 = c4 * 4 + kk * 2
                hi, lo, split = st.next([(down[k0 * 128:k0 * 128 + 256, :], 2, D)])
                lows()
                hi = hi.rearrange("p (k n) -> p k n", k=2)
                lo = lo.rearrange("p (k n) -> p k n", k=2)
                for n in range(2):
                    for c in range(2):
                        for k in range(2):
                            b = acc[2 * c + n]
                            sl = slice(c * 128, c * 128 + 128)
                            t = prod(b.t[:, :], uT[i][0][:, kk * 2 + k, sl], uT[i][1][:, kk * 2 + k, sl],
                                     hi[:, k, n * 512:n * 512 + 512], lo[:, k, n * 512:n * 512 + 512],
                                     k0 + k == 0, k0 + k == 31, b.free, split, state["u"][c4])
                st.done(t)
            q.u_free[i] = [t]

        def last_chunk(c4):
            i = c4 % 2
            blocks = []
            for kk in range(2):
                k0 = c4 * 4 + kk * 2
                hi, lo, split = st.next([(down[k0 * 128:k0 * 128 + 256, :], 2, D)], beside=kk == 1)
                blocks.append((hi.rearrange("p (k n) -> p k n", k=2), lo.rearrange("p (k n) -> p k n", k=2), split))
            for n, c in ((0, 0), (0, 1), (1, 0), (1, 1)):
                if (n, c) == (1, 1):
                    after.early()
                b = acc[2 * c + n]
                sl, nl = slice(c * 128, c * 128 + 128), slice(n * 512, n * 512 + 512)
                ends = []
                for kk, (hi, lo, split) in enumerate(blocks):
                    for k in range(2):
                        t = prod(b.t[:, :], uT[i][0][:, kk * 2 + k, sl], uT[i][1][:, kk * 2 + k, sl],
                                 hi[:, k, nl], lo[:, k, nl], False, kk + k == 2, split, state["u"][c4])
                    ends.append(t)
                add_x(n * 512, 512, c, b, t)
            for e in ends:
                st.done(e)

        def up_chunk(c4):
            run_all((gemm_a(up, c4 * 512, 512, hT, ready, evac), 1))

        g = gemm_a(up, 0, 512, hT, ready, evac, norm.rest)
        next(g)
        state["rs"] = scales(4)
        run_all((g, 1))
        for c4 in range(7):
            up_chunk(c4 + 1)
            if c4 == 6:
                q.hT_free = [st.used[-1]]
            down_chunk(c4)
        last_chunk(7)
        q.m_free = [q.xp[(1, 1)]]

    q.u_free = [None, None]
    q.xs_free = q.hT_free = q.m_free = None

    ready = Norm([(0, hT)]).rest()
    st.first()
    pr = scales(4)
    small_loads()
    W = A["a_w_in"][0]
    qT, kT = M[:, 0:1024], M[:, 1024:2048]
    bc, e1 = M[:, 2048:3072], M[:, 3072:4096]
    qt, kt_, kd = M[:, 4096:5120], M[:, 5120:6144], M[:, 6144:7168]
    kdt = M[:, 7168:8192]
    V = M[:, 8192:10240].rearrange("p (c n) -> p c n", c=2)
    GT = M[:, 10240:12288].rearrange("p (c n) -> p c n", c=2)
    O = M[:, 12288:14336].rearrange("p (c n) -> p c n", c=2)
    ST = M[:, 14336:17408]
    glr = xs[0:16, 0, 0:256]
    ev = {"qk": []}

    def ev_glr(f, m, b, t):
        r = tt(dve, glr, b.t[0:16, 0:256], S["RB"][0:16, 0:256], ALU.mult, t, ev["rb"], pr)
        b.free = [r]
        ev["glr"] = r

    def ev_qk(f, m, b, t):
        dst = M[:, 2 * f:2 * f + 512]
        sc = 128 ** -0.5 if f < 512 else 1.0
        if f == 0:
            ev["rb"] = rows_scale(4, pr)
        r = stt(dst, b.t[:, :], sc, S["RB"][:, :], ALU.mult, ALU.mult, t, ev["rb"], C["G"])
        b.free = [r]
        ev["qk"].append(r)

    g = gemm_a(W, 0, 1024, hT, ready, ev_qk)
    for _ in range(4):
        next(g)
    run_all((gemm_a(W, 3072, 16, hT, ready, ev_glr), 1))
    turn_rest()
    bias_rows()

    def gates():
        for h2 in range(2):
            b = misc_bank()
            for j in range(2):
                h = 2 * h2 + j
                t = mm(b.t[:, j * 256:j * 256 + 256], S["gk2"][:, h * 128:h * 128 + 128], glr, True, True,
                       ev["glr"], C["gk2"], b.free)
            for j in range(2):
                h = 2 * h2 + j
                d = ts(dve, bc[:, h * 256:h * 256 + 256], b.t[:, j * 256:j * 256 + 256], G[:, 64 + h:65 + h], None,
                       ALU.add, None, t, C["G"])
            b.free = [d]
            yield
        for n in range(2):
            sp("rope", S["cos"][:, n, :], A["c_cos"][n * 128:n * 128 + 128, :], t)
            C["rope"] = sp("rope", S["sin"][:, n, :], A["c_sin"][n * 128:n * 128 + 128, :], t)
        q.xs_free = [t]
        a = stt(e1, bc, -1.0, bc, ALU.mult, ALU.max, d)
        a = actf(e1, e1, ACT.Exp, a, scale=-1.0)
        a = actf(e1, e1, ACT.Ln, a, bias=1.0)
        d = ts(dve, bc, bc, 0.0, None, ALU.min, None, d, a)
        d = tt(dve, e1, bc, e1, ALU.subtract, a, d)
        d = ts(dve, e1, e1, 1.0 / 16.0, None, ALU.mult, None, d)
        yield
        for h in range(4):
            sl = slice(h * 256, h * 256 + 256)
            d2 = dve(lambda e, sl=sl: e.tensor_tensor_scan(bc[:, sl], S["scan"][:, :], e1[:, sl], 0.0, ALU.mult,
                                                           ALU.add), d, t_one)
        yield
        a = actf(qt, bc, ACT.Exp, d2)
        a2 = actf(kt_, bc, ACT.Exp, d2, scale=-1.0)
        b3 = bc.rearrange("p (g t) -> p g t", t=64)
        d = tt(dve, kd.rearrange("p (g t) -> p g t", t=64), b3, b3[:, :, 63:64].broadcast_to([128, 16, 64]), ALU.subtract,
               d2)
        a3 = actf(kd, kd, ACT.Exp, d, scale=-1.0)
        p = copy(pool, S["ebl"][:, :], qt.rearrange("p (g t) -> p g t", t=64)[:, :, 63:64].rearrange("p g t -> p (g t)"), a)
        ev["ebl"] = p
        yield
        while len(ev["qk"]) < 4:
            yield
        ev["qt"] = tt(dve, qt, qt, qT, ALU.mult, a, p, ev["qk"])
        ev["kt"] = tt(dve, kt_, kt_, kT, ALU.mult, a2, ev["qk"])
        ev["kd"] = tt(dve, kd, kd, kT, ALU.mult, a3, ev["qk"])

    def ev_v(f, m, c, b, t):
        r = actf(V[:, c, f:f + m], b.t[:, 0:m], ACT.Copy, t, pr, scale=S["st"][:, 4 + c:5 + c])
        b.free = [r]
        ev.setdefault("v", []).append(r)

    def ev_gate(f, m, c, b, t):
        sg = xs[:, c, 0:512]
        rs = S["st"][:, 4 + c:5 + c]
        a = actf(sg, b.t[:, 0:m], ACT.Sigmoid, t, q.xs_free, ev.get("g"), scale=rs)
        r = stt(GT[:, c, f:f + m], b.t[:, 0:m], rs, sg, ALU.mult, ALU.mult, a)
        b.free = [r]
        ev["g"] = r

    def attn_gla():
        for h2 in range(2):
            b = misc_bank()
            for j in range(2):
                h = 2 * h2 + j
                for c in range(2):
                    t = tr(b.t[:, j * 256 + c * 128:j * 256 + c * 128 + 128],
                           kd[:, h * 256 + c * 128:h * 256 + c * 128 + 128], b.free, ev["kd"], t_id)
            r = copy(act, kdt[:, h2 * 512:h2 * 512 + 512], b.t[:, :], t)
            b.free = [r]
            ev["kdt"] = r
            yield
            b = misc_bank()
            for j in range(2):
                h = 2 * h2 + j
                for c in range(2):
                    sl = slice(h * 256 + c * 128, h * 256 + c * 128 + 128)
                    t = mm(b.t[:, j * 256 + c * 128:j * 256 + c * 128 + 128], kt_[:, sl], qt[:, sl], True, True,
                           b.free, ev["kt"], ev["qt"])
            msk = S["mask"][:, :]
            for n in range(4):
                r = dve(lambda e, n=n, b=b, h2=h2: e.copy_predicated(
                    AT[:, h2 * 512 + n * 128:h2 * 512 + n * 128 + 128], msk, b.t[:, n * 128:n * 128 + 128]),
                    t, t_at0, C["msk"])
            b.free = [r]
            ev["at"] = r
            yield
        prev = None
        for c in range(3):
            rows = slice(64 * (c % 2), 64 * (c % 2) + 64)
            for h2 in range(2):
                b = misc_bank()
                for j in range(2):
                    h = 2 * h2 + j
                    t = mm(b.t[:, j * 256:j * 256 + 256], kdt[rows, h * 256 + (c // 2) * 128:h * 256 + (c // 2) * 128 + 128],
                           V[rows, c // 2, h * 256:h * 256 + 256], True, True, b.free, ev["kdt"], ev["v"])
                for j in range(2):
                    h = 2 * h2 + j
                    o = c * 1024 + h * 256
                    if c == 0:
                        r = copy(dve, ST[:, o:o + 256], b.t[:, j * 256:j * 256 + 256], t, C["scr1"], C["scr2"])
                    else:
                        r = stt(ST[:, o:o + 256], ST[:, o - 1024:o - 768], S["ebl"][:, h * 4 + c:h * 4 + c + 1],
                                b.t[:, j * 256:j * 256 + 256], ALU.mult, ALU.add, t, prev, ev["ebl"])
                b.free = [r]
            prev = r
            yield
        ev["st"] = prev
        for c2 in range(2):
            for h2 in range(2):
                b = misc_bank()
                for j in range(2):
                    h = 2 * h2 + j
                    out = b.t[:, j * 256:j * 256 + 256]
                    mm(out, AT[:, h * 256 + c2 * 128:h * 256 + c2 * 128 + 128], V[:, c2, h * 256:h * 256 + 256],
                       True, False, b.free, ev["at"], ev["v"])
                    for c in (2 * c2, 2 * c2 + 1):
                        if c:
                            rows = slice(64 * (c % 2), 64 * (c % 2) + 64)
                            t = mm(b.t[rows, j * 256:j * 256 + 256], qt[:, h * 256 + c * 64:h * 256 + c * 64 + 64],
                                   ST[:, (c - 1) * 1024 + h * 256:(c - 1) * 1024 + h * 256 + 256], False, True,
                                   ev["st"])
                r = copy(act, O[:, c2, h2 * 512:h2 * 512 + 512], b.t[:, :], t)
                b.free = [r]
                for j in range(2):
                    h = 2 * h2 + j
                    n = h * 2 + c2
                    s = O[:, c2, h * 256:h * 256 + 256]
                    r2 = dve(lambda e, s=s, n=n, j=j: e.tensor_tensor_reduce(
                        S["sq"][:, 0:256], s, s, 1.0, 0.0, ALU.mult, ALU.add, S["st"][:, 8 + n:9 + n]), r, ev.get("sq"), q.dg_free)
                    ev["sq"] = r2
                yield
        p = ts(pool, S["st"][:, 16:24], S["st"][:, 8:16], 1.0 / 256, EPS, ALU.mult, ALU.add, r2)
        p = tt(pool, S["st"][:, 24:32], S["st"][:, 16:24], S["half8"], ALU.pow, p, t_hm)
        yield
        for h in range(4):
            for c in range(2):
                s = O[:, c, h * 256:h * 256 + 256]
                ev["on"] = stt(s, s, S["st"][:, 24 + h * 2 + c:25 + h * 2 + c], S["onorm"], ALU.mult, ALU.mult, p,
                               C["bc"])
        yield

    def k_and_v():
        yield from g
        yield from gemm_b(W, 1024, 1024, hT, ready, ev_v)

    run_all((k_and_v(), 1), (gates(), 1))
    run_all((gemm_b(W, 2048, 1024, hT, ready, ev_gate), 1), (attn_gla(), 2))
    for n in range(2):
        for c in range(2):
            s = O[:, c, n * 512:n * 512 + 512]
            ev["o%d" % n] = tt(dve, s, s, GT[:, c, n * 512:n * 512 + 512], ALU.mult, ev["on"], ev["g"])
    q.xs_free = [ev["g"]]
    yT = (RR[:, 4096:6144].rearrange("p (k t) -> p k t", t=T), RR[:, 6144:8192].rearrange("p (k t) -> p k t", t=T))
    last, tp = turn_parts(O, 1024, yT[0], yT[1], [ev["o0"], ev["o1"]], None)
    q.hT_free = [tp]
    q.m_free = [tp]

    nm = Norm([(16, hT)])
    project(A["a_w_out"][0], yT, last, nm)
    q.u_free = [list(q.xp.values())] * 2

    BS = M[:, 13824:17920].rearrange("p (h c) -> p h c", h=16)
    t_bias = sp("bias", BS, A["toe1"].rearrange("h p c -> p h c"), C["toe1"], q.m_free)
    kvp = (RR[:, 4096:6144].rearrange("p (k t) -> p k t", t=T), RR[:, 6144:8192].rearrange("p (k t) -> p k t", t=T))
    nm2 = Norm([(8, hT), (32, kvp)])
    mlp(A["w_up"][0], A["w_down"][0], nm, nm2)

    QT = M[:, 0:2048].rearrange("p (f t) -> p f t", t=T)
    KT = M[:, 2048:2560].rearrange("p (g t) -> p g t", t=T)
    V = M[:, 2560:2816].rearrange("p (c n) -> p c n", c=2)
    qtok = {}

    def ev_q(f, m, b, t):
        r = copy(act, M[:, 2 * f:2 * f + 512], b.t[:, :], t, q.m_free)
        b.free = [r]
        qtok[f // 256] = r

    mlp_read = st.used[-1]
    gq = gemm_a(A["b_w_q"][0], 0, 1024, hT, nm2.parts, ev_q, lambda: nm2.rest(mlp_read))
    for _ in range(2):
        next(gq)
    ready = nm2.parts2
    hi, lo, split = st.next([(A["w_kv"], 8, 256)])
    hi = hi.rearrange("p (k n) -> p k n", k=8)
    lo = lo.rearrange("p (k n) -> p k n", k=8)
    b = misc_bank()
    for k in range(8):
        t = prod(b.t[:, 0:256], hi[:, k, 0:128], lo[:, k, 0:128], kvp[0][:, k, :], kvp[1][:, k, :],
                 k == 0, k == 7, b.free, split, ready[k // 2])
    bk, tk = b, t
    ps_ = scales(4)
    b = misc_bank()
    for c in range(2):
        for k in range(8):
            t = prod(b.t[:, c * 128:c * 128 + 128], kvp[0][:, k, c * 128:c * 128 + 128],
                     kvp[1][:, k, c * 128:c * 128 + 128], hi[:, k, 128:256], lo[:, k, 128:256], k == 0, k == 7, b.free)
    st.done(t)
    for c in range(2):
        t_v = actf(V[:, c, :], b.t[:, c * 128:c * 128 + 128], ACT.Copy, t, ps_, q.m_free, scale=S["st"][:, 4 + c:5 + c])
    b.free = [t_v]
    rb = rows_scale(4, ps_)
    for g in range(2):
        for half in range(2):
            t_k = tt(dve, KT[64 * half:64 * half + 64, g, :], bk.t[64 * g:64 * g + 64, 0:256],
                     S["RB"][64 * g:64 * g + 64, 0:256], ALU.mult, tk, q.m_free, rb)
    bk.free = [t_k]
    kv_used = [t]
    oT = (RR[:, 4096:6144].rearrange("p (k t) -> p k t", t=T), RR[:, 6144:8192].rearrange("p (k t) -> p k t", t=T))
    ring = {}

    t_nsink = ts(pool, S["nsink"][:, :], S["sink"], -1.0, None, ALU.mult, None, C["bc"])

    def swa():
        info = {}

        def scores(p):
            b = acc[0:2] if p < 6 else misc[0:2]
            kv = p // 4
            w = PS[:, b[0].n:b[0].n + 2, 0:384]
            for j in range(2):
                r0 = 64 * j
                mm(w[:, j, 0:128], QT[r0:r0 + 64, p, 0:128], KT[r0:r0 + 64, kv, 0:128], True, True, b[0].free,
                   b[1].free, qtok[p // 2], t_k)
                t = mm(w[:, j, 128:384], QT[r0:r0 + 64, p, 128:256], KT[r0:r0 + 64, kv, :], True, True)
            info[p] = (b, w, t)

        def soft(p):
            b, pp, t = info[p]
            s = M[:, 2816 + 768 * (p % 3):3584 + 768 * (p % 3)].rearrange("p (h k) -> p h k", h=2)
            rs = S["st"]
            stt(s[:, :, 0:128], pp[:, :, 0:128], rs[:, 6:7], BS[:, 2 * p:2 * p + 2, 128:256], ALU.mult, ALU.add, t,
                t_bias, rb, ring.get(("s", p % 3)))
            d = stt(s[:, :, 128:384], pp[:, :, 128:384], rs[:, 7:8], BS[:, 2 * p:2 * p + 2, :], ALU.mult, ALU.add)
            b[0].free = b[1].free = [d]
            c = S["cc"][:, 32 * (p % 3):32 * (p % 3) + 32]
            dve(lambda e: e.tensor_reduce(c[:, 0:2], s[:, :, 0:128], AX, ALU.max, negate=True), d)
            d = dve(lambda e: e.tensor_reduce(c[:, 2:4], s[:, :, 128:384], AX, ALU.max, negate=True))
            skb = S["sink"][:, 2 * p:2 * p + 2].rearrange("p (a h) -> p a h", a=1).broadcast_to([128, 2, 2])
            nskb = S["nsink"][:, 2 * p:2 * p + 2].rearrange("p (a h) -> p a h", a=1).broadcast_to([128, 2, 2])
            d = tt(dve, c[:, 4:8].rearrange("p (b h) -> p b h", b=2), c[:, 0:4].rearrange("p (b h) -> p b h", b=2), nskb,
                   ALU.min, d, t_nsink)
            k = tt(pool, c[:, 8:12].rearrange("p (b h) -> p b h", b=2), c[:, 4:8].rearrange("p (b h) -> p b h", b=2), skb,
                   ALU.add, d)
            for h in range(2):
                actf(s[:, h, 0:128], s[:, h, 0:128], ACT.Exp, d, bias=c[:, 4 + h:5 + h], accum_out=c[:, 12 + h:13 + h])
                actf(s[:, h, 128:384], s[:, h, 128:384], ACT.Exp, bias=c[:, 6 + h:7 + h],
                     accum_out=c[:, 14 + h:15 + h])
            a = actf(c[:, 16:20], c[:, 8:12], ACT.Exp, k)
            info[p] = (s, c, a)

        def turned(p):
            s, c, a = info[p]
            d = tt(dve, c[:, 20:24], c[:, 12:16], c[:, 16:20], ALU.add, a)
            d = dve(lambda e: e.reciprocal(c[:, 24:28], c[:, 20:24]), d)
            actf(s[:, 1, 0:128], s[:, 1, 0:128], ACT.Copy, d, scale=c[:, 25:26])
            d1 = actf(s[:, 1, 128:384], s[:, 1, 128:384], ACT.Copy, scale=c[:, 27:28])
            ts(dve, s[:, 0, 0:128], s[:, 0, 0:128], c[:, 24:25], None, ALU.mult, None, d)
            d = ts(dve, s[:, 0, 128:384], s[:, 0, 128:384], c[:, 26:27], None, ALU.mult, None)
            b = misc_pair() if p < 4 else misc[2:4]
            for h in range(2):
                for n in range(3):
                    t = tr(b[h].t[:, n * 128:n * 128 + 128], s[:, h, n * 128:n * 128 + 128], b[0].free, b[1].free, d1 if h else d)
            ring[("s", p % 3)] = t
            v = M[:, 5120 + 768 * (p % 2):5888 + 768 * (p % 2)].rearrange("p (h k) -> p h k", h=2)
            r = copy(act, v, PS[:, b[0].n:b[0].n + 2, 0:384], t, ring.get(("p", p % 2)))
            b[0].free = b[1].free = [r]
            info[p] = (v, r)

        def values(p):
            v, r = info[p]
            kv = p // 4
            b = acc[2 + p % 2] if p < 4 else misc[3]
            w = b.t[:, 0:256]
            v0, v1 = V[:, 0, 64 * kv:64 * kv + 64], V[:, 1, 64 * kv:64 * kv + 64]
            for h in range(2):
                rows = slice(64 * h, 64 * h + 64)
                mm(w[rows, 0:128], v0, v[:, h, 0:128], True, True, b.free, r, t_v)
                mm(w[rows, 128:256], v0, v[:, h, 128:256], True, False)
                t = mm(w[rows, 128:256], v1, v[:, h, 256:384], False, True)
            ring[("p", p % 2)] = t
            info[p] = (b, w, t)

        def parts(p):
            b, w, t = info[p]
            r = split_parts(oT[0][:, p, :], oT[1][:, p, :], w, t, kv_used)
            b.free = [r]
            ev["swa", p] = r

        scores(0)
        for i in range(11):
            if i < 8:
                soft(i)
            if i + 1 < 8:
                scores(i + 1)
            if 3 <= i:
                parts(i - 3)
            if 0 <= i - 1 < 8:
                turned(i - 1)
            if 0 <= i - 2 < 8:
                values(i - 2)
            yield

    next(gq)
    attn = swa()
    for _ in range(5):
        next(gq)
        next(attn)
    next(gq, None)
    next(attn)
    q.hT_free = [st.used[-1]]
    nm = Norm([(24, hT)])
    run_all((project_by_rows(A["b_w_out"][0], oT, lambda i: ev["swa", 2 * i + 1], nm), 1), (attn, 1))
    q.u_free = [[q.xp[(1, 1)]]] * 2
    q.m_free = [q.xp[(1, 1)]]
    BB = M[:, 13824:18432].rearrange("p (h c) -> p h c", h=12)
    t_bb = sp("bias", BB, A["toe2"].rearrange("h p c -> p h c"), C["toe2"], q.m_free)
    t_lnf = sp("lnf", M[:, 0:1024], spread(A["ln_final"]), q.m_free)
    nm2 = Norm([(76, hT)])
    mlp(A["w_up"][1], A["w_down"][1], nm, nm2)

    ready = nm2.parts
    ev = {}
    QA = M[:, 9216:12288].rearrange("p (c n) -> p c n", c=2)
    products_a = gemm_b(A["w_in_2"][0], 0, 1536, hT, ready, lambda *a: ev["to"](*a))
    next(products_a)
    nm2.rest()
    next(products_a)
    st.early()
    p = scales(32)
    st_ = S["st"]
    for c in range(2):
        for n in range(2):
            sl = slice(n * 512, n * 512 + 512)
            q.xp[(c, n)] = stt(x[:, c, sl], x[:, c, sl], st_[:, 32 + c:33 + c], M[:, n * 512:n * 512 + 512], ALU.mult,
                               ALU.mult, p, t_lnf, q.turned)
    q.m_free = [q.xp[(1, 1)]]
    pr2 = scales(34, q.xp[(1, 1)])
    pr2 = tt(pool, st_[:, 4:6], st_[:, 32:34], st_[:, 34:36], ALU.mult, pr2)
    W = A["w_in_2"][0]
    QB = M[:, 0:1536].rearrange("p (f t) -> p f t", t=T)
    KB = M[:, 1536:3072].rearrange("p (f t) -> p f t", t=T)
    VB = M[:, 3072:4608].rearrange("p (c n) -> p c n", c=2)

    def ev_b(base):
        def f_(f, m, b, t):
            o = base + 2 * f
            if base:
                r = tt(dve, M[:, o:o + 512], b.t[:, :], S["RB"][:, :], ALU.mult, t, q.m_free, rb2)
            else:
                r = copy(act, M[:, o:o + 512], b.t[:, :], t, q.m_free)
            ev[(base, f // 256)] = r
            b.free = [r]
        return f_

    def ev_vb(f, m, c, b, t):
        r = actf(VB[:, c, f:f + m], b.t[:, 0:m], ACT.Copy, t, q.m_free, pr2, scale=S["st"][:, 4 + c:5 + c])
        b.free = [r]
        ev["vb"] = r

    def ev_a(f, m, c, b, t):
        r = actf(QA[:, c, f:f + m], b.t[:, 0:m], ACT.Copy, t, q.m_free, pr2, scale=S["st"][:, 4 + c:5 + c])
        b.free = [r]
        ev["qa%d" % c] = r

    oB = (RR[:, 8192:8704].rearrange("p (k t) -> p k t", t=T), RR[:, 8704:9216].rearrange("p (k t) -> p k t", t=T))
    ev["to"] = ev_a
    run_all((products_a, 1))
    rb2 = rows_scale(4, pr2)

    def dilated():
        info = {}

        def scores(h, c):
            s = M[:, 4608 + (h % 2) * 1536 + c * 768:5376 + (h % 2) * 1536 + c * 768]
            b0, b1 = misc_pair()
            for g in range(3):
                hh = 4 * g + h
                r0 = 64 * (hh % 2)
                out = b0.t[:, g * 256:g * 256 + 256] if g < 2 else b1.t[:, 0:256]
                t = mm(out, QB[r0:r0 + 64, hh // 2, c * 128:c * 128 + 128], KB[r0:r0 + 64, hh // 2, :], True, True,
                       b0.free, b1.free, ev[(0, 2)], ev[(1536, 2)])
            info[(h, c)] = (s, b0, b1, t)

        def soft(h, c):
            s, b0, b1, t = info[(h, c)]
            cc = S["cc"][:, 8 * (2 * (h % 2) + c):8 * (2 * (h % 2) + c) + 8]
            c0 = 128 - 128 * c
            rs = S["st"][:, 6 + c:7 + c]
            stt(s[:, 0:512].rearrange("p (g c) -> p g c", g=2), b0.t[:, :].rearrange("p (g c) -> p g c", g=2), rs,
                BB[:, h:h + 5:4, c0:c0 + 256], ALU.mult, ALU.add, t, t_bb, rb2, ring.get(("s", h % 2, c)))
            d = stt(s[:, 512:768], b1.t[:, 0:256], rs, BB[:, 8 + h, c0:c0 + 256], ALU.mult, ALU.add)
            b0.free = b1.free = [d]
            d = dve(lambda e: e.tensor_reduce(cc[:, 0:1], s, AX, ALU.max, negate=True), d)
            a = actf(s, s, ACT.Exp, d, bias=cc[:, 0:1], accum_out=cc[:, 1:2])
            d = dve(lambda e: e.reciprocal(cc[:, 2:3], cc[:, 1:2]), a)
            d = ts(dve, s, s, cc[:, 2:3], None, ALU.mult, None, d)
            info[(h, c)] = (s, d)

        def turned(h, c):
            s, d = info[(h, c)]
            p = M[:, 7680 + 768 * c:8448 + 768 * c]
            b0, b1 = misc_pair()
            for n in range(6):
                out = b0.t[:, n * 128:n * 128 + 128] if n < 4 else b1.t[:, n * 128 - 512:n * 128 - 384]
                t = tr(out, s[:, n * 128:n * 128 + 128], b0.free, b1.free, d)
            ring[("s", h % 2, c)] = t
            copy(act, p[:, 0:512], b0.t[:, :], t, ring.get(("p", c)))
            r = copy(act, p[:, 512:768], b1.t[:, 0:256])
            b0.free = b1.free = [r]
            info[(h, c)] = (p, r)

        def values(h, c):
            p, r = info[(h, c)]
            b = acc[2 + h // 2]
            rows = slice(64 * (h % 2), 64 * (h % 2) + 64)
            for n in range(6):
                hh = 4 * (n // 2) + h
                t = mm(b.t[rows, c * 128:c * 128 + 128], VB[:, n % 2, hh * 64:hh * 64 + 64],
                       p[:, n * 128:n * 128 + 128], n == 0, n == 5, b.free, r, ev["vb"])
            ring[("p", c)] = t
            info[(h, c)] = (b, t)

        def parts(h, c):
            b, t = info[(h, c)]
            if h % 2 and c:
                r = split_parts(oB[0][:, h // 2, :], oB[1][:, h // 2, :], b.t[:, 0:256], t)
                b.free = [r]
                ev["ob"] = r

        order = [(h, c) for h in range(4) for c in range(2)]
        scores(*order[0])
        for i in range(11):
            if 0 <= i - 1 < 8:
                turned(*order[i - 1])
            if i < 8:
                soft(*order[i])
            yield
            if 0 <= i - 3 < 8:
                parts(*order[i - 3])
            if i + 1 < 8:
                scores(*order[i + 1])
            if 0 <= i - 2 < 8:
                values(*order[i - 2])
            yield
        ev["b_end"] = t_last = ring[("p", 1)]

    RT = M[:, 12288:13568]
    PHASE = {}

    def rope():
        for c in range(2):
            X = QA[:, c, 0:1280]
            X3 = X.rearrange("p (h d) -> p h d", d=128)
            a = actf(RT, X, ACT.Square, ev["qa%d" % c], PHASE.get("r"))
            s = S["st"][:, 32:64]
            yield
            d = dve(lambda e: e.tensor_reduce(s[:, 0:10], RT.rearrange("p (h d) -> p h d", d=128), AX, ALU.add), a)
            p = ts(pool, s[:, 10:20], s[:, 0:10], 1.0 / 128, EPS, ALU.mult, ALU.add, d)
            p = tt(pool, s[:, 20:30], s[:, 10:20], S["half10"], ALU.pow, p)
            yield
            for h in range(10):
                g = S["qg"] if h < 8 else S["kg"]
                d = stt(X3[:, h, :], X3[:, h, :], s[:, 20 + h:21 + h], g, ALU.mult, ALU.mult, p)
            yield
            x5 = X.rearrange("p (h a b d) -> p h a b d", a=2, b=2, d=32)
            r5 = RT.rearrange("p (h a b d) -> p h a b d", a=2, b=2, d=32)
            sn = S["sin"][:, c, :].rearrange("p (a b d) -> p a b d", a=2, b=2)
            for bb in range(2):
                for aa in range(2):
                    w = sn[:, aa:aa + 1, bb, :].broadcast_to([128, 10, 32])
                    d = tt(dve, r5[:, :, aa, bb, :], x5[:, :, aa, 1 - bb, :], w, ALU.mult, d if not (aa or bb) else None, C["rope"])
            p = tt(pool, X3, X3, S["cos"][:, c:c + 1, :].broadcast_to([128, 10, 128]), ALU.mult, d)
            yield
            PHASE["r"] = tt(dve, X, X, RT, ALU.add, p)
            yield
        QTA = xs[:, :, :].rearrange("p c n -> p (c n)")
        KTA = M[:, 12288:12800]
        for h2 in range(5):
            b = misc_bank()
            for j in range(2):
                for c in range(2):
                    h = 2 * h2 + j
                    t = tr(b.t[:, j * 256 + c * 128:j * 256 + c * 128 + 128], QA[:, c, h * 128:h * 128 + 128], b.free,
                           PHASE["r"])
            dst = QTA[:, h2 * 512:h2 * 512 + 512] if h2 < 4 else KTA
            r = copy(dve, dst, b.t[:, :], t, pr2)
            b.free = [r]
            PHASE["qt%d" % h2] = r
            yield

    def products_b():
        yield from gemm_a(W, 1536, 768, hT, ready, ev_b(0))
        yield from gemm_a(W, 2304, 768, hT, ready, ev_b(1536))
        yield from gemm_b(W, 3072, 768, hT, ready, ev_vb)

    QTA = xs[:, :, :].rearrange("p c n -> p (c n)")
    KTA = M[:, 12288:12800]
    run_all((products_b(), 2), (rope(), 1))
    SA = QA[:, :, 0:1024]
    SB = M[:, 4608:6656].rearrange("p (c n) -> p c n", c=2)
    BG, BG2 = M[:, 12800:13824], M[:, 6656:7680]
    t_bg = sp("bg", BG, spread(A["b_gate_2"][:, 0:1024]), PHASE["qt4"])

    def ev_ga(f, m, c, b, t):
        r = stt(SA[:, c, f:f + m], b.t[:, 0:m], S["st"][:, 4 + c:5 + c], BG[:, f:f + m], ALU.mult, ALU.add, t, t_bg,
                PHASE["qt4"], pr2)
        b.free = [r]
        ev["prea"] = r

    def ev_gb(f, m, c, b, t):
        r = stt(SB[:, c, f:f + m], b.t[:, 0:m], S["st"][:, 4 + c:5 + c], BG2[:, f:f + m], ALU.mult, ALU.add, t, t_bg2,
                b_end, pr2)
        b.free = [r]
        ev["preb"] = r

    gg = gemm_b(W, 3840, 1024, hT, ready, ev_ga, pairs=0)
    mix = dilated()
    next(mix)
    run_all((gg, 1), (mix, 2))
    b_end = ev["b_end"]
    t_bg2 = sp("bg", BG2, spread(A["b_gate_2"][:, 1024:2048]), b_end)
    gg = gemm_b(W, 4864, 1024, hT, ready, ev_gb)
    oA = yT
    u_free = q.u_free

    def full():
        info = {}

        def scores(h):
            b = misc_bank()
            for c in range(2):
                t = mm(b.t[:, c * 256:c * 256 + 256], QTA[:, h * 256 + c * 128:h * 256 + c * 128 + 128],
                       KTA[:, (h // 4) * 256:(h // 4) * 256 + 256], True, True, b.free, PHASE["qt%d" % (h // 2)],
                       PHASE["qt4"])
            info[h] = (b, t)

        def soft(h):
            b, t = info[h]
            s = M[:, 512 * (h % 3):512 * (h % 3) + 512]
            cc = S["cc"][:, 8 * (h % 3):8 * (h % 3) + 8]
            d = dve(lambda e: e.tensor_reduce(cc[:, 0:2], b.t[:, :].rearrange("p (c k) -> p c k", c=2), AX, ALU.max), t)
            d = ts(dve, cc[:, 2:4], cc[:, 0:2], -(128 ** -0.5), None, ALU.mult, None, d)
            for c in range(2):
                a = actf(s[:, c * 256:c * 256 + 256], b.t[:, c * 256:c * 256 + 256], ACT.Exp, d, b_end,
                         ring.get(("sa", h % 3)), bias=cc[:, 2 + c:3 + c], scale=128 ** -0.5, accum_out=cc[:, 4 + c:5 + c])
            b.free = [a]
            d = dve(lambda e: e.reciprocal(cc[:, 6:8], cc[:, 4:6]), a)
            for c in range(2):
                d = ts(dve, s[:, c * 256:c * 256 + 256], s[:, c * 256:c * 256 + 256], cc[:, 6 + c:7 + c], None, ALU.mult,
                       None, d if c == 0 else None)
            info[h] = (s, d)

        def turned(h):
            s, d = info[h]
            p = M[:, 1536 + 512 * (h % 2):2048 + 512 * (h % 2)]
            b = misc_bank()
            for kt in range(2):
                for c in range(2):
                    t = tr(b.t[:, kt * 256 + c * 128:kt * 256 + c * 128 + 128],
                           s[:, c * 256 + kt * 128:c * 256 + kt * 128 + 128], b.free, d)
            ring[("sa", h % 3)] = t
            r = copy(act, p, b.t[:, :], t, ring.get(("pa", h % 2)), b_end)
            b.free = [r]
            info[h] = (p, r)

        def values(h):
            p, r = info[h]
            b = misc_bank()
            for kt in range(2):
                t = mm(b.t[:, 0:256], QA[:, kt, 1280 + (h // 4) * 128:1408 + (h // 4) * 128], p[:, kt * 256:kt * 256 + 256],
                       kt == 0, kt == 1, b.free, r)
            ring[("pa", h % 2)] = t
            info[h] = (b, t)

        def parts(h):
            b, t = info[h]
            r = split_parts(oA[0][:, h, :], oA[1][:, h, :], b.t[:, 0:256], t, u_free)
            b.free = [r]
            ev["oa"] = r

        scores(0)
        for i in range(11):
            if 0 <= i - 1 < 8:
                turned(i - 1)
            if i < 8:
                soft(i)
            yield
            if 0 <= i - 3 < 8:
                parts(i - 3)
            if i + 1 < 8:
                scores(i + 1)
            if 0 <= i - 2 < 8:
                values(i - 2)
            yield

    u_free = [t for f in q.u_free for t in (f or [])]
    mix = full()
    next(mix)
    run_all((gg, 1), (mix, 2))
    q.xs_free = [ring[("pa", 1)]]
    for c in range(2):
        a = actf(SA[:, c, :], SA[:, c, :], ACT.Sigmoid, ev["prea"])
    a = actf(SB, SB, ACT.Sigmoid, ev["preb"])
    PT_ = M[:, 0:512].rearrange("p (c n) -> p c n", c=2)
    t_p = sp("p", PT_, A["p_2"][0, 0].rearrange("(c p) n -> p c n", p=128), ring[("pa", 1)])

    def ev_ya(f, m, c, b, t):
        r = tt(dve, SA[:, c, f:f + m], SA[:, c, f:f + m], b.t[:, 0:m], ALU.mult, t, a)
        b.free = [r]

    def ev_yb(f, m, c, b, t):
        s = SB[:, c, f:f + m]
        r = tt(dve, s, s, b.t[:, 0:m], ALU.mult, t, a)
        b.free = [r]
        ev["m", f // 512] = tt(dve, s, s, SA[:, c, f:f + m], ALU.add, r)

    run_all((gemm_b(A["w_out_a_2"][0], 0, D, oA, ev["oa"], ev_ya), 1))
    ya_read = st.used[-1]
    run_all((gemm_b(A["w_out_b_2"][0], 0, D, oB, ev["ob"], ev_yb), 1))
    last, tp = turn_parts(SB, 1024, yT[0], yT[1], [ev["m", 0], ev["m", 1]], ya_read)
    q.hT_free = [tp]
    nm = Norm([(48, hT)])
    project(A["w_out_2"][0], yT, last, nm)
    q.u_free = [[q.xp[(1, 1)]]] * 2
    q.m_free = [tp]
    pT = oB
    b = misc_bank()
    for j in range(2):
        for c in range(2):
            t = tr(b.t[:, j * 256 + c * 128:j * 256 + c * 128 + 128], PT_[:, c, j * 128:j * 128 + 128], b.free, t_p)
    t_pT = split_parts(pT[0].rearrange("p k t -> p (k t)"), pT[1].rearrange("p k t -> p (k t)"), b.t[:, :], t, tp)
    b.free = [t_pT]
    t_fin = sp("fin", M[:, 0:1024], spread(A["final_norm_g_2"]), t)
    nm2 = Norm([(56, hT)])
    mlp(A["w_ff1_2"][0], A["w_ff2_2"][0], nm, nm2)

    PW = M[:, 4096:6144].rearrange("p (c n) -> p c n", c=2)
    SG = M[:, 6144:8192].rearrange("p (c n) -> p c n", c=2)
    ev["pw"] = []

    def ev_pw(f, m, c, b, t):
        r = copy(act, PW[:, c, f:f + m], b.t[:, 0:m], t)
        b.free = [r]
        ev["pw"].append(r)

    def ev_pg(f, m, c, b, t):
        s, xc, n = SG[:, c, f:f + m], x[:, c, f:f + m], f // 512
        a = actf(s, b.t[:, 0:m], ACT.Sigmoid, t, pr3, scale=S["st"][:, 4 + c:5 + c])
        b.free = [a]
        d = tt(dve, s, s, PW[:, c, f:f + m], ALU.mult, a, ev["pw"])
        d = tt(dve, xc, xc, s, ALU.add, d, q.turned)
        ev["sq", c, n] = actf(s, xc, ACT.Square, d, accum_out=S["st"][:, 40 + 2 * c + n:41 + 2 * c + n])

    g = gemm_b(A["w_ple_2"][0], 0, D, pT, t_pT, ev_pw)
    next(g)
    nm2.rest()
    next(g)
    next(g)
    pr3 = scales(4)
    run_all((g, 1))
    run_all((gemm_b(A["w_ple_gate_2"][0], 0, D, hT, nm2.parts, ev_pg), 1))
    s = S["st"]
    for c in range(2):
        p = tt(pool, s[:, 44 + c:45 + c], s[:, 40 + 2 * c:41 + 2 * c], s[:, 41 + 2 * c:42 + 2 * c], ALU.add,
               ev["sq", c, 0], ev["sq", c, 1])
        p = ts(pool, s[:, 46 + c:47 + c], s[:, 44 + c:45 + c], 1.0 / D, EPS, ALU.mult, ALU.add, p)
        p = tt(pool, s[:, 48 + c:49 + c], s[:, 46 + c:47 + c], S["half_"][:, 0:1], ALU.pow, p)
        for n in range(2):
            sl = slice(n * 512, n * 512 + 512)
            xc = x[:, c, sl]
            d = stt(xc, xc, s[:, 48 + c:49 + c], M[:, n * 512:n * 512 + 512], ALU.mult, ALU.mult, p, t_fin)
            sp("out", A["out"][0, c * 128:c * 128 + 128, sl], xc, d)


def build(nc, A):
    with ExitStack() as ctx:
        def sb(name, shape, dt=F32):
            return ctx.enter_context(nc.sbuf_tensor(name, shape, dt))

        def sem(name):
            return ctx.enter_context(nc.semaphore(name))

        A = dict(A)
        A["scr1"] = nc.dram_tensor("scr1", (16, 383), F32, kind="Internal").ap()
        A["scr2"] = nc.dram_tensor("scr2", (12, 511), F32, kind="Internal").ap()
        A["toe1"] = nc.dram_tensor("toe1", (16, 128, 256), F32, kind="Internal").ap()
        A["toe2"] = nc.dram_tensor("toe2", (12, 128, 384), F32, kind="Internal").ap()
        raw = sb("raw", [128, NR, SLOT])
        hi = sb("whi", [128, NS, SLOT], F32R)
        lo = sb("wlo", [128, NS, SLOT], F32R)
        S = {
            "M": sb("M", [128, 18432]), "RR": sb("RR", [128, 9216], F32R), "x": sb("x", [128, 2, D]),
            "xs": sb("xs", [128, 2, D]), "ident": sb("ident", [128, 128]), "rope": sb("rope", [128, 512]),
            "scan": sb("scan", [128, 256]), "mask": sb("mask", [128, 128], I32),
            "G": sb("G", [128, 84]), "ones": sb("ones", [128, 128]), "dg": sb("dg", [128, 2, 128]),
            "RB": sb("RB", [128, 512]), "tab": sb("tab", [33, 28]),
            "st": sb("st", [128, 64]), "cc": sb("cc", [128, 96]), "ebl": sb("ebl", [128, 16]),
            "half_": sb("half_", [128, 10]), "bcs": sb("bcs", [128, 528]),
            "nsink": sb("nsink", [128, 16]),
        }
        bcs = S["bcs"]
        S["cos"] = S["rope"][:, 0:256].rearrange("p (c d) -> p c d", c=2)
        S["sin"] = S["rope"][:, 256:512].rearrange("p (c d) -> p c d", c=2)
        S["gk2"] = S["rope"][0:16, :]
        S["sq"] = S["dg"][:, :, :].rearrange("p c t -> p (c t)")
        S["onorm"], S["qg"], S["kg"], S["sink"] = bcs[:, 0:256], bcs[:, 256:384], bcs[:, 384:512], bcs[:, 512:528]
        S["half"] = S["half_"][:, 0:2]
        S["half8"] = S["half_"][:, 0:8]
        S["half10"] = S["half_"][:, 0:10]
        S["sel"] = S["M"][0:33, 12288:14204]
        banks = ctx.enter_context(nc.psum_tensor("ps", [128, 8, 512], F32))

        sems = [sem("s_pe"), sem("s_dve"), sem("s_act"), sem("s_pool")]
        made = {}

        def dma_sem(name):
            if name not in made:
                made[name] = sem(name)
            return made[name]

        plan = None
        for _ in range(2):
            q = Queues(sems, dma_sem)
            st = Stream(plan, q, raw, hi, lo)
            write_program(q, S, st, A, [Bank(banks, n) for n in range(8)], banks)
            plan = st.seen
        for engine in (q.pe, q.dve, q.act, q.pool):
            engine.number()
        ends = [(s, n) for s, n in q.sp.sems.values()]

        block = ctx.enter_context(nc.Block())

        @block.sync
        def _(e):
            q.sp.write(e)
            for s, n in ends:
                e.wait_ge(s, n)

        @block.tensor
        def _(e):
            q.pe.write(e)

        @block.vector
        def _(e):
            q.dve.write(e)

        @block.scalar
        def _(e):
            q.act.write(e)

        @block.gpsimd
        def _(e):
            q.pool.write(e)


def constants():
    c = {"c_ident": np.eye(128, dtype=np.float32)}
    j, i = np.arange(128)[:, None], np.arange(128)[None, :]
    c["c_mask"] = ((j <= i) & (j // 64 == i // 64)).astype(np.int32)
    sel = np.zeros((33, 383 + 3 * 511), np.float32)
    d = 255 - np.arange(383)
    n = np.maximum(d, 0)
    large = 16 + (np.log(np.maximum(n, 1) / 16) / np.log(128 / 16) * 16).astype(np.int32)
    bucket = np.where(n < 16, n, np.minimum(large, 31))
    valid = (d >= 0) & (d < 128)
    for m in range(383):
        sel[bucket[m] if valid[m] else 32, m] = 1.0
    for g, (window, dil) in enumerate(((128, 1), (512, 4), (2048, 16))):
        rel = np.arange(511) - 255
        n = np.abs(rel)
        large = 8 + (np.log(np.maximum(n, 1) / 8) / np.log(1024 / 8) * 8).astype(np.int32)
        bucket = (rel > 0) * 16 + np.where(n < 8, n, np.minimum(large, 15))
        valid = (rel % dil == 0) & (n <= window // 2)
        for m in range(511):
            sel[bucket[m] if valid[m] else 32, 383 + 511 * g + m] = 1.0
    c["c_sel"] = sel
    f = np.power(np.float32(10000.0), -np.arange(0, 64, 2, dtype=np.float32) / np.float32(64))
    t = np.arange(256)
    ang = [(p.astype(np.float32)[:, None] * f[None, :]).astype(np.float32) for p in (t // 64, t % 64)]
    cos, sin = [np.cos(a) for a in ang], [np.sin(a) for a in ang]
    c["c_cos"] = np.concatenate([cos[0], cos[0], cos[1], cos[1]], 1).astype(np.float32)
    c["c_sin"] = np.concatenate([-sin[0], sin[0], -sin[1], sin[1]], 1).astype(np.float32)
    return c


INS = ["x", "a_w_in", "a_w_gk2", "a_b_gk", "a_onorm", "a_w_out", "kv_norm", "w_kv", "b_w_q", "b_sinks", "b_w_out",
       "rel_table", "ln_mix", "ln_mlp", "w_up", "w_down", "ln_final", "p_2", "norm_mix_g_2", "w_in_2", "b_gate_2",
       "q_norm_g_2", "k_norm_g_2", "rel_bias_2", "w_out_a_2", "w_out_b_2", "w_out_2", "norm_mlp_g_2", "w_ff1_2",
       "w_ff2_2", "norm_ple_g_2", "w_ple_gate_2", "w_ple_2", "final_norm_g_2"]


def kernel(**inputs):
    import concourse.bacc as bacc
    from concourse.bass_utils import run_bass_kernel_spmd as run

    nc = bacc.Bacc("TRN2", target_bir_lowering=False, num_devices=1)
    arrays, A = {}, {}
    for name in INS:
        arrays["in_" + name] = np.ascontiguousarray(inputs[name])
    for name, a in constants().items():
        arrays["in_" + name] = a
    for name, a in arrays.items():
        A[name[3:]] = nc.dram_tensor(name, a.shape, mybir.dt.from_np(a.dtype), kind="ExternalInput").ap()
    A["out"] = nc.dram_tensor("out_0", (1, T, D), F32, kind="ExternalOutput").ap()
    build(nc, A)
    r = run(nc, [arrays], core_ids=[0])
    return r.results[0]["out_0"]
```
